# Optimizing a Trainium2 kernel written in Bass

```python
import jax, jax.numpy as jnp
from jax import lax
import numpy as np

D_MODEL = 1024
BATCH = 1
SEQ = 256
DEPTH = 2

D_MIX = D_MODEL
W_GROUP = D_MIX // 4
HEAD_DIM = 64
ROT_DIM = HEAD_DIM // 4
ROPE_THETA = 500000.0
Q_BLOCK = 128
EPS = 1e-6
DSA_HEADS = W_GROUP // HEAD_DIM
IDX_HEADS = 8
IDX_DIM = 32
IDX_ROT = IDX_DIM // 4
DSA_TOPK = 256
NSA_HEADS = W_GROUP // HEAD_DIM
CMP_LEN = 32
CMP_STRIDE = 16
SLC_BLOCK = 64
SLC_TOPN = 16
WINDOW = 512
CONV_WIDTH = 3
POOL_GROUPS = 4
POOL_WINDOWS = (2, 4, 8, 16)
POOL_CH = W_GROUP // POOL_GROUPS

IN_SPLITS = (
    ("a_q", DSA_HEADS * HEAD_DIM), ("a_k", HEAD_DIM), ("a_v", HEAD_DIM),
    ("a_qi", IDX_HEADS * IDX_DIM), ("a_ki", IDX_DIM), ("a_wi", IDX_HEADS), ("a_gate", W_GROUP),
    ("b_q", NSA_HEADS * HEAD_DIM), ("b_kc", HEAD_DIM), ("b_vc", HEAD_DIM), ("b_ks", HEAD_DIM),
    ("b_vs", HEAD_DIM), ("b_kw", HEAD_DIM), ("b_vw", HEAD_DIM), ("b_g", 3 * NSA_HEADS), ("b_gate", W_GROUP),
    ("c_b", W_GROUP), ("c_c", W_GROUP), ("c_x", W_GROUP), ("c_gate", W_GROUP),
    ("d_u", W_GROUP), ("d_gate", W_GROUP),
)
D_IN = sum(w for _, w in IN_SPLITS)


def split_cols(z):
    offs = np.cumsum([w for _, w in IN_SPLITS])[:-1].tolist()
    return dict(zip([n for n, _ in IN_SPLITS], jnp.split(z, offs, axis=-1)))

def rmsnorm(x, g):
    xf = x.astype(jnp.float32)
    y = xf * lax.rsqrt(jnp.mean(xf * xf, axis=-1, keepdims=True) + EPS)
    return (y * g.astype(jnp.float32)).astype(x.dtype)

def rope(x, pos, rot):
    half = rot // 2
    inv = ROPE_THETA ** (-jnp.arange(half, dtype=jnp.float32) / half)
    ang = pos.astype(jnp.float32)[:, None] * inv[None, :]
    cos = jnp.cos(ang)[:, None, :].astype(x.dtype)
    sin = jnp.sin(ang)[:, None, :].astype(x.dtype)
    x1, x2, rest = x[..., :half], x[..., half:rot], x[..., rot:]
    return jnp.concatenate([x1 * cos - x2 * sin, x2 * cos + x1 * sin, rest], axis=-1)

def masked_softmax(s, valid):
    s = jnp.where(valid, s.astype(jnp.float32), -jnp.inf)
    m = jnp.max(s, axis=-1, keepdims=True)
    m = jnp.where(jnp.isfinite(m), m, 0.0)
    e = jnp.where(valid, jnp.exp(s - m), 0.0)
    return e / jnp.maximum(jnp.sum(e, axis=-1, keepdims=True), 1e-30)

take_rows = jax.vmap(lambda a, i: a[i])

def dsa_mixer(q, k, v, qi, ki, wi):
    B, T = q.shape[:2]
    topk = min(DSA_TOPK, T // 4)
    key_pos = jnp.arange(T)

    def block(i):
        q0 = i * Q_BLOCK
        t = q0 + jnp.arange(Q_BLOCK)
        qb = lax.dynamic_slice_in_dim(q, q0, Q_BLOCK, axis=1)
        qib = lax.dynamic_slice_in_dim(qi, q0, Q_BLOCK, axis=1)
        wib = lax.dynamic_slice_in_dim(wi, q0, Q_BLOCK, axis=1) * (IDX_HEADS ** -0.5)
        logits = jnp.einsum('bqhd,bsd->bqhs', qib, ki) * (IDX_DIM ** -0.5)
        score = jnp.einsum('bqhs,bqh->bqs', jax.nn.relu(logits), wib).astype(jnp.float32)
        causal = key_pos[None, :] <= t[:, None]
        score = jnp.where(causal[None], score, -jnp.inf)
        _, idx = lax.top_k(score, topk)
        k_sel = take_rows(k, idx)
        v_sel = take_rows(v, idx)
        s = jnp.einsum('bqhd,bqkd->bhqk', qb, k_sel) * (HEAD_DIM ** -0.5)
        valid = (idx <= t[None, :, None])[:, None]
        p = masked_softmax(s, valid).astype(v.dtype)
        return jnp.einsum('bhqk,bqkd->bqhd', p, v_sel)

    out = lax.map(block, jnp.arange(T // Q_BLOCK))
    return jnp.moveaxis(out, 0, 1).reshape(B, T, -1)

def nsa_mixer(q, kc_tok, vc_tok, ks, vs, kw, vw, gates, pe_cmp, w_cmp_k, w_cmp_v):
    B, T = q.shape[:2]
    dtype = q.dtype
    n_cmp = (T - CMP_LEN) // CMP_STRIDE + 1
    n_slc = T // SLC_BLOCK
    topn = min(SLC_TOPN, n_slc)
    scale = HEAD_DIM ** -0.5
    cmp_start = jnp.arange(n_cmp) * CMP_STRIDE
    cmp_end = cmp_start + CMP_LEN - 1
    cmp_idx = cmp_start[:, None] + jnp.arange(CMP_LEN)[None, :]

    def compress(tok, w):
        blocks = tok[:, cmp_idx] + pe_cmp
        return blocks.reshape(B, n_cmp, CMP_LEN * HEAD_DIM) @ w

    k_cmp = rope(compress(kc_tok, w_cmp_k)[:, :, None], cmp_end, ROT_DIM)[:, :, 0]
    v_cmp = compress(vc_tok, w_cmp_v)
    slc_start = jnp.arange(n_slc) * SLC_BLOCK
    overlap = ((cmp_start[:, None] < slc_start[None, :] + SLC_BLOCK)
               & (cmp_end[:, None] >= slc_start[None, :])).astype(jnp.float32)
    ks_blocks = ks.reshape(B, n_slc, SLC_BLOCK, HEAD_DIM)
    vs_blocks = vs.reshape(B, n_slc, SLC_BLOCK, HEAD_DIM)
    kw_pad = jnp.pad(kw, ((0, 0), (WINDOW, 0), (0, 0)))
    vw_pad = jnp.pad(vw, ((0, 0), (WINDOW, 0), (0, 0)))
    blk_ids = jnp.arange(n_slc)
    in_blk = jnp.arange(SLC_BLOCK)

    def block(i):
        q0 = i * Q_BLOCK
        t = q0 + jnp.arange(Q_BLOCK)
        qb = lax.dynamic_slice_in_dim(q, q0, Q_BLOCK, axis=1)
        gb = lax.dynamic_slice_in_dim(gates, q0, Q_BLOCK, axis=1)
        s_c = jnp.einsum('bqhd,bnd->bhqn', qb, k_cmp) * scale
        valid_c = (cmp_end[None, :] <= t[:, None])[None, None]
        p_c = masked_softmax(s_c, valid_c)
        o_c = jnp.einsum('bhqn,bnd->bqhd', p_c.astype(dtype), v_cmp)
        imp = jnp.einsum('bhqn,nj->bqj', p_c, overlap)
        blk_t = t // SLC_BLOCK
        forced = (blk_ids[None, :] == 0) | (blk_ids[None, :] == blk_t[:, None])
        admissible = blk_ids[None, :] <= blk_t[:, None]
        imp = jnp.where(forced, jnp.inf, jnp.where(admissible, imp, -jnp.inf))
        _, idx = lax.top_k(imp, topn)
        k_sel = take_rows(ks_blocks, idx).reshape(B, Q_BLOCK, topn * SLC_BLOCK, HEAD_DIM)
        v_sel = take_rows(vs_blocks, idx).reshape(B, Q_BLOCK, topn * SLC_BLOCK, HEAD_DIM)
        pos_sel = (idx[..., None] * SLC_BLOCK + in_blk).reshape(B, Q_BLOCK, topn * SLC_BLOCK)
        s_s = jnp.einsum('bqhd,bqkd->bhqk', qb, k_sel) * scale
        p_s = masked_softmax(s_s, (pos_sel <= t[None, :, None])[:, None]).astype(dtype)
        o_s = jnp.einsum('bhqk,bqkd->bqhd', p_s, v_sel)
        kwb = lax.dynamic_slice_in_dim(kw_pad, q0, Q_BLOCK + WINDOW, axis=1)
        vwb = lax.dynamic_slice_in_dim(vw_pad, q0, Q_BLOCK + WINDOW, axis=1)
        pos_w = q0 - WINDOW + jnp.arange(Q_BLOCK + WINDOW)
        valid_w = ((pos_w[None, :] >= 0) & (pos_w[None, :] <= t[:, None])
                   & (t[:, None] - pos_w[None, :] < WINDOW))
        s_w = jnp.einsum('bqhd,bkd->bhqk', qb, kwb) * scale
        p_w = masked_softmax(s_w, valid_w[None, None]).astype(dtype)
        o_w = jnp.einsum('bhqk,bkd->bqhd', p_w, vwb)
        g = jax.nn.sigmoid(gb.astype(jnp.float32)).astype(dtype)
        return g[..., 0:1] * o_c + g[..., 1:2] * o_s + g[..., 2:3] * o_w

    out = lax.map(block, jnp.arange(T // Q_BLOCK))
    return jnp.moveaxis(out, 0, 1).reshape(B, T, -1)

def shortconv_mixer(b_gate, c_gate, xc, conv_w):
    T = xc.shape[1]
    u = c_gate * xc
    up = jnp.pad(u, ((0, 0), (CONV_WIDTH - 1, 0), (0, 0)))
    y = up[:, 0:T] * conv_w[0]
    for j in range(1, CONV_WIDTH):
        y = y + up[:, j:j + T] * conv_w[j]
    return b_gate * y

def pool_mixer(u, pool_w, pool_scale):
    B, T, _ = u.shape
    ug = u.reshape(B, T, POOL_GROUPS, POOL_CH)
    cs = jnp.cumsum(ug.astype(jnp.float32), axis=1)
    cs = jnp.pad(cs, ((0, 0), (1, 0), (0, 0), (0, 0)))
    win = jnp.array(POOL_WINDOWS, dtype=jnp.int32)
    t = jnp.arange(T)
    start = jnp.maximum(t[:, None] + 1 - win[None, :], 0)
    lower = cs[:, start, jnp.arange(POOL_GROUPS)[None, :]]
    count = jnp.minimum(t[:, None] + 1, win[None, :]).astype(jnp.float32)
    mean = (cs[:, 1:] - lower) / count[None, :, :, None]
    pooled = (mean - ug.astype(jnp.float32)).astype(u.dtype)
    y = jnp.einsum('btgc,gcd->btgd', pooled, pool_w).reshape(B, T, W_GROUP)
    return y * pool_scale

def hybrid_layer(x, norm_w, w_in, w_out, conv_w, pe_cmp, w_cmp_k, w_cmp_v, pool_w, pool_scale):
    B, T, _ = x.shape
    pos = jnp.arange(T)
    h = rmsnorm(x, norm_w)
    p = split_cols(h @ w_in)
    heads = lambda a, n: a.reshape(B, T, n, -1)
    one_head_rope = lambda a, rot: rope(a[:, :, None], pos, rot)[:, :, 0]
    o_a = dsa_mixer(rope(heads(p['a_q'], DSA_HEADS), pos, ROT_DIM), one_head_rope(p['a_k'], ROT_DIM),
                    p['a_v'], rope(heads(p['a_qi'], IDX_HEADS), pos, IDX_ROT),
                    one_head_rope(p['a_ki'], IDX_ROT), p['a_wi'])
    o_b = nsa_mixer(rope(heads(p['b_q'], NSA_HEADS), pos, ROT_DIM), p['b_kc'], p['b_vc'],
                    one_head_rope(p['b_ks'], ROT_DIM), p['b_vs'],
                    one_head_rope(p['b_kw'], ROT_DIM), p['b_vw'],
                    heads(p['b_g'], NSA_HEADS), pe_cmp, w_cmp_k, w_cmp_v)
    o_c = shortconv_mixer(p['c_b'], p['c_c'], p['c_x'], conv_w)
    o_d = pool_mixer(p['d_u'], pool_w, pool_scale)
    mixed = jnp.concatenate([jax.nn.silu(p['a_gate']) * o_a, jax.nn.silu(p['b_gate']) * o_b,
                             jax.nn.silu(p['c_gate']) * o_c, jax.nn.silu(p['d_gate']) * o_d], axis=-1)
    return x + mixed @ w_out

def first_inputs(seed: int = 0) -> dict:
    key = jax.random.key(seed)
    ks = jax.random.split(key, 11)
    f32 = jnp.float32
    x = jax.random.normal(ks[0], (BATCH, SEQ, D_MODEL), f32)
    norm_w = 1.0 + 0.1 * jax.random.normal(ks[1], (DEPTH, D_MODEL), f32)
    w_in = jax.random.normal(ks[2], (DEPTH, D_MODEL, D_IN), f32) * D_MODEL ** -0.5
    w_out = jax.random.normal(ks[3], (DEPTH, D_MIX, D_MODEL), f32) * D_MIX ** -0.5
    conv_w = jax.random.normal(ks[4], (DEPTH, CONV_WIDTH, W_GROUP), f32) * CONV_WIDTH ** -0.5
    pe_cmp = 0.02 * jax.random.normal(ks[5], (DEPTH, CMP_LEN, HEAD_DIM), f32)
    w_cmp_k = jax.random.normal(ks[6], (DEPTH, CMP_LEN * HEAD_DIM, HEAD_DIM), f32) * (CMP_LEN * HEAD_DIM) ** -0.5
    w_cmp_v = jax.random.normal(ks[7], (DEPTH, CMP_LEN * HEAD_DIM, HEAD_DIM), f32) * (CMP_LEN * HEAD_DIM) ** -0.5
    pool_w = jax.random.normal(ks[8], (DEPTH, POOL_GROUPS, POOL_CH, POOL_CH), f32) * POOL_CH ** -0.5
    pool_scale = 1.0 + 0.1 * jax.random.normal(ks[9], (DEPTH, W_GROUP), f32)
    final_norm_w = 1.0 + 0.1 * jax.random.normal(ks[10], (D_MODEL,), f32)
    return {"x": x, "norm_w": norm_w, "w_in": w_in, "w_out": w_out, "conv_w": conv_w,
            "pe_cmp": pe_cmp, "w_cmp_k": w_cmp_k, "w_cmp_v": w_cmp_v, "pool_w": pool_w,
            "pool_scale": pool_scale, "final_norm_w": final_norm_w}

def first_block(x, norm_w, w_in, w_out, conv_w, pe_cmp, w_cmp_k, w_cmp_v, pool_w, pool_scale, final_norm_w):
    for l in range(DEPTH):
        x = hybrid_layer(x, norm_w[l], w_in[l], w_out[l], conv_w[l], pe_cmp[l],
                         w_cmp_k[l], w_cmp_v[l], pool_w[l], pool_scale[l])
    return rmsnorm(x, final_norm_w)


GRID_W = 64
CTX_LEN = 256

D_FF = 2816

GLA_HEADS = 4
GLA_DK = 64
GLA_DV = 128
GLA_QK = GLA_HEADS * GLA_DK
GLA_V = GLA_HEADS * GLA_DV
GLA_RANK = 16
GLA_TAU = 16.0
GLA_CHUNK = 64

MLA_HEADS = 4
MLA_D_NOPE = 128
MLA_D_ROPE = 64
MLA_D_V = 128
MLA_D_CQ = 384
MLA_D_CKV = 128
MLA_SCALE = (MLA_D_NOPE + MLA_D_ROPE) ** -0.5

NA_HEADS = 16
NA_HEAD_DIM = 64
NA_KH = 8
NA_KW = 16

ROPE_BASE = 10000.0
N_EVEN = (DEPTH + 1) // 2
N_ODD = DEPTH // 2
ALPHA = (2 * DEPTH) ** 0.25
BETA = (8 * DEPTH) ** -0.25

EVEN_SIZES = (GLA_QK, GLA_QK, GLA_V, GLA_V, GLA_RANK, GLA_RANK, MLA_D_CQ, MLA_D_CKV, MLA_D_ROPE)
EVEN_OUT_IN = GLA_V + MLA_HEADS * MLA_D_V
NA_WIDTH = NA_HEADS * NA_HEAD_DIM


def layer_norm(x):
    xf = x.astype(jnp.float32)
    mu = jnp.mean(xf, axis=-1, keepdims=True)
    var = jnp.mean(jnp.square(xf - mu), axis=-1, keepdims=True)
    return ((xf - mu) * lax.rsqrt(var + EPS)).astype(x.dtype)

def rms_norm(x, g):
    xf = x.astype(jnp.float32)
    y = xf * lax.rsqrt(jnp.mean(jnp.square(xf), axis=-1, keepdims=True) + EPS)
    return y.astype(x.dtype) * g

def modulate(x, shift, scale):
    return x * (1.0 + scale) + shift

def post_norm(x, y):
    return layer_norm(ALPHA * x + y)

def swiglu(h, w_in, w_out):
    gate, up = jnp.split(h @ w_in, 2, axis=-1)
    return (jax.nn.silu(gate) * up) @ w_out

def axial_rope(n_tokens):
    t = jnp.arange(n_tokens)
    row = (t // GRID_W).astype(jnp.float32)
    col = (t % GRID_W).astype(jnp.float32)
    n_freq = MLA_D_ROPE // 4
    inv = ROPE_BASE ** (-jnp.arange(n_freq, dtype=jnp.float32) / n_freq)
    ang = jnp.concatenate([row[:, None] * inv, col[:, None] * inv], axis=-1)
    return jnp.cos(ang), jnp.sin(ang)

def apply_rope(x, cos, sin):
    x2 = x.reshape(*x.shape[:-1], -1, 2).astype(jnp.float32)
    x0, x1 = x2[..., 0], x2[..., 1]
    out = jnp.stack([x0 * cos - x1 * sin, x0 * sin + x1 * cos], axis=-1)
    return out.reshape(x.shape).astype(x.dtype)

def dense_attention(q, k, v, scale):
    B, T, H, dk = q.shape
    nb = T // Q_BLOCK
    qb = q.reshape(B, nb, Q_BLOCK, H, dk).transpose(1, 0, 2, 3, 4)

    def block(qi):
        s = jnp.einsum('bqhd,bkhd->bhqk', qi, k).astype(jnp.float32) * scale
        p = jax.nn.softmax(s, axis=-1).astype(v.dtype)
        return jnp.einsum('bhqk,bkhd->bqhd', p, v)

    o = lax.map(block, qb)
    return o.transpose(1, 0, 2, 3, 4).reshape(B, T, H, v.shape[-1])

def gla_chunked(q, k, v, log_g, s0, include_diag):
    B, T, H, DK = q.shape
    DV = v.shape[-1]
    n = T // GLA_CHUNK

    def to_chunks(a):
        return a.reshape(B, n, GLA_CHUNK, H, a.shape[-1]).transpose(1, 0, 3, 2, 4)

    idx = jnp.arange(GLA_CHUNK)
    mask = (idx[:, None] >= idx[None, :]) if include_diag else (idx[:, None] > idx[None, :])

    def step(s, inp):
        qi, ki, vi, gi = inp
        b = jnp.cumsum(gi.astype(jnp.float32), axis=-2)
        diff = b[:, :, :, None, :] - b[:, :, None, :, :]
        decay = jnp.exp(jnp.where(mask[:, :, None], diff, -jnp.inf)).astype(qi.dtype)
        att = jnp.einsum('bhid,bhjd,bhijd->bhij', qi, ki, decay)
        o_intra = jnp.einsum('bhij,bhjv->bhiv', att, vi)
        o_inter = jnp.einsum('bhid,bhdv->bhiv', qi * jnp.exp(b).astype(qi.dtype), s)
        b_last = b[:, :, -1:, :]
        k_dec = ki * jnp.exp(b_last - b).astype(ki.dtype)
        s_new = s * jnp.exp(b_last[:, :, 0, :])[..., None].astype(s.dtype) + jnp.einsum('bhjd,bhjv->bhdv', k_dec, vi)
        return s_new, o_intra + o_inter

    s_fin, o = lax.scan(step, s0, (to_chunks(q), to_chunks(k), to_chunks(v), to_chunks(log_g)))
    return o.transpose(1, 0, 3, 2, 4).reshape(B, T, H, DV), s_fin

def gla_log_gate(lr, wg2, bg):
    return jax.nn.log_sigmoid((lr @ wg2 + bg).astype(jnp.float32)) / GLA_TAU

def gla_out(o, r, norm_g):
    B, T = o.shape[:2]
    return rms_norm(o, norm_g).reshape(B, T, GLA_V) * jax.nn.silu(r)

def even_project(h, w_in, wg2_f, bg_f, wg2_b, bg_b, q_norm_g, kv_norm_g, w_uq, w_ukv):
    B, T, _ = h.shape
    split_points = np.cumsum(EVEN_SIZES)[:-1].tolist()
    q_g, k_g, v_g, r_g, lr_f, lr_b, c_q, c_kv, k_r = jnp.split(h @ w_in, split_points, axis=-1)
    heads = lambda a, n: a.reshape(B, T, n, -1)
    gla = (heads(q_g, GLA_HEADS) * GLA_DK ** -0.5, heads(k_g, GLA_HEADS), heads(v_g, GLA_HEADS),
           heads(gla_log_gate(lr_f, wg2_f, bg_f), GLA_HEADS), heads(gla_log_gate(lr_b, wg2_b, bg_b), GLA_HEADS), r_g)
    q = heads(rms_norm(c_q, q_norm_g) @ w_uq, MLA_HEADS)
    kv = heads(rms_norm(c_kv, kv_norm_g) @ w_ukv, MLA_HEADS)
    mla = (q[..., :MLA_D_NOPE], q[..., MLA_D_NOPE:], kv[..., :MLA_D_NOPE], k_r, kv[..., MLA_D_NOPE:])
    return gla, mla

def even_mixer(hc, hl, cos, sin, w_in, wg2_f, bg_f, wg2_b, bg_b, gla_norm_g, q_norm_g, kv_norm_g,
               w_uq, w_ukv, w_out, with_ctx_out):
    B, S, _ = hl.shape
    args = (w_in, wg2_f, bg_f, wg2_b, bg_b, q_norm_g, kv_norm_g, w_uq, w_ukv)
    (gq_c, gk_c, gv_c, gf_c, gb_c, r_c), (qn_c, qr_c, kn_c, kr_c, v_c) = even_project(hc, *args)
    (gq_l, gk_l, gv_l, gf_l, gb_l, r_l), (qn_l, qr_l, kn_l, kr_l, v_l) = even_project(hl, *args)

    s0 = jnp.zeros((B, GLA_HEADS, GLA_DK, GLA_DV), hl.dtype)
    flip = lambda a: a[:, ::-1]
    o_cf, s_cf = gla_chunked(gq_c, gk_c, gv_c, gf_c, s0, True)
    o_cb, s_cb = gla_chunked(flip(gq_c), flip(gk_c), flip(gv_c), flip(gb_c), s0, False)
    o_lf, _ = gla_chunked(gq_l, gk_l, gv_l, gf_l, s_cf, True)
    o_lb, _ = gla_chunked(flip(gq_l), flip(gk_l), flip(gv_l), flip(gb_l), s_cb, False)
    gla_l = gla_out(o_lf + flip(o_lb), r_l, gla_norm_g)

    rope_shape = kn_l.shape[:-1] + (MLA_D_ROPE,)
    q_l = jnp.concatenate([qn_l, apply_rope(qr_l, cos[None, :, None], sin[None, :, None])], axis=-1)
    kr_l_rot = apply_rope(kr_l, cos[None], sin[None])
    k_l = jnp.concatenate([kn_l, jnp.broadcast_to(kr_l_rot[:, :, None], rope_shape)], axis=-1)
    k_c = jnp.concatenate([kn_c, jnp.broadcast_to(kr_c[:, :, None], kn_c.shape[:-1] + (MLA_D_ROPE,))], axis=-1)
    k_all = jnp.concatenate([k_c, k_l], axis=1)
    v_all = jnp.concatenate([v_c, v_l], axis=1)
    mla_l = dense_attention(q_l, k_all, v_all, MLA_SCALE).reshape(B, S, -1)

    yl = jnp.concatenate([gla_l, mla_l], axis=-1) @ w_out
    yc = None
    if with_ctx_out:
        Tc = hc.shape[1]
        gla_c = gla_out(o_cf + flip(o_cb), r_c, gla_norm_g)
        q_c = jnp.concatenate([qn_c, qr_c], axis=-1)
        mla_c = dense_attention(q_c, k_c, v_c, MLA_SCALE).reshape(B, Tc, -1)
        yc = jnp.concatenate([gla_c, mla_c], axis=-1) @ w_out
    return yc, yl

def neighbourhood_attention(q, k, v, k_ctx, v_ctx, rpb):
    B, S, H, d = q.shape
    rows = S // GRID_W
    kh = min(NA_KH, rows)
    scale = d ** -0.5
    qg = q.reshape(B, rows, GRID_W, H, d)
    kg = k.reshape(B, rows, GRID_W, H, d)
    vg = v.reshape(B, rows, GRID_W, H, d)
    col = jnp.arange(GRID_W)
    col_start = jnp.clip(col - NA_KW // 2, 0, GRID_W - NA_KW)
    col_idx = col_start[:, None] + jnp.arange(NA_KW)[None, :]
    bias_col = rpb[:, :, col_idx - col[:, None] + (NA_KW - 1)]

    def row_block(r):
        r_start = jnp.clip(r - kh // 2, 0, rows - kh)
        k_win = lax.dynamic_slice_in_dim(kg, r_start, kh, axis=1)[:, :, col_idx]
        v_win = lax.dynamic_slice_in_dim(vg, r_start, kh, axis=1)[:, :, col_idx]
        q_r = lax.dynamic_index_in_dim(qg, r, axis=1, keepdims=False)
        rel_row = r_start + jnp.arange(kh) - r + (NA_KH - 1)
        bias = jnp.take(bias_col, rel_row, axis=1).transpose(0, 2, 1, 3)
        s_nb = jnp.einsum('bchd,brcwhd->bhcrw', q_r, k_win).astype(jnp.float32) * scale + bias[None]
        s_cx = jnp.einsum('bchd,bkhd->bhck', q_r, k_ctx).astype(jnp.float32) * scale
        p = jax.nn.softmax(jnp.concatenate([s_nb.reshape(B, H, GRID_W, kh * NA_KW), s_cx], axis=-1), axis=-1)
        p = p.astype(v.dtype)
        p_nb = p[..., :kh * NA_KW].reshape(B, H, GRID_W, kh, NA_KW)
        p_cx = p[..., kh * NA_KW:]
        return (jnp.einsum('bhcrw,brcwhd->bchd', p_nb, v_win)
                + jnp.einsum('bhck,bkhd->bchd', p_cx, v_ctx))

    o = lax.map(row_block, jnp.arange(rows))
    return o.transpose(1, 0, 2, 3, 4).reshape(B, S, H, d)

def odd_mixer(hc, hl, w_in, rpb, w_out, with_ctx_out):
    def project(h):
        B, T, _ = h.shape
        q, k, v = jnp.split(h @ w_in, 3, axis=-1)
        return (q.reshape(B, T, NA_HEADS, NA_HEAD_DIM), k.reshape(B, T, NA_HEADS, NA_HEAD_DIM),
                v.reshape(B, T, NA_HEADS, NA_HEAD_DIM))

    B, S, _ = hl.shape
    q_c, k_c, v_c = project(hc)
    q_l, k_l, v_l = project(hl)
    yl = neighbourhood_attention(q_l, k_l, v_l, k_c, v_c, rpb).reshape(B, S, NA_WIDTH) @ w_out
    yc = None
    if with_ctx_out:
        o_c = dense_attention(q_c, k_c, v_c, NA_HEAD_DIM ** -0.5)
        yc = o_c.reshape(B, hc.shape[1], NA_WIDTH) @ w_out
    return yc, yl

def second_inputs(seed: int = 0) -> dict:
    key = jax.random.key(seed)
    it = iter(list(jax.random.split(key, 32)))
    nrm = lambda shape, scale: jax.random.normal(next(it), shape, jnp.float32) * scale
    D = D_MODEL
    gate_base = jnp.tile(jnp.concatenate([jnp.zeros((2 * D,), jnp.float32), jnp.ones((D,), jnp.float32)]), 3)
    return {
        'x': nrm((BATCH, SEQ, D), 1.0),
        'c': nrm((BATCH, D), 1.0),
        'ctx': nrm((BATCH, CTX_LEN, D), 1.0),
        'c_ctx': nrm((D,), 1.0),
        'ada_w': nrm((DEPTH, D, 9 * D), 0.5 * D ** -0.5),
        'ada_b': gate_base + nrm((DEPTH, 9 * D), 0.02),
        'ffn1_w_in': nrm((DEPTH, D, 2 * D_FF), D ** -0.5),
        'ffn1_w_out': nrm((DEPTH, D_FF, D), BETA * D_FF ** -0.5),
        'ffn2_w_in': nrm((DEPTH, D, 2 * D_FF), D ** -0.5),
        'ffn2_w_out': nrm((DEPTH, D_FF, D), BETA * D_FF ** -0.5),
        'even_w_in': nrm((N_EVEN, D, sum(EVEN_SIZES)), D ** -0.5),
        'gla_wg2_f': nrm((N_EVEN, GLA_RANK, GLA_QK), GLA_RANK ** -0.5),
        'gla_bg_f': nrm((N_EVEN, GLA_QK), 0.5),
        'gla_wg2_b': nrm((N_EVEN, GLA_RANK, GLA_QK), GLA_RANK ** -0.5),
        'gla_bg_b': nrm((N_EVEN, GLA_QK), 0.5),
        'gla_norm_g': 1.0 + nrm((N_EVEN, GLA_DV), 0.02),
        'mla_q_norm_g': 1.0 + nrm((N_EVEN, MLA_D_CQ), 0.02),
        'mla_kv_norm_g': 1.0 + nrm((N_EVEN, MLA_D_CKV), 0.02),
        'mla_w_uq': nrm((N_EVEN, MLA_D_CQ, MLA_HEADS * (MLA_D_NOPE + MLA_D_ROPE)), MLA_D_CQ ** -0.5),
        'mla_w_ukv': nrm((N_EVEN, MLA_D_CKV, MLA_HEADS * (MLA_D_NOPE + MLA_D_V)), MLA_D_CKV ** -0.5),
        'even_w_out': nrm((N_EVEN, EVEN_OUT_IN, D), BETA * EVEN_OUT_IN ** -0.5),
        'na_w_in': nrm((N_ODD, D, 3 * NA_WIDTH), D ** -0.5),
        'na_rpb': nrm((N_ODD, NA_HEADS, 2 * NA_KH - 1, 2 * NA_KW - 1), 0.5),
        'na_w_out': nrm((N_ODD, NA_WIDTH, D), BETA * NA_WIDTH ** -0.5),
    }

def second_block(x, c, ctx, c_ctx, ada_w, ada_b, ffn1_w_in, ffn1_w_out, ffn2_w_in, ffn2_w_out,
              even_w_in, gla_wg2_f, gla_bg_f, gla_wg2_b, gla_bg_b, gla_norm_g, mla_q_norm_g, mla_kv_norm_g,
              mla_w_uq, mla_w_ukv, even_w_out, na_w_in, na_rpb, na_w_out):
    S = x.shape[1]
    cos, sin = axial_rope(S)
    xl, xc = x, ctx
    for l in range(DEPTH):
        last = l == DEPTH - 1
        i = l // 2
        mod_l = jax.nn.silu(c) @ ada_w[l] + ada_b[l]
        mod_c = jax.nn.silu(c_ctx) @ ada_w[l] + ada_b[l]
        sh1, sc1, g1, sh2, sc2, g2, sh3, sc3, g3 = [m[:, None, :] for m in jnp.split(mod_l, 9, axis=-1)]
        csh1, csc1, cg1, csh2, csc2, cg2, csh3, csc3, cg3 = jnp.split(mod_c, 9)

        xl = post_norm(xl, 0.5 * g1 * swiglu(modulate(xl, sh1, sc1), ffn1_w_in[l], ffn1_w_out[l]))
        xc = post_norm(xc, 0.5 * cg1 * swiglu(modulate(xc, csh1, csc1), ffn1_w_in[l], ffn1_w_out[l]))

        hl = modulate(xl, sh2, sc2)
        hc = modulate(xc, csh2, csc2)
        if l % 2 == 0:
            yc, yl = even_mixer(hc, hl, cos, sin, even_w_in[i], gla_wg2_f[i], gla_bg_f[i], gla_wg2_b[i], gla_bg_b[i],
                                gla_norm_g[i], mla_q_norm_g[i], mla_kv_norm_g[i], mla_w_uq[i], mla_w_ukv[i],
                                even_w_out[i], not last)
        else:
            yc, yl = odd_mixer(hc, hl, na_w_in[i], na_rpb[i], na_w_out[i], not last)
        xl = post_norm(xl, g2 * yl)

        xl = post_norm(xl, 0.5 * g3 * swiglu(modulate(xl, sh3, sc3), ffn2_w_in[l], ffn2_w_out[l]))
        if not last:
            xc = post_norm(xc, cg2 * yc)
            xc = post_norm(xc, 0.5 * cg3 * swiglu(modulate(xc, csh3, csc3), ffn2_w_in[l], ffn2_w_out[l]))
    return xl


def setup_inputs(seed=0):
    out = dict(first_inputs(seed))
    for name, value in second_inputs(seed + 1).items():
        if name != "x":
            out[name + "_2"] = value
    return out


def reference(
    x, norm_w, w_in, w_out, conv_w, pe_cmp, w_cmp_k, w_cmp_v, pool_w, pool_scale, final_norm_w,
    c_2, ctx_2, c_ctx_2, ada_w_2, ada_b_2, ffn1_w_in_2, ffn1_w_out_2, ffn2_w_in_2, ffn2_w_out_2,
    even_w_in_2, gla_wg2_f_2, gla_bg_f_2, gla_wg2_b_2, gla_bg_b_2, gla_norm_g_2, mla_q_norm_g_2,
    mla_kv_norm_g_2, mla_w_uq_2, mla_w_ukv_2, even_w_out_2, na_w_in_2, na_rpb_2, na_w_out_2,
):
    x = first_block(
        x, norm_w, w_in, w_out, conv_w, pe_cmp, w_cmp_k, w_cmp_v, pool_w, pool_scale,
        final_norm_w,
    )
    return second_block(
        x, c_2, ctx_2, c_ctx_2, ada_w_2, ada_b_2, ffn1_w_in_2, ffn1_w_out_2, ffn2_w_in_2,
        ffn2_w_out_2, even_w_in_2, gla_wg2_f_2, gla_bg_f_2, gla_wg2_b_2, gla_bg_b_2,
        gla_norm_g_2, mla_q_norm_g_2, mla_kv_norm_g_2, mla_w_uq_2, mla_w_ukv_2, even_w_out_2,
        na_w_in_2, na_rpb_2, na_w_out_2,
    )


_drawn_inputs = setup_inputs


def setup_inputs(seed=0):
    import zlib

    import numpy as np

    out = dict(_drawn_inputs(seed))
    spreads = {}
    factors = {'pe_cmp': 8.0,
     'gla_wg2_b_2': 2.948,
     'gla_norm_g_2': 8.0,
     'mla_q_norm_g_2': 8.0,
     'mla_kv_norm_g_2': 8.0,
     'na_rpb_2': 5.028}
    for name, (base, spread) in spreads.items():
        noise = np.random.default_rng([zlib.crc32(name.encode()), seed]).standard_normal(out[name].shape)
        drawn = base * np.exp(spread * noise) if base else spread * noise
        out[name] = __import__('jax').numpy.asarray(drawn.astype(out[name].dtype))
    for name, factor in factors.items():
        out[name] = (out[name] * factor).astype(out[name].dtype)
    return out
```

```python
from contextlib import ExitStack

import numpy as np
import concourse.bass as bass
from concourse import mybir

F32 = mybir.dt.float32
F32R = mybir.dt.float32r
ALU = mybir.AluOpType
ACT = mybir.ActivationFunctionType
AX = mybir.AxisListType.X

P = 128
D = 1024
KT = D // P
T = 256
DEPTH = 2
EPS = 1e-6
HD = 64
DFF = 2816
FH = DFF // P // 2
ALPHA = (2 * DEPTH) ** 0.25
TOPK = T // 4
NCMP = (T - 32) // 16 + 1
GC = 64
MLA_SCALE = 192.0 ** -0.5
NEG = -1e30
FLOOR = 1e29
TAKEN = -3e38

SLAB = 2 * KT * P
RING = 4

def stage_table():
    runs = []
    for l in range(DEPTH):
        runs += [(f"in{l}", 6, 2 * KT * P), (f"vb{l}", 1, KT * 148), (f"kcvc{l}", 1, KT * P),
                 (f"tail{l}", 10, 2 * KT * P), (f"out{l}", 4, 2 * KT * P)]
    for l in range(DEPTH):
        for f in (1, 2):
            if f == 2 and l == 0:
                runs += [("even", 9, 2 * KT * P), ("uq", 3, 6 * P), ("ukv", 4, 2 * P), ("eout", 4, 2 * KT * P)]
            if f == 2 and l == 1:
                runs += [("odd", 12, 2 * KT * P), ("oout", 4, 2 * KT * P)]
            for half in range(2):
                runs += [(f"ffi{f}{l}{half}", FH, 2 * KT * P), (f"ffo{f}{l}{half}", KT, FH * P)]
    return runs


RUNS = stage_table()
START, SIZE = {}, []
for _name, _n, _f in RUNS:
    START[_name] = len(SIZE)
    SIZE += [_f] * _n
NSLABS = len(SIZE)

def columns(parts):
    at, o = {}, 0
    for name, n in parts:
        at[name] = (o, n)
        o += n
    return at, o


CONST, CONST_N = columns([("ident", P), ("ones", P), ("permA", P), ("permI", P), ("permM", P)])
C1, C1_N = columns([("ropeA", 2 * T), ("ropeI", 2 * T), ("ropeC", 32), ("tri", T), ("cmpm", 32), ("invc", 2 * T)])
C2, C2_N = columns([("ropeM", 2 * T), ("gmask", 2 * GC), ("reset", 2 * T)])
VEC, VEC_N = columns([("norm", DEPTH * KT), ("fnorm", KT), ("conv", DEPTH * 6), ("pscale", DEPTH * 2), ("pe", DEPTH * 32),
                      ("adab", DEPTH * 72), ("c", 2 * KT), ("bg", 4), ("gnorm", 1), ("qnorm", 3), ("kvnorm", 1)])
SML, SML_N = columns([("poolw", DEPTH * 2 * P), ("wg2", 2 * P)])

ARENA = 0


class Idx:

    def __init__(self, base, reg=None):
        self.base, self.reg = base, reg

    def __add__(self, n):
        return Idx(self.base + n, self.reg)

    @property
    def slot(self):
        return self.base % RING

    @property
    def par(self):
        return self.base % 2

    def count(self, per_group, at_zero):
        return at_zero if self.reg is None else self.reg * per_group + at_zero


UPTO = 9
LAST_X = 9


def build(nc, a):
    UPTO_SLAB = {1: START["in1"], 2: START["ffi100"], 3: START["ffi100"], 4: START["even"], 5: START["ffi200"], 6: START["ffi110"],
                 7: START["odd"], 8: START["ffi210"], 9: NSLABS}[UPTO]
    ctx = ExitStack()
    sems = {}

    def sig(name):
        if name not in sems:
            sems[name] = ctx.enter_context(nc.semaphore(name))
        return sems[name]

    with ctx:
        base = [(nc.sbuf_base + 63) // 64 * 64]
        limit = nc.sbuf_usable_end

        def fixed(name, shape, dt=F32):
            n = int(np.prod(shape[1:])) * 4
            t = nc.alloc_sbuf_tensor_at(name, shape, dt, offset=base[0])
            base[0] += (n + 31) // 32 * 32
            return t

        raw = fixed("raw", [P, RING, SLAB])
        wh = fixed("wh", [P, 2, SLAB], F32R)
        wl = fixed("wl", [P, 2, SLAB], F32R)
        X = fixed("X", [P, KT, 2 * T])
        xh = fixed("xh", [P, KT, 2 * T], F32R)
        xl = fixed("xl", [P, KT, 2 * T], F32R)
        const = fixed("const", [P, CONST_N])
        vec = fixed("vec", [P, VEC_N])
        sml = fixed("sml", [P, SML_N])
        mod = fixed("mod", [P, DEPTH, 9, KT, 2])
        sc = fixed("sc", [P, KT, 2])
        tiny = fixed("tiny", [P, 144])
        tiny2 = fixed("tiny2", [P, T])
        tiny3 = fixed("tiny3", [P, T])
        arena0 = base[0]

        def phase(spec):
            out, o = {}, arena0
            for name, shape, *dt in spec:
                n = (int(np.prod(shape[1:])) * 4 + 31) // 32 * 32
                out[name] = nc.alloc_sbuf_tensor_at(name, shape, dt[0] if dt else F32, offset=o)
                o += n
            assert o <= limit, (spec[0][0], o - limit)
            return out

        def cst(name, tab=None, at=None):
            at, tab = at or CONST, tab or const
            o, n = at[name]
            return tab[:, o:o + n]

        def vcol(name, i, n=1):
            o, _ = VEC[name]
            return vec[:, o + i:o + i + n]

        ident, ones = cst("ident"), cst("ones")
        PS = ctx.enter_context(nc.psum_tensor("PS", [P, 8, 512], F32))

        slab_full = [sig(f"slab_full{s}") for s in range(RING)]
        hi_done, lo_done, slab_used = sig("hi_done"), sig("lo_done"), sig("slab_used")
        drained = [sig("drained_even"), sig("drained_odd")]
        consts_in, acts_in = sig("consts_in"), sig("acts_in")
        out_stored = sig("out_stored")
        dve_step, act_step = sig("dve_step"), sig("act_step")
        ada_full = [sig("ada_full0"), sig("ada_full1")]
        ada_used = sig("ada_used")
        NADA = DEPTH * 36

        b1 = phase([("ada", [P, 2, SLAB]), ("c1", [P, C1_N]), ("MIX", [P, 8, T]), ("SM", [P, 2, 4, T]),
                    ("QK", [P, 7, T]), ("QI", [P, 3, T]), ("PT", [P, 2, 2, 512]), ("BH", [P, 16, 32], F32R),
                    ("BL", [P, 16, 32], F32R), ("CC", [P, 2, T]), ("CX", [P, 2, T]), ("CB", [P, 2, T]),
                    ("DU", [P, 2, 16 + T]), ("SG", [P, 8, T]), ("VT", [P, 2, T]), ("VW", [P, 2, 148]),
                    ("KC", [P, 2, 16]), ("VC", [16, P]), ("UP", [P, 2, 2 + T]), ("W2", [P, 2, 16 + T])])
        ff = phase([("HH", [P, FH, 2 * T], F32R), ("HL", [P, FH, 2 * T], F32R), ("SQ", [P, KT, 2 * T]),
                    ("HF", [P, 2, 2 * T]), ("SI", [P, 2, 2 * T]), ("NRM", [P, 4, 2 * T])])
        ev = phase([("c2", [P, C2_N]), ("Q", [P, 2, 2 * T]), ("K", [P, 2, 2 * T]), ("LK", [P, 2, 2 * T]),
                    ("V", [P, 4, 512]), ("CQ", [P, 4, 2 * T]), ("RS", [P, 4, 2 * T]),
                    ("W", [P, 12, 2 * T]), ("KDT", [P, 2, 4, P]), ("S", [P, 8, 2, P]),
                    ("OA", [P, 4, 2 * T])])
        ml = phase([("c2_", [P, C2_N]), ("PR", [P, 2, 512]), ("K_", [P, 2, 2 * T]), ("LK_", [P, 2, 2 * T]),
                    ("PTM", [P, 2, 512]), ("V_", [P, 2, 512]), ("CQ_", [P, 4, 2 * T]),
                    ("CH", [P, 4, 2 * T], F32R), ("CL", [P, 4, 2 * T], F32R), ("QN", [P, 4, 2 * T]),
                    ("QR", [P, 2, 2 * T]), ("KN", [P, 4, 2 * T]), ("VM", [P, 4, 512])])
        od = phase([("nmask", [P, 64]), ("RPB", [P, 16, 7, 64]), ("NQ", [P, 8, T]), ("NK", [P, 8, 2 * T]),
                    ("NV", [P, 4, 1024]), ("NP", [P, 2, 512]), ("NPT", [P, 2, 512])])

        def turns_of(name):
            n = next(r[1] for r in RUNS if r[0] == name)
            turns = (n - (START[name] + n == NSLABS)) // 4
            return turns if turns >= 2 else 0

        def runs_of(eng, name, step, nxt=None):
            s0, n = START[name], dict((r[0], r[1]) for r in RUNS)[name]
            turns = turns_of(name)
            if turns:
                with eng.Fori(0, turns) as it:
                    for u in range(4):
                        step(Idx(s0 + u, it), it * 4 + u)
            for k in range(4 * turns, n):
                step(Idx(s0 + k), k)

        def width(i, after):
            turns = 1
            if i.reg is not None:
                turns = next(turns_of(name) for name, n, _ in RUNS if START[name] <= i.base < START[name] + n)
            return max([SIZE[n] for n in range(i.base + after, i.base + after + 4 * turns, 4) if n < NSLABS], default=0)

        def split_hi(act, i, n):
            act.wait_ge(slab_full[i.slot], i.count(16, 16 * (i.base // RING + 1)))
            if i.base >= 2:
                act.wait_ge(slab_used, i.count(4, i.base - 1))
            act.activation(wh[:, i.par, 0:n], raw[:, i.slot, 0:n], ACT.Copy).then_inc(hi_done, 1)

        def split_lo(dve, i, n):
            dve.wait_ge(hi_done, i.count(4, i.base + 1))
            dve.tensor_tensor(wl[:, i.par, 0:n], raw[:, i.slot, 0:n], wh[:, i.par, 0:n].bitcast(F32),
                              ALU.subtract).then_inc(lo_done, 1)

        def act_ahead(act, i):
            if width(i, 1):
                split_hi(act, i + 1, width(i, 1))

        def dve_ahead(dve, i):
            if width(i, 1):
                split_lo(dve, i + 1, width(i, 1))

        def slab_begin(pe, i):
            pe.wait_ge(lo_done, i.count(4, i.base + 1))
            if i.base >= 2:
                pe.wait_ge(drained[i.par], i.count(2, i.base // 2))

        def product(pe, out, i, tiles, rows=slice(0, P), xs=None, first=True, last=True):
            m = None
            for n, (o, h, lo) in enumerate(tiles):
                for j, (w, x) in enumerate(((wh, h), (wh, lo), (wl, h))):
                    m = pe.matmul(out, w[rows, i.par, o:o + P], x, start=first and n == 0 and j == 0,
                                  stop=last and n == len(tiles) - 1 and j == 2)
            return m

        def dense(pe, i, chunks, kts, xhi, xlo, c0, c1_):
            slab_begin(pe, i)
            for c in range(chunks):
                m = product(pe, PS[:, 2 * i.par + c, 0:c1_ - c0], i,
                            [((c * kts + k) * P, xhi[:, k, c0:c1_], xlo[:, k, c0:c1_]) for k in range(kts)])
            m.then_inc(slab_used, 1)

        def token_major(pe, i, ntok, n, xhi, xlo, kts, krow=0):
            slab_begin(pe, i)
            for tt in range(ntok):
                out = PS[:, 2 * i.par + tt // 2, (tt % 2) * 256:(tt % 2) * 256 + n]
                for k in range(kts):
                    for j, (x, w) in enumerate(((xhi, wh), (xhi, wl), (xlo, wh))):
                        m = pe.matmul(out, x[:, krow + k, tt * P:(tt + 1) * P], w[:, i.par, k * n:(k + 1) * n],
                                      start=k == 0 and j == 0, stop=k == kts - 1 and j == 2)
            m.then_inc(slab_used, 1)

        def banks(i, n):
            return PS[:, 2 * i.par:2 * i.par + 2, 0:n]

        class Chain:

            def __init__(self, eng, sem):
                self.eng, self.sem, self.n = eng, sem, 0

            def after(self, ins):
                self.n += 1
                ins.then_inc(self.sem, 1)
                self.eng.wait_ge(self.sem, self.n)

        def rstd(ch, dve, out, total, n):
            inverse_root(ch, dve, out, dve.tensor_scalar(out, total, 1.0 / n, EPS, ALU.mult, ALU.add))

        roots = {"dve": 0, "act": 0}

        def inverse_root(ch, dve, out, ins):
            roots["dve"] += 1
            ins.then_inc(ev_["var_ready"], 1)
            dve.wait_ge(ev_["root_done"], roots["dve"])
            ch.after(dve.reciprocal(out, out))

        def act_root(act, out):
            roots["act"] += 1
            act.wait_ge(ev_["var_ready"], roots["act"])
            act.activation(out, out, ACT.Sqrt).then_inc(ev_["root_done"], 1)

        def bc(ap, n):
            return ap.unsqueeze(1).broadcast_to([ap.shape[0], n, ap.shape[1]])

        def bl(ap, n):
            return ap.unsqueeze(len(ap.shape)).broadcast_to(list(ap.shape) + [n])

        IN = ["qi", "kika", "qa", "qb", "kskw", "va"]
        UNITS = [("S", 0), ("W", 0), ("C", 0), ("A", 0), ("S", 1), ("W", 1), ("C", 1), ("A", 1)]
        UN = len(UNITS)
        ada, c1 = b1["ada"], b1["c1"]
        SMF = b1["SM"][:, :, :, :].rearrange("p a b c -> p (a b c)")
        BLK = b1["PT"][:, 0, 0, :].rearrange("p (n j) -> p n j", n=16)
        KCV = b1["PT"][:, 1, 0, 0:T]
        ccol = lambda name: cst(name, c1, C1)

        def keys_of(u):
            kind, blk = UNITS[u]
            return NCMP if kind == "C" else P * (blk + 1)

        names1 = """sq_ready rms_in rms_out xm_written qi_raw perms_done roped blk_ready cmp_raw cmp_done idx_scores_out
                    idx_relu idx_used scores_out soft_max exp_done p_ready pt_ready pt_copied pv_done o_taken pool_in pool_out
                    var_ready root_done mixh_done mixl_done gates_e kc_ready rms_sum sc_ready x_ready
                    md_tmp xm_hi xm_lo x_scaled gate_act h_hi h_lo ln_sq ln_in ln_sum
                    z_out z_in z_ln ge_in ge_done kq_ready kd_t kdt_done att_out att_masked u_out s_ready og_out oa_done
                    gq_sum gq_sq mg_hi mg_ready cq_sq cq_sum cq_ready cq_hi cq_lo qk2_ready rm_out c2_in c3_in
                    fmax fsoft fexp fnorm ftr fcopy fpv fhi flo qkv_ready""".split()
        ev_ = {n: sig(n) for n in names1}

        block = ctx.enter_context(nc.Block())

        @block.sync
        def _(sp):
            for name, n, f in RUNS:
                if START[name] > UPTO_SLAB:
                    break

                def load(i, k, name=name, f=f):
                    if i.base >= RING:
                        sp.wait_ge(lo_done, i.count(4, i.base - RING + 1))
                    src = a[name][bass.ds(k, 1)].rearrange("a p n -> p (a n)") if i.reg is not None else a[name][k]
                    sp.dma_start(raw[:, i.slot, 0:f], src).then_inc(slab_full[i.slot], 16)
                if START[name] == UPTO_SLAB:
                    load(Idx(UPTO_SLAB), 0)
                    break
                runs_of(sp, name, load)
            sp.wait_ge(ev_["x_ready"], UPTO)
            sp.dma_start(a["out"], X[:, :, 0:T]).then_inc(out_stored, 16)
            sp.wait_ge(out_stored, 16)

        @block.gpsimd
        def _(pool):
            for s in range(2):
                pool.dma_start(ada[:, s, :], a["ada"][s]).then_inc(ada_full[s], 16)
            with pool.Fori(1, NADA // 2) as it:
                for s in range(2):
                    pool.wait_ge(ada_used, it * 2 + (s - 1))
                    pool.dma_start(ada[:, s, :], a["ada"][bass.ds(it * 2 + s, 1)].rearrange("a p n -> p (a n)"))\
                        .then_inc(ada_full[s], 16)

        FFN_STAGES = {0: (0, 1, 0, 2 * T), 2: (0, 2, 6, 2 * T), 3: (1, 1, 0, 2 * T), 5: (1, 2, 6, T)}
        WIDTH = [2 * T, 2 * T, 2 * T, 2 * T, T, T]
        X0 = DEPTH + 1
        SQ, HF, SI, NRM, HH, HL = (ff[n] for n in ("SQ", "HF", "SI", "NRM", "HH", "HL"))
        c2 = ev["c2"]
        W = ev["W"]
        work = lambda n: W[:, 2 * n:2 * n + 2, :]
        G_, B_, T1, QE, KE, QB = range(6)
        AM = W[:, 2 * T1:2 * T1 + 2, :].rearrange("p a (b t) -> p a b t", t=GC)
        ORDER = ([4, 5, 6, 7, 0, 1, 2, 3], [7, 6, 5, 4, 3, 2, 1, 0])
        MLA_UNITS = [(h, blk, 0) for h in range(4) for blk in range(2)] + [(h, blk, 1) for h in range(4) for blk in range(2)]
        NA_UNITS = [(h, blk, 0) for h in range(16) for blk in range(2)]

        def hidden_before(m, half):
            return ([0, 2, 3, 5].index(m) * 2 + half) * FH

        def act_modulate(act, m, l, j, n):
            act.wait_ge(ev_["x_ready"], X0 + m)
            for k in range(KT):
                for br in range(n // T):
                    mm = act.activation(xh[:, k, br * T:(br + 1) * T], X[:, k, br * T:(br + 1) * T], ACT.Identity,
                                        bias=mod[:, l, j, k, br:br + 1], scale=mod[:, l, j + 1, k, br:br + 1])
            mm.then_inc(ev_["xm_hi"], 1)
            act.wait_ge(ev_["xm_hi"], m + 1)
            act.wait_ge(ev_["md_tmp"], m + 1)
            act.activation(X[:, :, 0:WIDTH[m]], X[:, :, 0:WIDTH[m]], ACT.Copy, scale=ALPHA).then_inc(ev_["x_scaled"], 1)

        def dve_modulate(dve, m, l, j, n):
            dve.wait_ge(ev_["x_ready"], X0 + m)
            for k in range(KT):
                for br in range(n // T):
                    mm = dve.tensor_scalar(SQ[:, k, br * T:(br + 1) * T], X[:, k, br * T:(br + 1) * T],
                                           mod[:, l, j + 1, k, br:br + 1], mod[:, l, j, k, br:br + 1], ALU.mult, ALU.add)
            mm.then_inc(ev_["md_tmp"], 1)
            dve.wait_ge(ev_["md_tmp"], m + 1)
            dve.wait_ge(ev_["xm_hi"], m + 1)
            dve.tensor_tensor(xl[:, :, 0:n], SQ[:, :, 0:n], xh[:, :, 0:n].bitcast(F32), ALU.subtract)\
                .then_inc(ev_["xm_lo"], 1)

        def last_pair(eng, i):
            for par in range(2):
                last = i.base - (i.base - par) % 2
                eng.wait_ge(drained[par], last // 2 + 1)

        def add_residual(dve, m, l, j, i, k, bank, inc):
            for br in range(WIDTH[m] // T):
                if i.reg is None:
                    xk, g = X[:, k, br * T:(br + 1) * T], mod[:, l, j, k, br:br + 1]
                else:
                    xk = X[:, bass.ds(k, 1), br * T:(br + 1) * T].rearrange("p a t -> p (a t)")
                    g = mod[:, l, j, bass.ds(k, 1), br]
                mm = dve.scalar_tensor_tensor(out=xk, in0=PS[:, bank, br * T:(br + 1) * T], scalar=g, in1=xk,
                                              op0=ALU.mult, op1=ALU.add)
            if inc:
                mm.then_inc(drained[i.par], 1)

        def act_squares(act, m, i):
            last_pair(act, i)
            n = WIDTH[m]
            act.activation(SQ[:, :, 0:n], X[:, :, 0:n], ACT.Square).then_inc(ev_["ln_sq"], 1)
            act_root(act, NRM[:, 3, 0:n])

        def pe_sums(pe, m):
            n = WIDTH[m]
            for j in range(2):
                pe.wait_ge(ev_["ln_in"], 2 * m + j + 1)
                mm = pe.matmul(PS[:, 4 + j, 0:n], ones, NRM[:, j, 0:n], start=True, stop=True)
            mm.then_inc(ev_["ln_sum"], 1)

        def post_norm(dve, ch, m, i):
            n = WIDTH[m]
            last_pair(dve, i)
            dve.tensor_reduce(NRM[:, 0, 0:n], X[:, :, 0:n].rearrange("p k t -> p t k"), AX, ALU.add)\
                .then_inc(ev_["ln_in"], 1)
            dve.wait_ge(ev_["ln_sq"], m + 1)
            dve.tensor_reduce(NRM[:, 1, 0:n], SQ[:, :, 0:n].rearrange("p k t -> p t k"), AX, ALU.add)\
                .then_inc(ev_["ln_in"], 1)
            dve.wait_ge(ev_["ln_sum"], m + 1)
            mean, var = NRM[:, 2, 0:n], NRM[:, 3, 0:n]
            ch.after(dve.tensor_scalar(mean, PS[:, 4, 0:n], 1.0 / D, None, ALU.mult))
            ch.after(dve.tensor_tensor(var, mean, mean, ALU.mult))
            ch.after(dve.scalar_tensor_tensor(out=var, in0=PS[:, 5, 0:n], scalar=1.0 / D, in1=var,
                                              op0=ALU.mult, op1=ALU.subtract))
            inverse_root(ch, dve, var, dve.tensor_scalar(var, var, 0.0, EPS, ALU.max, ALU.add))
            ch.after(dve.tensor_tensor(X[:, :, 0:n], X[:, :, 0:n], bc(mean, KT), ALU.subtract))
            dve.tensor_tensor(X[:, :, 0:n], X[:, :, 0:n], bc(var, KT), ALU.mult).then_inc(ev_["x_ready"], 1)

        def act_ffn(act, m):
            l, f, j, n = FFN_STAGES[m]
            act_modulate(act, m, l, j, n)
            for half in range(2):
                def gate(i, k):
                    act_ahead(act, i)
                    act.wait_ge(slab_used, i.count(4, i.base + 1))
                    act.activation(SI[:, i.par, 0:n], PS[:, 2 * i.par, 0:n], ACT.Silu).then_inc(ev_["gate_act"], 1)
                runs_of(act, f"ffi{f}{l}{half}", gate)
                runs_of(act, f"ffo{f}{l}{half}", lambda i, k: act_ahead(act, i))
            act_squares(act, m, Idx(START[f"ffo{f}{l}1"] + KT - 1))

        def pe_ffn(pe, m):
            l, f, j, n = FFN_STAGES[m]
            pe.wait_ge(ev_["xm_lo"], m + 1)
            for half in range(2):
                runs_of(pe, f"ffi{f}{l}{half}", lambda i, k: dense(pe, i, 2, KT, xh, xl, 0, n))
                pe.wait_ge(ev_["h_lo"], hidden_before(m, half) + FH)
                runs_of(pe, f"ffo{f}{l}{half}", lambda i, k: dense(pe, i, 1, FH, HH, HL, 0, n))
            pe_sums(pe, m)

        def dve_ffn(dve, ch, m):
            l, f, j, n = FFN_STAGES[m]
            dve_modulate(dve, m, l, j, n)
            dve.wait_ge(ev_["x_scaled"], m + 1)
            for half in range(2):
                h0 = hidden_before(m, half)

                def hidden(i, k):
                    dve_ahead(dve, i)
                    dve.wait_ge(ev_["gate_act"], k + (h0 + 1))
                    hf = HF[:, i.par, 0:n]
                    dve.tensor_tensor(hf, SI[:, i.par, 0:n], PS[:, 2 * i.par + 1, 0:n], ALU.mult)\
                        .then_inc(drained[i.par], 1)
                    dve.wait_ge(drained[i.par], i.count(2, i.base // 2 + 1))
                    if i.reg is None:
                        hh, hl = HH[:, k, 0:n], HL[:, k, 0:n]
                    else:
                        hh = HH[:, bass.ds(k, 1), 0:n].rearrange("p a t -> p (a t)")
                        hl = HL[:, bass.ds(k, 1), 0:n].rearrange("p a t -> p (a t)")
                    dve.tensor_copy(hh, hf).then_inc(ev_["h_hi"], 1)
                    dve.wait_ge(ev_["h_hi"], k + (h0 + 1))
                    dve.tensor_tensor(hl, hf, hh.bitcast(F32), ALU.subtract).then_inc(ev_["h_lo"], 1)
                runs_of(dve, f"ffi{f}{l}{half}", hidden)

                def down(i, k):
                    dve_ahead(dve, i)
                    dve.wait_ge(slab_used, i.count(4, i.base + 1))
                    add_residual(dve, m, l, j + 2, i, k, 2 * i.par, True)
                runs_of(dve, f"ffo{f}{l}{half}", down)
            post_norm(dve, ch, m, Idx(START[f"ffo{f}{l}1"] + KT - 1))

        def unit_keys(units, u):
            return (0, 2 * T) if units[u][2] == 0 else (T, 2 * T)

        def groups(units, na):
            step = 4 if na else 2
            return {g * step + step - 1: g for g in range(len(units) // step)}

        def pe_attend(pe, units, na, f0, g0, q_ap, k_ap, v_ap, pr, ptm):
            ends = groups(units, na)

            def score(u):
                h, blk, ctx_ = units[u]
                k0, k1 = unit_keys(units, u)
                if f0 + u >= 2 and u >= 2:
                    pe.wait_ge(ev_["fexp"], f0 + u - 1)
                pairs = q_ap(h, ctx_ * T + blk * P, k0, k1)
                for n, (q, k) in enumerate(pairs):
                    mm = pe.matmul(PS[:, u % 2, 0:k1 - k0], q, k, start=n == 0, stop=n == len(pairs) - 1)
                mm.then_inc(ev_["fmax"], 1)
            score(0)
            score(1)
            for u in range(len(units)):
                h, blk, ctx_ = units[u]
                k0, k1 = unit_keys(units, u)
                pe.wait_ge(ev_["fnorm"], f0 + u + 1)
                if u >= 2:
                    pe.wait_ge(ev_["fcopy"], f0 + u - 1)
                for kt in range((k1 - k0) // P):
                    mm = pe.transpose(PS[:, 2 + u % 2, kt * P:(kt + 1) * P], pr[:, u % 2, kt * P:(kt + 1) * P], ident)
                mm.then_inc(ev_["ftr"], 1)
                if u + 2 < len(units):
                    score(u + 2)
                pe.wait_ge(ev_["fcopy"], f0 + u + 1)
                g = u // (4 if na else 2)
                if g >= 2 and u % (4 if na else 2) == 0:
                    pe.wait_ge(ev_["flo"], g0 + g - 1)
                rows = slice((h % 2) * HD, (h % 2) * HD + HD) if na else slice(0, P)
                nk = (k1 - k0) // P
                for kt in range(nk):
                    mm = pe.matmul(PS[rows, 4 + g % 2, blk * P:(blk + 1) * P], v_ap(h, k0 // P + kt),
                                   ptm[:, u % 2, kt * P:(kt + 1) * P], start=kt == 0, stop=kt == nk - 1)
                mm.then_inc(ev_["fpv"], 1)

        def act_attend(act, units, na, f0, g0, scale, pr, ptm, chunk0):
            ends = groups(units, na)

            def exp(u):
                k0, k1 = unit_keys(units, u)
                act.wait_ge(ev_["fsoft"], f0 + u + 1)
                if u >= 2:
                    act.wait_ge(ev_["ftr"], f0 + u - 1)
                act.activation(pr[:, u % 2, 0:k1 - k0], PS[:, u % 2, 0:k1 - k0], ACT.Exp, scale=scale,
                               bias=tiny[:, u % 2:u % 2 + 1], accum_out=tiny[:, 2 + u % 2:3 + u % 2]).then_inc(ev_["fexp"], 1)

            def hi(g):
                size = 4 if na else 2
                act.wait_ge(ev_["fpv"], f0 + (g + 1) * size)
                ctx_ = units[g * size][2]
                act.activation(xh[:, chunk0 + g % (8 if na else 4), ctx_ * T:ctx_ * T + T], PS[:, 4 + g % 2, 0:T], ACT.Copy)\
                    .then_inc(ev_["fhi"], 1)
            exp(0)
            for u in range(len(units)):
                if u + 1 < len(units):
                    exp(u + 1)
                k0, k1 = unit_keys(units, u)
                act.wait_ge(ev_["ftr"], f0 + u + 1)
                if u >= 2:
                    act.wait_ge(ev_["fpv"], f0 + u - 1)
                act.activation(ptm[:, u % 2, 0:k1 - k0], PS[:, 2 + u % 2, 0:k1 - k0], ACT.Copy).then_inc(ev_["fcopy"], 1)
                if u - 1 in ends:
                    hi(ends[u - 1])
            hi(ends[len(units) - 1])

        def dve_attend(dve, ch, units, na, f0, g0, scale, pr, chunk0):
            ends = groups(units, na)

            def maxima(u):
                h, blk, ctx_ = units[u]
                k0, k1 = unit_keys(units, u)
                dve.wait_ge(ev_["fmax"], f0 + u + 1)
                s = PS[:, u % 2, 0:k1 - k0]
                if na:
                    for half in range(2):
                        r, rows = 2 * blk + half, slice(half * HD, half * HD + HD)
                        o = PS[rows, u % 2, 0:T].rearrange("p (r c) -> p r c", c=64)
                        mm = dve.tensor_tensor(o, o, od["RPB"][rows, h, 3 - r:7 - r, :], ALU.add)
                    ch.after(mm)
                nm = tiny[:, u % 2:u % 2 + 1]
                mm = dve.tensor_reduce(nm, s, AX, ALU.max, negate=True)
                if scale != 1.0:
                    ch.after(mm)
                    mm = dve.tensor_scalar(nm, nm, scale, None, ALU.mult)
                mm.then_inc(ev_["fsoft"], 1)

            def lo(g):
                size = 4 if na else 2
                dve.wait_ge(ev_["fhi"], g0 + g + 1)
                ctx_ = units[g * size][2]
                c = chunk0 + g % (8 if na else 4)
                dve.tensor_tensor(xl[:, c, ctx_ * T:ctx_ * T + T], PS[:, 4 + g % 2, 0:T],
                                  xh[:, c, ctx_ * T:ctx_ * T + T].bitcast(F32), ALU.subtract).then_inc(ev_["flo"], 1)
            maxima(0)
            for u in range(len(units)):
                if u + 1 < len(units):
                    maxima(u + 1)
                k0, k1 = unit_keys(units, u)
                dve.wait_ge(ev_["fexp"], f0 + u + 1)
                r = tiny[:, 4 + u % 2:5 + u % 2]
                mm = dve.reciprocal(r, tiny[:, 2 + u % 2:3 + u % 2])
                ch.after(mm)
                p = pr[:, u % 2, 0:k1 - k0]
                dve.tensor_scalar(p, p, r, None, ALU.mult).then_inc(ev_["fnorm"], 1)
                if u - 2 in ends:
                    lo(ends[u - 2])
            lo(ends[len(units) - 1])

        def act_even(act, ch):
            act.wait_ge(ev_["x_ready"], X0 + 1)
            act.dma_start(c2[:, :], a["c2"]).then_inc(ev_["c2_in"], 16)
            act_modulate(act, 1, 0, 3, 2 * T)
            s0 = START["even"]
            for k in range(9):
                i = Idx(s0 + k)
                act_ahead(act, i)
                if k >= 7:
                    act.wait_ge(slab_used, i.base + 1)
                    act.activation(ev["RS"][:, 2 * (k - 7):2 * (k - 7) + 2, :], banks(i, 2 * T), ACT.Silu)\
                        .then_inc(drained[i.par], 1)
            for d in range(2):
                act.wait_ge(ev_["z_in"], d + 1)
                ch.after(act.activation(work(T1), work(T1), ACT.Exp))
                act.activation(work(T1), work(T1), ACT.Ln, bias=1.0).then_inc(ev_["z_ln"], 1)
                act.wait_ge(ev_["ge_in"], 2 * d + 1)
                act.activation(work(QE), work(T1), ACT.Exp)
                act.activation(work(KE), work(T1), ACT.Exp, scale=-1.0)
                act.activation(work(QB), work(B_), ACT.Exp).then_inc(ev_["ge_done"], 1)
                act.wait_ge(ev_["ge_in"], 2 * d + 2)
                act.activation(work(G_), work(G_), ACT.Exp)
                act.activation(tiny[:, 32:48], tiny[:, 0:16], ACT.Exp).then_inc(ev_["ge_done"], 1)
                act.wait_ge(ev_["kd_t"], d + 1)
                act.activation(ev["KDT"][:, :, :, :], PS[:, 4:6, :].rearrange("p a (t c) -> p a t c", c=P), ACT.Copy)\
                    .then_inc(ev_["kdt_done"], 1)
            act.wait_ge(ev_["oa_done"], 2)
            act.activation(W[:, 0:4, :], ev["OA"][:, :, :], ACT.Square).then_inc(ev_["gq_sq"], 1)
            act_root(act, W[:, 4:8, :])
            act.wait_ge(ev_["mg_ready"], 1)
            act.activation(xh[:, 0:4, :], ev["OA"][:, :, :], ACT.Copy).then_inc(ev_["mg_hi"], 1)
            act.activation(ml["QN"][:, :, :], ev["CQ"][:, :, :], ACT.Square).then_inc(ev_["cq_sq"], 1)
            for j in range(2):
                act_root(act, ml["VM"][:, j, :])
            act.wait_ge(ev_["cq_ready"], 1)
            act.activation(ml["CH"][:, :, :], ml["QN"][:, :, :], ACT.Copy).then_inc(ev_["cq_hi"], 1)
            for k in range(7):
                act_ahead(act, Idx(START["uq"] + k))
            act_attend(act, MLA_UNITS, False, 0, 0, MLA_SCALE, ml["PR"], ml["PTM"], 4)
            for k in range(4):
                act_ahead(act, Idx(START["eout"] + k))
            act_squares(act, 1, Idx(START["eout"] + 3))

        def pe_even(pe):
            pe.wait_ge(ev_["xm_lo"], 2)
            s0 = START["even"]
            for k in range(9):
                i = Idx(s0 + k)
                if k in (3, 4):
                    token_major(pe, i, 4, 256, xh, xl, KT)
                else:
                    dense(pe, i, 2, KT, xh, xl, 0, 2 * T)
            last_pair(pe, Idx(s0 + 8))
            Qw, Kw = QE, KE
            for d in range(2):
                if d:
                    pe.wait_ge(ev_["oa_done"], d)
                o, _ = SML["wg2"]
                for ft in range(2):
                    r = slice(32 * d, 32 * d + 16)
                    mm = pe.matmul(PS[:, 4 + ft, :], sml[r, o + ft * P:o + (ft + 1) * P], ev["LK"][r, 0, :], start=True, stop=True)
                mm.then_inc(ev_["z_out"], 1)
                pe.wait_ge(ev_["kq_ready"], d + 1)
                for ft in range(2):
                    for tt in range(4):
                        mm = pe.transpose(PS[:, 4 + ft, tt * P:(tt + 1) * P], W[:, 2 * G_ + ft, tt * P:(tt + 1) * P], ident)
                mm.then_inc(ev_["kd_t"], 1)
                for c in range(8):
                    for h in range(4):
                        r, ft, tt = slice((h % 2) * HD, (h % 2) * HD + HD), h // 2, c // 2
                        mm = pe.matmul(PS[(c % 2) * HD:(c % 2) * HD + HD, h % 2, (tt * 2 + ft) * GC:(tt * 2 + ft + 1) * GC],
                                       W[r, 2 * KE + ft, c * GC:(c + 1) * GC], W[r, 2 * QE + ft, c * GC:(c + 1) * GC],
                                       start=True, stop=True)
                mm.then_inc(ev_["att_out"], 1)
                pe.wait_ge(ev_["kdt_done"], d + 1)
                for c in ORDER[d][:7]:
                    cp, tt = c % 2, c // 2
                    rows = slice(cp * HD, cp * HD + HD)
                    for h in range(4):
                        o = (tt % 2) * 256 + (h // 2) * P
                        mm = pe.matmul(PS[(h % 2) * HD:(h % 2) * HD + HD, 2 + 4 * cp + tt // 2, o:o + P],
                                       ev["KDT"][rows, h // 2, tt, (h % 2) * HD:(h % 2) * HD + HD],
                                       ev["V"][rows, tt, h * P:(h + 1) * P], start=True, stop=True)
                mm.then_inc(ev_["u_out"], 1)
                pe.wait_ge(ev_["att_masked"], d + 1)
                pe.wait_ge(ev_["s_ready"], d + 1)
                for c in range(8):
                    cp, tt, n = c % 2, c // 2, ORDER[d].index(c)
                    tp = tt // 2
                    for h in range(4):
                        rows = slice(cp * HD, cp * HD + HD)
                        o = ((tt % 2) * 4 + h) * GC
                        pe.matmul(PS[:, 2 * tp + cp, o:o + GC], ev["V"][rows, tt, h * P:(h + 1) * P],
                                  AM[rows, h % 2, tt * 2 + h // 2, :], start=True, stop=True)
                        r = slice((h % 2) * HD, (h % 2) * HD + HD)
                        o = (h // 2) * T + (c % 4) * GC
                        mm = pe.matmul(PS[:, 4 + 2 * tp + h % 2, o:o + GC], ev["S"][r, n, h // 2, :],
                                       W[r, 2 * QB + h // 2, c * GC:(c + 1) * GC], start=True, stop=True)
                mm.then_inc(ev_["og_out"], 1)
            pe.wait_ge(ev_["gq_sq"], 1)
            for h in range(4):
                mm = pe.matmul(PS[:, h, :], ones, W[:, h, :], start=True, stop=True)
            mm.then_inc(ev_["gq_sum"], 1)
            pe.wait_ge(ev_["cq_sq"], 1)
            for k in range(3):
                pe.matmul(PS[:, 4, :], ones, ml["QN"][:, k, :], start=k == 0, stop=k == 2)
            pe.matmul(PS[:, 5, :], ones, ml["QN"][:, 3, :], start=True, stop=True).then_inc(ev_["cq_sum"], 1)
            pe.wait_ge(ev_["cq_lo"], 1)
            for k in range(3):
                dense(pe, Idx(START["uq"] + k), 2, 3, ml["CH"], ml["CL"], 0, 2 * T)
            for k in range(4):
                i = Idx(START["ukv"] + k)
                if k < 2:
                    slab_begin(pe, i)
                    for c in range(2):
                        mm = product(pe, PS[:, 2 * i.par + c, :], i, [(c * P, ml["CH"][:, 3, :], ml["CL"][:, 3, :])])
                    mm.then_inc(slab_used, 1)
                else:
                    token_major(pe, i, 4, 256, ml["CH"], ml["CL"], 1, krow=3)
            last_pair(pe, Idx(START["ukv"] + 3))
            pe.matmul(PS[:, 4, :], cst("permM"), ml["QR"][:, :, 0:T], start=True, stop=True)
            pe.matmul(PS[:, 5, 0:T], cst("permM"), ev["LK"][:, 1, 0:T], start=True, stop=True).then_inc(ev_["rm_out"], 1)
            pe.wait_ge(ev_["qk2_ready"], 1)

            def qk(h, q0, k0, k1):
                r = slice((h % 2) * HD, (h % 2) * HD + HD)
                return [(ml["QN"][:, h, q0:q0 + P], ml["KN"][:, h, k0:k1]), (ml["QR"][r, h // 2, q0:q0 + P], ev["LK"][r, 1, k0:k1])]
            pe_attend(pe, MLA_UNITS, False, 0, 0, qk, None, lambda h, tt: ml["VM"][:, tt, h * P:(h + 1) * P], ml["PR"], ml["PTM"])
            pe.wait_ge(ev_["flo"], 8)
            for k in range(4):
                dense(pe, Idx(START["eout"] + k), 2, KT, xh, xl, 0, 2 * T)
            pe_sums(pe, 1)

        def dve_even(dve, ch):
            dve_modulate(dve, 1, 0, 3, 2 * T)
            s0 = START["even"]
            for k in range(9):
                i = Idx(s0 + k)
                dve_ahead(dve, i)
                if k >= 7:
                    continue
                dve.wait_ge(slab_used, i.base + 1)
                if k == 0:
                    mm = dve.tensor_scalar(ev["Q"][:, :, :], banks(i, 2 * T), HD ** -0.5, None, ALU.mult)
                elif k in (1, 2):
                    mm = dve.tensor_copy(ev["K" if k == 1 else "LK"][:, :, :], banks(i, 2 * T))
                elif k in (3, 4):
                    mm = dve.tensor_copy(ev["V"][:, :, 256 * (k - 3):256 * (k - 2)],
                                         banks(i, 512).rearrange("p a (b n) -> p (a b) n", b=2))
                else:
                    mm = dve.tensor_copy(ev["CQ"][:, 2 * (k - 5):2 * (k - 5) + 2, :], banks(i, 2 * T))
                mm.then_inc(drained[i.par], 1)
            dve.wait_ge(ev_["c2_in"], 16)
            S = ev["S"]
            dve.memset(S[:, 0, :, :], 0.0)
            chunks = lambda t: t.rearrange("p f (c t) -> p (f c) t", t=GC)
            for d in range(2):
                dve.wait_ge(ev_["z_out"], d + 1)
                for ft in range(2):
                    mm = dve.tensor_scalar(W[:, 2 * G_ + ft, :], PS[:, 4 + ft, :], vcol("bg", 2 * d + ft), None, ALU.add)
                ch.after(mm)
                dve.scalar_tensor_tensor(out=work(T1), in0=work(G_), scalar=-1.0, in1=work(G_), op0=ALU.mult, op1=ALU.min)\
                    .then_inc(ev_["z_in"], 1)
                dve.wait_ge(ev_["z_in"], d + 1)
                ch.after(dve.tensor_scalar(work(G_), work(G_), 0.0, 1.0 / 16, ALU.min, ALU.mult))
                dve.wait_ge(ev_["z_ln"], d + 1)
                ch.after(dve.scalar_tensor_tensor(out=work(G_), in0=work(T1), scalar=-1.0 / 16, in1=work(G_),
                                                  op0=ALU.mult, op1=ALU.add))
                for ft in range(2):
                    mm = dve.tensor_tensor_scan(W[:, 2 * B_ + ft, :], cst("reset", c2, C2), W[:, 2 * G_ + ft, :], 0.0,
                                                ALU.mult, ALU.add)
                ch.after(mm)
                g, b, t1 = chunks(work(G_)), chunks(work(B_)), chunks(work(T1))
                tot, ref = tiny[:, 0:16], tiny[:, 16:32]
                ch.after(dve.tensor_copy(tot, b[:, :, GC - 1]))
                if d:
                    ch.after(dve.tensor_tensor(b, bl(tot, GC), b, ALU.subtract))
                    ch.after(dve.tensor_tensor(b, b, g, ALU.add))
                ch.after(dve.tensor_copy(ref, b[:, :, GC // 2 - 1 + d]))
                ch.after(dve.tensor_tensor(t1, b, bl(ref, GC), ALU.subtract))
                dve.tensor_scalar(work(T1), work(T1), 80.0, -80.0, ALU.min, ALU.max).then_inc(ev_["ge_in"], 1)
                dve.tensor_tensor(g, bl(tot, GC), b, ALU.subtract).then_inc(ev_["ge_in"], 1)
                dve.wait_ge(ev_["ge_in"], 2 * d + 2)
                dve.wait_ge(ev_["ge_done"], 2 * d + 1)
                dve.tensor_tensor(work(QE), work(QE), ev["Q"][:, :, :], ALU.mult)
                dve.tensor_tensor(work(KE), work(KE), ev["K"][:, :, :], ALU.mult)
                dve.tensor_tensor(work(QB), work(QB), ev["Q"][:, :, :], ALU.mult)
                dve.wait_ge(ev_["ge_done"], 2 * d + 2)
                dve.tensor_tensor(work(G_), work(G_), ev["K"][:, :, :], ALU.mult).then_inc(ev_["kq_ready"], 1)
                dve.wait_ge(ev_["att_out"], d + 1)
                mk = cst("gmask", c2, C2)[:, d * GC:(d + 1) * GC]
                dve.tensor_tensor(AM[:, :, :, :].rearrange("p a b t -> p (a b) t"),
                                  PS[:, 0:2, :].rearrange("p a (b t) -> p (a b) t", t=GC), bc(mk, 16), ALU.mult)\
                    .then_inc(ev_["att_masked"], 1)
                dve.wait_ge(ev_["u_out"], d + 1)
                for n, c in enumerate(ORDER[d][:7]):
                    cp, tt = c % 2, c // 2
                    u = PS[:, 2 + 4 * cp + tt // 2, (tt % 2) * 256:(tt % 2) * 256 + 256].rearrange("p (f t) -> p f t", f=2)
                    if n == 0:
                        mm = dve.tensor_copy(S[:, 1, :, :], u)
                    else:
                        for ft in range(2):
                            mm = dve.scalar_tensor_tensor(out=S[:, n + 1, ft, :], in0=S[:, n, ft, :],
                                                          scalar=tiny[:, 32 + 8 * ft + c:33 + 8 * ft + c], in1=u[:, ft, :],
                                                          op0=ALU.mult, op1=ALU.add)
                    if n < 6:
                        ch.after(mm)
                mm.then_inc(ev_["s_ready"], 1)
                dve.wait_ge(ev_["og_out"], d + 1)
                OA = ev["OA"]
                for tp in range(2):
                    for cp in range(2):
                        o = OA[:, :, tp * T:(tp + 1) * T].rearrange("p h (t c i) -> p t h c i", t=2, c=2)[:, :, :, cp, :]
                        src = PS[:, 2 * tp + cp, :].rearrange("p (t h i) -> p t h i", t=2, h=4)
                        if d == 0:
                            mm = dve.tensor_copy(o, src)
                        else:
                            mm = dve.tensor_tensor(o, o, src, ALU.add)
                    ch.after(mm)
                    for hp in range(2):
                        o = OA[:, :, tp * T:(tp + 1) * T].rearrange("p (f q) t -> p f q t", q=2)[:, :, hp, :]
                        src = PS[:, 4 + 2 * tp + hp, :].rearrange("p (f t) -> p f t", f=2)
                        mm = dve.tensor_tensor(o, o, src, ALU.add)
                    if tp == 0:
                        ch.after(mm)
                mm.then_inc(ev_["oa_done"], 1)
                dve.wait_ge(ev_["oa_done"], d + 1)
            dve.wait_ge(ev_["gq_sum"], 1)
            rs = W[:, 4:8, :]
            rstd(ch, dve, rs, PS[:, 0:4, :], P)
            ch.after(dve.tensor_tensor(OA[:, :, :], OA[:, :, :], rs, ALU.mult))
            dve.scalar_tensor_tensor(out=OA[:, :, :], in0=OA[:, :, :], scalar=vcol("gnorm", 0), in1=ev["RS"][:, :, :],
                                     op0=ALU.mult, op1=ALU.mult).then_inc(ev_["mg_ready"], 1)
            dve.wait_ge(ev_["mg_hi"], 1)
            ch.after(dve.tensor_tensor(xl[:, 0:4, :], OA[:, :, :], xh[:, 0:4, :].bitcast(F32), ALU.subtract))
            CQ, QN, VM = ev["CQ"], ml["QN"], ml["VM"]
            dve.wait_ge(ev_["cq_sum"], 1)
            for j, n in ((0, 384), (1, P)):
                rstd(ch, dve, VM[:, j, :], PS[:, 4 + j, :], n)
            for k in range(4):
                g = vcol("qnorm", k) if k < 3 else vcol("kvnorm", 0)
                mm = dve.scalar_tensor_tensor(out=QN[:, k, :], in0=CQ[:, k, :], scalar=g, in1=VM[:, k // 3, :],
                                              op0=ALU.mult, op1=ALU.mult)
            mm.then_inc(ev_["cq_ready"], 1)
            dve.wait_ge(ev_["cq_hi"], 1)
            dve.tensor_tensor(ml["CL"][:, :, :], QN[:, :, :], ml["CH"][:, :, :].bitcast(F32), ALU.subtract)\
                .then_inc(ev_["cq_lo"], 1)
            dve.wait_ge(ev_["cq_lo"], 1)
            for k in range(7):
                i = Idx(START["uq"] + k)
                dve_ahead(dve, i)
                dve.wait_ge(slab_used, i.base + 1)
                if k < 2:
                    mm = dve.tensor_copy(QN[:, 2 * k:2 * k + 2, :], banks(i, 2 * T))
                elif k == 2:
                    mm = dve.tensor_copy(ml["QR"][:, :, :], banks(i, 2 * T))
                elif k < 5:
                    mm = dve.tensor_copy(ml["KN"][:, 2 * (k - 3):2 * (k - 3) + 2, :], banks(i, 2 * T))
                else:
                    mm = dve.tensor_copy(VM[:, :, 256 * (k - 5):256 * (k - 4)],
                                         banks(i, 512).rearrange("p a (b n) -> p (a b) n", b=2))
                mm.then_inc(drained[i.par], 1)
            dve.wait_ge(ev_["rm_out"], 1)
            cs = cst("ropeM", c2, C2)
            CT, ST = cs[:, 0:T], cs[:, T:2 * T]
            LK, PR, QR = ev["LK"], ml["PR"], ml["QR"]
            rq, rk = PR[:, 0, :].rearrange("p (c t) -> p c t", c=2), PR[:, 1, 0:T]
            dve.tensor_tensor(rq, PS[:, 4, :].rearrange("p (c t) -> p c t", c=2), bc(ST, 2), ALU.mult)
            dve.tensor_tensor(rk, PS[:, 5, 0:T], ST, ALU.mult)
            dve.tensor_tensor(QR[:, :, 0:T], QR[:, :, 0:T], bc(CT, 2), ALU.mult)
            ch.after(dve.tensor_tensor(LK[:, 1, 0:T], LK[:, 1, 0:T], CT, ALU.mult))
            dve.tensor_tensor(QR[:, :, 0:T], QR[:, :, 0:T], rq, ALU.add)
            dve.tensor_tensor(LK[:, 1, 0:T], LK[:, 1, 0:T], rk, ALU.add).then_inc(ev_["qk2_ready"], 1)
            dve_attend(dve, ch, MLA_UNITS, False, 0, 0, MLA_SCALE, ml["PR"], 4)
            dve_out(dve, ch, 1, 0, "eout")

        def dve_out(dve, ch, m, l, name):
            dve.wait_ge(ev_["x_scaled"], m + 1)
            for k in range(4):
                i = Idx(START[name] + k)
                dve_ahead(dve, i)
                dve.wait_ge(slab_used, i.base + 1)
                for c in range(2):
                    add_residual(dve, m, l, 5, i, 2 * k + c, 2 * i.par + c, c == 1)
            post_norm(dve, ch, m, i)

        def act_odd(act, ch):
            act.wait_ge(ev_["x_ready"], X0 + 4)
            act.dma_start(od["nmask"][:, :], a["nmask"]).then_inc(ev_["c3_in"], 16)
            act.dma_start(od["RPB"][:, :, :, :], a["rpb"]).then_inc(ev_["c3_in"], 16)
            act_modulate(act, 4, 1, 3, 2 * T)
            for k in range(12):
                act_ahead(act, Idx(START["odd"] + k))
            act_attend(act, NA_UNITS, True, 16, 8, 1.0, od["NP"], od["NPT"], 0)
            for k in range(4):
                act_ahead(act, Idx(START["oout"] + k))
            act_squares(act, 4, Idx(START["oout"] + 3))

        def pe_odd(pe):
            pe.wait_ge(ev_["xm_lo"], 5)
            for k in range(12):
                i = Idx(START["odd"] + k)
                if k < 8:
                    dense(pe, i, 2, KT, xh, xl, 0, T if k < 4 else 2 * T)
                else:
                    token_major(pe, i, 4, 256, xh, xl, KT)
            last_pair(pe, Idx(START["odd"] + 11))
            pe.wait_ge(ev_["qkv_ready"], 1)

            def qk(h, q0, k0, k1):
                r = slice((h % 2) * HD, (h % 2) * HD + HD)
                return [(od["NQ"][r, h // 2, q0:q0 + P], od["NK"][r, h // 2, k0:k1])]
            pe_attend(pe, NA_UNITS, True, 16, 8, qk, None, lambda h, tt: od["NV"][:, tt, h * HD:(h + 1) * HD], od["NP"], od["NPT"])
            pe.wait_ge(ev_["flo"], 16)
            for k in range(4):
                dense(pe, Idx(START["oout"] + k), 2, KT, xh, xl, 0, T)
            pe_sums(pe, 4)

        def dve_odd(dve, ch):
            dve_modulate(dve, 4, 1, 3, 2 * T)
            for k in range(12):
                i = Idx(START["odd"] + k)
                dve_ahead(dve, i)
                dve.wait_ge(slab_used, i.base + 1)
                if k < 4:
                    mm = dve.tensor_scalar(od["NQ"][:, 2 * k:2 * k + 2, :], banks(i, T), HD ** -0.5, None, ALU.mult)
                elif k < 8:
                    mm = dve.tensor_copy(od["NK"][:, 2 * (k - 4):2 * (k - 4) + 2, :], banks(i, 2 * T))
                else:
                    mm = dve.tensor_copy(od["NV"][:, :, 256 * (k - 8):256 * (k - 7)],
                                         banks(i, 512).rearrange("p a (b n) -> p (a b) n", b=2))
                mm.then_inc(drained[i.par], 1)
            dve.wait_ge(ev_["c3_in"], 32)
            rp = od["RPB"][:, :, :, :].rearrange("p h d c -> p (h d) c")
            dve.tensor_tensor(rp, rp, bc(od["nmask"][:, :], 112), ALU.add).then_inc(ev_["qkv_ready"], 1)
            dve.wait_ge(ev_["qkv_ready"], 1)
            dve_attend(dve, ch, NA_UNITS, True, 16, 8, 1.0, od["NP"], 0)
            dve_out(dve, ch, 4, 1, "oout")

        def scalar_block2(act, ch):
            for m in range(6):
                if UPTO >= 4 + m:
                    act_ffn(act, m) if m in FFN_STAGES else (act_even if m == 1 else act_odd)(act, ch)

        def tensor_block2(pe):
            for m in range(6):
                if UPTO >= 4 + m:
                    pe_ffn(pe, m) if m in FFN_STAGES else (pe_even if m == 1 else pe_odd)(pe)

        def vector_block2(dve, ch):
            for m in range(6):
                if UPTO >= 4 + m:
                    dve_ffn(dve, ch, m) if m in FFN_STAGES else (dve_even if m == 1 else dve_odd)(dve, ch)

        @block.scalar
        def _(act):
            ch = Chain(act, act_step)
            act.dma_start(X[:, :, 0:T], a["x"]).then_inc(acts_in, 16)
            for dst, src in ((const, "const"), (vec, "vec"), (sml, "sml"), (c1, "c1")):
                act.dma_start(dst[:, :], a[src]).then_inc(consts_in, 16)
            act.dma_start(X[:, :, T:2 * T], a["ctx"]).then_inc(consts_in, 16)
            act.wait_ge(consts_in, 5 * 16)
            o = VEC["c"][0]
            act.activation(sc[:, :, :], vec[:, o:o + 2 * KT].rearrange("p (k b) -> p k b", b=2), ACT.Silu)\
                .then_inc(ev_["sc_ready"], 1)
            act.wait_ge(acts_in, 16)
            split_hi(act, Idx(0), SIZE[0])

            def softmax_exp(l, u):
                n = keys_of(u)
                act.wait_ge(ev_["soft_max"], l * UN + u + 1)
                for g in range(4):
                    m = act.activation(b1["SM"][:, u % 2, g, 0:n], b1["SM"][:, u % 2, g, 0:n], ACT.Exp,
                                       bias=tiny[:, 8 * (u % 2) + g:8 * (u % 2) + g + 1],
                                       accum_out=tiny[:, 16 + 8 * (u % 2) + g:17 + 8 * (u % 2) + g])
                m.then_inc(ev_["exp_done"], 1)

            def block1(l):
                if l:
                    act.wait_ge(ev_["x_ready"], l)
                act.activation(b1["MIX"][:, :, :], X[:, :, 0:T], ACT.Square).then_inc(ev_["sq_ready"], 1)
                act_root(act, tiny3[:, :])
                act.wait_ge(ev_["rms_out"], 2 * l + 1)
                act.activation(xh[:, :, 0:T], b1["MIX"][:, :, :], ACT.Copy).then_inc(ev_["xm_written"], 1)
                s0 = START[f"in{l}"]
                for k in range(18):
                    i = Idx(s0 + k)
                    act_ahead(act, i)
                    if k >= 14:
                        act.wait_ge(slab_used, i.base + 1)
                        act.activation(b1["SG"][:, 2 * (k - 14):2 * (k - 14) + 2, :], banks(i, T), ACT.Silu)\
                            .then_inc(drained[i.par], 1)
                    if k == 9:
                        act.wait_ge(ev_["blk_ready"], l + 1)
                        act.activation(b1["BH"][:, :, :], BLK, ACT.Copy).then_inc(ev_["cmp_raw"], 1)
                act.wait_ge(ev_["gates_e"], 2 * l + 1)
                act.activation(tiny[:, 64:88], tiny[:, 64:88], ACT.Exp, scale=-1.0).then_inc(ev_["gates_e"], 1)
                for blk in range(2):
                    n = P * (blk + 1)
                    act.wait_ge(ev_["idx_scores_out"], 2 * l + blk + 1)
                    act.wait_ge(ev_["pool_in"], l + 1)
                    if blk:
                        act.wait_ge(ev_["idx_used"], 2 * l + 1)
                    for hg in range(2):
                        m = act.activation(SMF.rearrange("p (h b t) -> p b h t", h=2, b=4)[:, :, hg, 0:n],
                                           PS[:, 0:4, hg * T:hg * T + n], ACT.Relu)
                    m.then_inc(ev_["idx_relu"], 1)
                softmax_exp(l, 0)
                for u in range(UN):
                    if u + 1 < UN:
                        softmax_exp(l, u + 1)
                    act.wait_ge(ev_["pt_ready"], l * UN + u + 1)
                    if u >= 2:
                        act.wait_ge(ev_["pv_done"], l * UN + u - 1)
                    kind, blk = UNITS[u]
                    if kind == "C":
                        m = act.activation(b1["PT"][0:NCMP, u % 2, 0, :], PS[0:NCMP, 4, :], ACT.Copy)
                    else:
                        m = act.activation(b1["PT"][:, u % 2, 0:blk + 1, :], PS[:, 4:5 + blk, :], ACT.Copy)
                    m.then_inc(ev_["pt_copied"], 1)
                act.wait_ge(ev_["o_taken"], 4 * l + 4)
                act.activation(xh[:, :, 0:T], b1["MIX"][:, :, :], ACT.Copy).then_inc(ev_["mixh_done"], 1)
                for k in range(4):
                    act_ahead(act, Idx(START[f"out{l}"] + k))

            for l in range(DEPTH):
                if UPTO >= 1 + l:
                    block1(l)
            if UPTO >= 3:
                act.wait_ge(ev_["x_ready"], DEPTH)
                act.activation(b1["MIX"][:, :, :], X[:, :, 0:T], ACT.Square).then_inc(ev_["sq_ready"], 1)
                act_root(act, tiny3[:, :])
            scalar_block2(act, ch)

        def ada_pairs(pe, first, n):
            layer = first // 18
            with pe.Fori(first, first + n) as it:
                for s in range(2):
                    pe.wait_ge(ada_full[s], it * 16 + 16)
                    for c in range(2):
                        for k in range(KT):
                            m = pe.matmul(PS[:, 7, bass.ds(it * 8 + (s * 4 + c * 2 - layer * 144), 2)],
                                          ada[:, s, (c * KT + k) * P:(c * KT + k + 1) * P], sc[:, k, :],
                                          start=k == 0, stop=k == KT - 1)
                    m.then_inc(ada_used, 1)

        @block.tensor
        def _(pe):
            pe.wait_ge(consts_in, 5 * 16)
            pe.wait_ge(ev_["sc_ready"], 1)

            def scores(l, u):
                kind, blk = UNITS[u]
                if u >= 2:
                    pe.wait_ge(ev_["soft_max"], l * UN + u - 1)
                q = {"A": 0}.get(kind, 3)
                for g in range(4):
                    h = (g % 2) * 2 + g // 2
                    r = slice((h % 2) * HD, (h % 2) * HD + HD)
                    lhs = b1["QK"][r, q + h // 2, blk * P:(blk + 1) * P]
                    if kind == "C":
                        rhs = b1["KC"][r, 0, 0:NCMP]
                    else:
                        rhs = b1["QK"][r, {"A": 2, "S": 5, "W": 6}[kind], 0:keys_of(u)]
                    o = (h // 2) * T
                    m = pe.matmul(PS[:, (u % 2) * 2 + h % 2, o:o + keys_of(u)], lhs, rhs, start=True, stop=True)
                m.then_inc(ev_["scores_out"], 1)

            def block1(l):
                pe.wait_ge(ev_["rms_in"], l + 1)
                pe.matmul(PS[:, 4, 0:T], ones, tiny2[:, :], start=True, stop=True).then_inc(ev_["rms_sum"], 1)
                s0 = START[f"in{l}"]
                pe.wait_ge(ev_["rms_out"], 2 * l + 2)
                for k in range(18):
                    i = Idx(s0 + k)
                    if k == 5 or k == 6:
                        token_major(pe, i, 2, 256 if k == 5 else 148, xh, xl, KT)
                    elif k == 7:
                        dense(pe, i, 1, KT, xh, xl, 0, T)
                    elif k in (10, 11):
                        slab_begin(pe, i)
                        pe.wait_ge(ev_["cmp_raw"], 2 * l + 2)
                        for half in range(2):
                            r = slice(half * HD, half * HD + HD)
                            j0 = (k - 10) * 16
                            m = product(pe, PS[:, 2 * i.par + half, 0:16], i,
                                        [(j * P, b1["BH"][r, :, j0 + j], b1["BL"][r, :, j0 + j]) for j in range(16)], rows=r)
                        m.then_inc(slab_used, 1)
                    else:
                        dense(pe, i, 2, KT, xh, xl, 0, T)
                for par in range(2):
                    last = s0 + 17 - (s0 + 17 - par) % 2
                    pe.wait_ge(drained[par], last // 2 + 1)
                perm = (cst("permI"), cst("permA"))
                pe.matmul(PS[:, 0, :], perm[0], b1["QI"][:, 0:2, :], start=True, stop=True)
                pe.matmul(PS[:, 1, 0:T], perm[0], b1["QI"][:, 2, :], start=True, stop=True).then_inc(ev_["perms_done"], 1)
                for j in range(3):
                    pe.matmul(PS[:, 2 + j, :], perm[1], b1["QK"][:, 2 * j:2 * j + 2, :], start=True, stop=True)
                pe.matmul(PS[:, 5, 0:T], perm[1], b1["QK"][:, 6, :], start=True, stop=True).then_inc(ev_["perms_done"], 1)
                pe.matmul(PS[:, 6, 0:NCMP], perm[1], b1["KC"][:, 0, 0:NCMP], start=True, stop=True)
                pe.transpose(PS[0:16, 6, P:2 * P], b1["KC"][:, 1, :], ident).then_inc(ev_["perms_done"], 1)
                if l == 0:
                    ada_pairs(pe, 0, 10)
                else:
                    ada_pairs(pe, 18, 10)
                for blk in range(2):
                    pe.wait_ge(ev_["roped"], 2 * l + 2)
                    if blk:
                        pe.wait_ge(ev_["idx_relu"], 2 * l + 1)
                    for h in range(8):
                        r = slice((h % 4) * 32, (h % 4) * 32 + 32)
                        m = pe.matmul(PS[:, h % 4, (h // 4) * T:(h // 4) * T + P * (blk + 1)],
                                      b1["QI"][r, h // 4, blk * P:(blk + 1) * P], b1["QI"][r, 2, 0:P * (blk + 1)],
                                      start=True, stop=True)
                    m.then_inc(ev_["idx_scores_out"], 1)
                pe.wait_ge(ev_["pool_in"], l + 1)
                for c in range(2):
                    o, _ = SML["poolw"]
                    m = pe.matmul(PS[:, 6, c * T:(c + 1) * T], sml[:, o + (2 * l + c) * P:o + (2 * l + c + 1) * P],
                                  b1["W2"][:, c, 16:16 + T], start=True, stop=True)
                m.then_inc(ev_["pool_out"], 1)
                pe.wait_ge(ev_["kc_ready"], l + 1)
                pe.wait_ge(ev_["idx_relu"], 2 * l + 2)
                scores(l, 0)
                scores(l, 1)
                ada_pairs(pe, 18 * l + 10, 8)
                for u in range(UN):
                    kind, blk = UNITS[u]
                    pe.wait_ge(ev_["p_ready"], l * UN + u + 1)
                    if u:
                        pe.wait_ge(ev_["pt_copied"], l * UN + u)
                    for kt in range(1 if kind == "C" else blk + 1):
                        n = NCMP if kind == "C" else P
                        for g in range(4):
                            h = (g % 2) * 2 + g // 2
                            m = pe.transpose(PS[0:n, 4 + kt, h * P:(h + 1) * P],
                                             b1["SM"][:, u % 2, (h % 2) * 2 + h // 2, kt * P:kt * P + n], ident)
                    m.then_inc(ev_["pt_ready"], 1)
                    if u + 2 < UN:
                        scores(l, u + 2)
                    pe.wait_ge(ev_["pt_copied"], l * UN + u + 1)
                    if kind in "AS":
                        n_taken = {0: 0, 3: 1, 4: 2, 7: 3}[u]
                        pe.wait_ge(ev_["o_taken"], 4 * l + n_taken) if 4 * l + n_taken else None
                        if u == 0:
                            pe.wait_ge(ev_["pool_out"], 2 * l + 2)
                    if kind == "C":
                        m = pe.matmul(PS[:, 6, :], b1["VC"][0:NCMP, :], b1["PT"][0:NCMP, u % 2, 0, :], start=False, stop=True)
                    else:
                        for kt in range(blk + 1):
                            v = {"A": b1["VT"][:, kt, 0:P], "S": b1["VT"][:, kt, P:2 * P], "W": b1["VW"][:, kt, 0:P]}[kind]
                            m = pe.matmul(PS[:, 6, :], v, b1["PT"][:, u % 2, kt, :], start=kt == 0 and kind in "AS",
                                          stop=kt == blk and kind == "A")
                    m.then_inc(ev_["pv_done"], 1)
                pe.wait_ge(ev_["mixl_done"], l + 1)
                for k in range(4):
                    dense(pe, Idx(START[f"out{l}"] + k), 2, KT, xh, xl, 0, T)

            for l in range(DEPTH):
                if UPTO >= 1 + l:
                    block1(l)
            if UPTO >= 3:
                pe.wait_ge(ev_["rms_in"], 3)
                pe.matmul(PS[:, 4, 0:T], ones, tiny2[:, :], start=True, stop=True).then_inc(ev_["rms_sum"], 1)
            tensor_block2(pe)

        @block.vector
        def _(dve):
            ch = Chain(dve, dve_step)
            dve.memset(b1["DU"][:, :, 0:16], 0.0)
            ch.after(dve.memset(b1["UP"][:, :, 0:2], 0.0))
            dve.wait_ge(consts_in, 5 * 16)
            dve.wait_ge(acts_in, 16)
            split_lo(dve, Idx(0), SIZE[0])
            M, W2, DU = b1["MIX"], b1["W2"], b1["DU"]

            def rms(l):
                dve.wait_ge(ev_["sq_ready"], l + 1)
                dve.tensor_reduce(tiny2[:, :], M[:, :, :].rearrange("p k t -> p t k"), AX, ALU.add)\
                    .then_inc(ev_["rms_in"], 1)
                dve.wait_ge(ev_["rms_sum"], l + 1)
                rstd(ch, dve, tiny3[:, :], PS[:, 4, 0:T], D)

            def soft1(l, u):
                kind, blk = UNITS[u]
                n = keys_of(u)
                dve.wait_ge(ev_["scores_out"], l * UN + u + 1)
                if kind == "A":
                    bias = b1["CX"][:, 0, 0:P] if blk == 0 else b1["CX"][:, 1, :]
                elif kind == "C":
                    bias = ccol("cmpm")[:, 16 * blk:16 * blk + NCMP]
                else:
                    bias = ccol("tri")[:, P:2 * P] if blk == 0 else ccol("tri")
                if u >= 2:
                    dve.wait_ge(ev_["pt_ready"], l * UN + u - 1)
                s = b1["SM"][:, u % 2, :, 0:n]
                src = PS[:, (u % 2) * 2:(u % 2) * 2 + 2, :].rearrange("p a (b t) -> p (a b) t", b=2)[:, :, 0:n]
                ch.after(dve.scalar_tensor_tensor(out=s, in0=src, scalar=HD ** -0.5, in1=bc(bias, 4), op0=ALU.mult, op1=ALU.add))
                nm = tiny[:, 8 * (u % 2):8 * (u % 2) + 4]
                ch.after(dve.tensor_reduce(nm, s, AX, ALU.max, negate=True))
                dve.tensor_scalar(nm, nm, FLOOR, None, ALU.min).then_inc(ev_["soft_max"], 1)

            def soft2(l, u):
                kind, blk = UNITS[u]
                n = keys_of(u)
                dve.wait_ge(ev_["exp_done"], l * UN + u + 1)
                r = tiny[:, 32 + 8 * (u % 2):36 + 8 * (u % 2)]
                ch.after(dve.tensor_scalar(r, tiny[:, 16 + 8 * (u % 2):20 + 8 * (u % 2)], 1e-30, None, ALU.max))
                ch.after(dve.reciprocal(r, r))
                if kind != "A":
                    o = 96 + 12 * blk + 4 * "CSW".index(kind)
                    ch.after(dve.tensor_tensor(r, r, tiny[:, o:o + 4], ALU.mult))
                s = b1["SM"][:, u % 2, :, 0:n]
                dve.tensor_tensor(s, s, bl(r, n), ALU.mult).then_inc(ev_["p_ready"], 1)

            def take_o(l, u):
                kind, blk = UNITS[u]
                dve.wait_ge(ev_["pv_done"], l * UN + u + 1)
                c0 = 0 if kind == "A" else 2
                for par in range(2):
                    r = slice(par * HD, par * HD + HD)
                    o = PS[r, 6, :].rearrange("p (c h t) -> p c h t", c=2, h=2)[:, :, par, :]
                    m = dve.tensor_tensor(M[r, c0:c0 + 2, blk * P:(blk + 1) * P], o,
                                          b1["SG"][r, c0:c0 + 2, blk * P:(blk + 1) * P], ALU.mult)
                m.then_inc(ev_["o_taken"], 1)

            def top_k(l, blk):
                n = P * (blk + 1)
                dve.wait_ge(ev_["idx_relu"], 2 * l + blk + 1)
                s = tiny2[:, 0:n]
                acc = ccol("tri")[:, P:2 * P] if blk == 0 else ccol("tri")
                for h in range(8):
                    ins = dve.scalar_tensor_tensor(out=s, in0=SMF[:, h * T:h * T + n],
                                                   scalar=b1["VW"][:, blk, P + h:P + h + 1], in1=acc, op0=ALU.mult, op1=ALU.add)
                    acc = s
                    if h == 7:
                        ins.then_inc(ev_["idx_used"], 1)
                        dve.wait_ge(ev_["idx_used"], 2 * l + blk + 1)
                    else:
                        ch.after(ins)
                for r in range(TOPK // 8):
                    ch.after(dve.max(tiny[:, 48:56], s))
                    ch.after(dve.match_replace(out=s, in_to_replace=tiny[:, 48:56], in_values=s, imm_value=TAKEN))
                ab = b1["CX"][:, 0, 0:P] if blk == 0 else b1["CX"][:, 1, :]
                tri = ccol("tri")[:, P:2 * P] if blk == 0 else ccol("tri")
                ch.after(dve.tensor_scalar(s, s, TAKEN / 2, -NEG, ALU.is_le, ALU.mult))
                ch.after(dve.scalar_tensor_tensor(out=ab, in0=s, scalar=NEG, in1=tri, op0=ALU.add, op1=ALU.add))

            def block1(l):
                if l:
                    dve.wait_ge(ev_["x_ready"], l)
                rms(l)
                for k in range(KT):
                    m = dve.scalar_tensor_tensor(out=M[:, k, :], in0=X[:, k, 0:T], scalar=vcol("norm", l * KT + k),
                                                 in1=tiny3[:, :], op0=ALU.mult, op1=ALU.mult)
                m.then_inc(ev_["rms_out"], 1)
                dve.wait_ge(ev_["xm_written"], l + 1)
                dve.tensor_tensor(xl[:, :, 0:T], M[:, :, :], xh[:, :, 0:T].bitcast(F32), ALU.subtract)\
                    .then_inc(ev_["rms_out"], 1)
                s0 = START[f"in{l}"]
                QI, QK = b1["QI"], b1["QK"]
                for k in range(18):
                    i = Idx(s0 + k)
                    dve_ahead(dve, i)
                    if k >= 14:
                        continue
                    dve.wait_ge(slab_used, i.base + 1)
                    if k == 0:
                        m = dve.tensor_copy(QI[:, 0:2, :], banks(i, T))
                    elif k == 1:
                        dve.tensor_copy(QI[:, 2, :], PS[:, 2 * i.par, 0:T])
                        m = dve.tensor_copy(QK[:, 2, :], PS[:, 2 * i.par + 1, 0:T])
                    elif k in (2, 3, 4):
                        o = {2: 0, 3: 3, 4: 5}[k]
                        m = dve.tensor_copy(QK[:, o:o + 2, :], banks(i, T))
                    elif k == 5:
                        m = dve.tensor_copy(b1["VT"][:, :, :], PS[:, 2 * i.par, :].rearrange("p (a n) -> p a n", a=2))
                    elif k == 6:
                        m = dve.tensor_copy(b1["VW"][:, :, :], PS[:, 2 * i.par, :].rearrange("p (a n) -> p a n", a=2)[:, :, 0:148])
                    elif k == 7:
                        m = dve.tensor_copy(KCV, PS[:, 2 * i.par, 0:T])
                    elif k in (8, 9):
                        m = dve.tensor_copy(b1["CC" if k == 8 else "CX"][:, :, :], banks(i, T))
                    elif k in (10, 11):
                        src = banks(i, 16)
                        if k == 10:
                            m = dve.tensor_copy(b1["KC"][:, :, :], src)
                        else:
                            m = dve.tensor_tensor(b1["KC"][:, :, :], b1["KC"][:, :, :], src, ALU.add)
                    elif k == 12:
                        m = dve.tensor_copy(b1["CB"][:, :, :], banks(i, T))
                    elif k == 13:
                        m = dve.tensor_copy(DU[:, :, 16:16 + T], banks(i, T))
                    m.then_inc(drained[i.par], 1)
                    if k == 6:
                        dve.wait_ge(drained[i.par], i.base // 2 + 1)
                        dve.tensor_copy(tiny[:, 64:88].rearrange("p (b g) -> p b g", b=2), b1["VW"][:, :, P + 8:P + 20])\
                            .then_inc(ev_["gates_e"], 1)
                    if k == 7:
                        dve.wait_ge(drained[i.par], i.base // 2 + 1)
                        o = VEC["pe"][0] + 32 * l
                        for half in range(2):
                            kv = KCV[:, 16 * half:16 * half + 240].rearrange("p (n j) -> p n j", j=16)
                            m = dve.tensor_tensor(BLK[:, 0:NCMP, 16 * half:16 * half + 16], kv,
                                                  bc(vec[:, o + 16 * half:o + 16 * half + 16], NCMP), ALU.add)
                        dve.memset(BLK[:, NCMP:16, :], 0.0).then_inc(ev_["blk_ready"], 1)
                    if k == 9:
                        dve.wait_ge(ev_["cmp_raw"], 2 * l + 1)
                        dve.tensor_tensor(b1["BL"][:, :, :], BLK, b1["BH"][:, :, :].bitcast(F32), ALU.subtract)\
                            .then_inc(ev_["cmp_raw"], 1)
                    if k == 10:
                        dve.wait_ge(drained[i.par], i.base // 2 + 1)
                for j, (t, nch, tab) in enumerate(((QI, 3, "ropeI"), (QK, 7, "ropeA"))):
                    dve.wait_ge(ev_["perms_done"], 3 * l + j + 1)
                    cs = ccol(tab)
                    src = PS[:, 0:2, :] if j == 0 else PS[:, 2:6, :]
                    src = src.rearrange("p a b -> p (a b)")[:, 0:nch * T].rearrange("p (c t) -> p c t", t=T)
                    rt = SMF[:, 0:nch * T].rearrange("p (c t) -> p c t", t=T)
                    dve.tensor_tensor(rt, src, bc(cs[:, T:2 * T], nch), ALU.mult)
                    ch.after(dve.tensor_tensor(t[:, :, :], t[:, :, :], bc(cs[:, 0:T], nch), ALU.mult))
                    dve.tensor_tensor(t[:, :, :], t[:, :, :], rt, ALU.add).then_inc(ev_["roped"], 1)
                    dve.wait_ge(ev_["roped"], 2 * l + j + 1)
                dve.wait_ge(ev_["perms_done"], 3 * l + 3)
                cs = ccol("ropeC")
                dve.tensor_copy(b1["VC"][:, :], PS[0:16, 6, P:2 * P])
                ch.after(dve.tensor_tensor(tiny[:, 128:128 + NCMP], PS[:, 6, 0:NCMP], cs[:, 16:16 + NCMP], ALU.mult))
                ch.after(dve.tensor_tensor(b1["KC"][:, 0, 0:NCMP], b1["KC"][:, 0, 0:NCMP], cs[:, 0:NCMP], ALU.mult))
                ch.after(dve.tensor_tensor(b1["KC"][:, 0, 0:NCMP], b1["KC"][:, 0, 0:NCMP], tiny[:, 128:128 + NCMP], ALU.add))
                dve.wait_ge(ev_["gates_e"], 2 * l + 2)
                ch.after(dve.tensor_scalar(tiny[:, 96:120], tiny[:, 64:88], 1.0, None, ALU.add))
                dve.reciprocal(tiny[:, 96:120], tiny[:, 96:120]).then_inc(ev_["kc_ready"], 1)
                ch.after(dve.tensor_tensor(W2[:, :, 1:], DU[:, :, 1:], DU[:, :, 0:15 + T], ALU.add))
                pm, inv = SMF[:, 0:2 * T].rearrange("p (c t) -> p c t", c=2), ccol("invc").rearrange("p (c t) -> p c t", c=2)
                lo, hi = slice(0, HD), slice(HD, P)
                TW = b1["QK"]
                ch.after(dve.tensor_tensor(pm[lo, 0, :], W2[lo, 0, 16:], inv[lo, 0, :], ALU.mult))
                a4 = SMF[:, 2 * T:2 * T + 2 * (T + 16)].rearrange("p (c t) -> p c t", c=2)
                a8 = SMF[:, 4 * T + 32:4 * T + 32 + T + 16]
                ch.after(dve.tensor_tensor(a4[:, :, 3:], W2[:, :, 3:], W2[:, :, 1:14 + T], ALU.add))
                dve.tensor_tensor(pm[hi, 0, :], a4[hi, 0, 16:], inv[hi, 0, :], ALU.mult)
                ch.after(dve.tensor_tensor(a8[:, 7:], a4[:, 1, 7:], a4[:, 1, 3:12 + T], ALU.add))
                dve.tensor_tensor(pm[lo, 1, :], a8[lo, 16:], inv[lo, 1, :], ALU.mult)
                ch.after(dve.tensor_tensor(W2[:, 1, 16:], a8[:, 16:], a8[:, 8:8 + T], ALU.add))
                ch.after(dve.tensor_tensor(pm[hi, 1, :], W2[hi, 1, 16:], inv[hi, 1, :], ALU.mult))
                dve.tensor_tensor(W2[:, :, 16:], pm, DU[:, :, 16:], ALU.subtract).then_inc(ev_["pool_in"], 1)
                dve.wait_ge(ev_["pool_in"], l + 1)
                UP = b1["UP"]
                ch.after(dve.tensor_tensor(UP[:, :, 2:], b1["CC"][:, :, :], b1["CX"][:, :, :], ALU.mult))
                for c in range(2):
                    y = M[:, 4 + c, :]
                    ch.after(dve.tensor_scalar(y, UP[:, c, 0:T], vcol("conv", l * 6 + c), None, ALU.mult))
                    for j in (1, 2):
                        ch.after(dve.scalar_tensor_tensor(out=y, in0=UP[:, c, j:j + T], scalar=vcol("conv", l * 6 + 2 * j + c),
                                                          in1=y, op0=ALU.mult, op1=ALU.add))
                ch.after(dve.tensor_tensor(M[:, 4:6, :], M[:, 4:6, :], b1["CB"][:, :, :], ALU.mult))
                ch.after(dve.tensor_tensor(M[:, 4:6, :], M[:, 4:6, :], b1["SG"][:, 4:6, :], ALU.mult))
                top_k(l, 0)
                top_k(l, 1)
                dve.wait_ge(ev_["pool_out"], 2 * l + 1)
                for c in range(2):
                    m = dve.scalar_tensor_tensor(out=M[:, 6 + c, :], in0=PS[:, 6, c * T:(c + 1) * T],
                                                 scalar=vcol("pscale", 2 * l + c), in1=b1["SG"][:, 6 + c, :],
                                                 op0=ALU.mult, op1=ALU.mult)
                m.then_inc(ev_["pool_out"], 1)
                soft1(l, 0)
                soft1(l, 1)
                for u in range(UN):
                    soft2(l, u)
                    if u + 2 < UN:
                        soft1(l, u + 2)
                    if u in (3, 4, 7):
                        take_o(l, u - 1)
                take_o(l, UN - 1)
                dve.wait_ge(ev_["mixh_done"], l + 1)
                dve.tensor_tensor(xl[:, :, 0:T], M[:, :, :], xh[:, :, 0:T].bitcast(F32), ALU.subtract)\
                    .then_inc(ev_["mixl_done"], 1)
                for k in range(4):
                    i = Idx(START[f"out{l}"] + k)
                    dve_ahead(dve, i)
                    dve.wait_ge(slab_used, i.base + 1)
                    m = dve.tensor_tensor(X[:, 2 * k:2 * k + 2, 0:T], X[:, 2 * k:2 * k + 2, 0:T], banks(i, T), ALU.add)
                    m.then_inc(drained[i.par], 1)
                for par in range(2):
                    last = i.base - (i.base - par) % 2
                    dve.wait_ge(drained[par], last // 2 + 1)
                dve.wait_ge(ada_used, 36 * (l + 1))
                o = VEC["adab"][0] + 72 * l
                mm = mod[:, l, :, :, :].rearrange("p j k b -> p (j k) b")
                ch.after(dve.tensor_tensor(mm, PS[:, 7, 0:144].rearrange("p (c b) -> p c b", b=2), bl(vec[:, o:o + 72], 2), ALU.add))
                for j in (1, 4, 7):
                    dve.tensor_scalar(mod[:, l, j, :, :], mod[:, l, j, :, :], 1.0, None, ALU.add)
                for j in (2, 8):
                    m = dve.tensor_scalar(mod[:, l, j, :, :], mod[:, l, j, :, :], 0.5, None, ALU.mult)
                m.then_inc(ev_["x_ready"], 1)

            for l in range(DEPTH):
                if UPTO >= 1 + l:
                    block1(l)
            if UPTO >= 3:
                dve.wait_ge(ev_["x_ready"], 2)
                rms(2)
                for k in range(KT):
                    m = dve.scalar_tensor_tensor(out=X[:, k, 0:T], in0=X[:, k, 0:T], scalar=vcol("fnorm", k),
                                                 in1=tiny3[:, :], op0=ALU.mult, op1=ALU.mult)
                m.then_inc(ev_["x_ready"], 1)
            vector_block2(dve, ch)


IN_SPLITS = (("a_q", 256), ("a_k", 64), ("a_v", 64), ("a_qi", 256), ("a_ki", 32), ("a_wi", 8), ("a_gate", 256),
             ("b_q", 256), ("b_kc", 64), ("b_vc", 64), ("b_ks", 64), ("b_vs", 64), ("b_kw", 64), ("b_vw", 64),
             ("b_g", 12), ("b_gate", 256), ("c_b", 256), ("c_c", 256), ("c_x", 256), ("c_gate", 256),
             ("d_u", 256), ("d_gate", 256))
EVEN_SPLITS = (("q", 256), ("k", 256), ("v", 512), ("r", 512), ("lf", 16), ("lb", 16), ("cq", 384), ("ckv", 128), ("kr", 64))


def spans(splits):
    at, o = {}, 0
    for name, n in splits:
        at[name] = np.arange(o, o + n)
        o += n
    return at


def rows_by_partition(w, cols):
    w = np.concatenate([w, np.zeros((w.shape[0], 1), w.dtype)], 1)
    return w[:, cols].reshape(-1, P, len(cols)).transpose(1, 0, 2)


def slab(w, *chunks):
    return np.concatenate([rows_by_partition(w, c).reshape(P, -1) for c in chunks], 1)


def by_feature(v):
    return v.reshape(-1, P).T


def rope_tables(pos_angles, head, rot, interleaved=False):
    n = pos_angles.shape[0]
    c, s, perm = np.ones((P, n), np.float32), np.zeros((P, n), np.float32), np.zeros((P, P), np.float32)
    cos, sin = np.cos(pos_angles).astype(np.float32), np.sin(pos_angles).astype(np.float32)
    for p in range(P):
        d = p % head
        if d >= rot:
            continue
        if interleaved:
            f, first, partner = d // 2, d % 2 == 0, p ^ 1
        else:
            half = rot // 2
            f, first, partner = d % half, d < half, p + half if d < half else p - half
        c[p], s[p], perm[partner, p] = cos[:, f], (-sin if first else sin)[:, f], 1.0
    return c, s, perm


def constants():
    t = np.arange(T)
    inv = lambda base, n: (np.float32(base) ** (-np.arange(n, dtype=np.float32) / n)).astype(np.float32)
    ang = lambda pos, f: (pos.astype(np.float32)[:, None] * f[None, :]).astype(np.float32)
    ca, sa, pa = rope_tables(ang(t, inv(500000.0, 8)), 64, 16)
    ci, si, pi = rope_tables(ang(t, inv(500000.0, 4)), 32, 8)
    cc, sc_, _ = rope_tables(ang(np.arange(16) * 16 + 31, inv(500000.0, 8)), 64, 16)
    f = inv(10000.0, 16)
    cm, sm, pm = rope_tables(np.concatenate([ang(t // 64, f), ang(t % 64, f)], 1), 64, 64, True)
    const = np.concatenate([np.eye(P), np.ones((P, P)), pa, pi, pm], 1)
    q = np.arange(P)
    tri = np.concatenate([np.zeros((P, P)), np.where(q[None, :] > q[:, None], NEG, 0.0)], 1)
    cmpm = np.concatenate([np.where((np.arange(16) * 16 + 31)[None, :] <= (q + b * P)[:, None], 0.0, NEG) for b in range(2)], 1)
    win = np.array([[2, 8], [4, 16]])
    invc = np.stack([[1.0 / np.minimum(t + 1, win[p // HD][c]) for c in range(2)] for p in range(P)]).reshape(P, -1)
    c1 = np.concatenate([ca, sa, ci, si, cc, sc_, tri, cmpm, invc], 1)
    j, i = q[:, None] % GC, np.arange(GC)[None, :]
    reset = np.broadcast_to((np.arange(2 * T) % GC != 0), (P, 2 * T))
    c2 = np.concatenate([cm, sm, j <= i, j > i, reset], 1)
    col, key = q[:, None] % 64, np.arange(64)[None, :]
    start = np.clip(col - 8, 0, 48)
    nmask = np.where((key >= start) & (key < start + 16), 0.0, NEG)
    out = {"const": const, "c1": c1, "c2": c2, "nmask": nmask}
    assert const.shape[1] == CONST_N and c1.shape[1] == C1_N and c2.shape[1] == C2_N
    return {n: np.ascontiguousarray(v, dtype=np.float32) for n, v in out.items()}


def pack(x, norm_w, w_in, w_out, conv_w, pe_cmp, w_cmp_k, w_cmp_v, pool_w, pool_scale, final_norm_w,
         c_2, ctx_2, c_ctx_2, ada_w_2, ada_b_2, ffn1_w_in_2, ffn1_w_out_2, ffn2_w_in_2, ffn2_w_out_2,
         even_w_in_2, gla_wg2_f_2, gla_bg_f_2, gla_wg2_b_2, gla_bg_b_2, gla_norm_g_2, mla_q_norm_g_2,
         mla_kv_norm_g_2, mla_w_uq_2, mla_w_ukv_2, even_w_out_2, na_w_in_2, na_rpb_2, na_w_out_2):
    out = {}
    tokens = lambda v: np.ascontiguousarray(v[0].T.reshape(KT, P, T).transpose(1, 0, 2))
    out["x"], out["ctx"] = tokens(x), tokens(ctx_2)
    chunk = lambda idx, n=0: idx[n * P:(n + 1) * P]
    seq = np.arange(D)
    whole = lambda w: np.stack([slab(w, chunk(seq, 2 * n), chunk(seq, 2 * n + 1)) for n in range(4)])
    s = spans(IN_SPLITS)
    dup = lambda n: np.concatenate([s[n], s[n]])
    for l in range(DEPTH):
        w = w_in[l]
        pair = lambda n: slab(w, chunk(s[n]), chunk(s[n], 1))
        va = rows_by_partition(w, np.concatenate([dup("a_v"), dup("b_vs")])).reshape(P, -1)
        out[f"in{l}"] = np.stack([pair("a_qi"), slab(w, np.tile(s["a_ki"], 4), dup("a_k")), pair("a_q"), pair("b_q"),
                                  slab(w, dup("b_ks"), dup("b_kw")), va])
        g = s["b_g"].reshape(2, 2, 3).transpose(2, 1, 0).reshape(-1)
        out[f"vb{l}"] = rows_by_partition(w, np.concatenate([dup("b_vw"), s["a_wi"], g])).reshape(1, P, -1)
        out[f"kcvc{l}"] = slab(w, np.concatenate([s["b_kc"], s["b_vc"]]))[None]
        cw = np.concatenate([np.tile(v[l].reshape(32, HD, HD), (1, 1, 2)).transpose(1, 0, 2) for v in (w_cmp_k, w_cmp_v)], 0)
        cmp_slabs = cw.reshape(P, 2, -1).transpose(1, 0, 2)
        out[f"tail{l}"] = np.concatenate([np.stack([pair("c_c"), pair("c_x")]), cmp_slabs,
                                          np.stack([pair(n) for n in ("c_b", "d_u", "a_gate", "b_gate", "c_gate", "d_gate")])])
        out[f"out{l}"] = whole(w_out[l])
    cols = np.arange(DFF)
    for l in range(DEPTH):
        for f, wi, wo in ((1, ffn1_w_in_2[l], ffn1_w_out_2[l]), (2, ffn2_w_in_2[l], ffn2_w_out_2[l])):
            for half in range(2):
                ms = range(half * FH, half * FH + FH)
                out[f"ffi{f}{l}{half}"] = np.stack([slab(wi, chunk(cols, m), chunk(cols, m) + DFF) for m in ms])
                rows = wo[half * FH * P:(half + 1) * FH * P]
                out[f"ffo{f}{l}{half}"] = np.stack([slab(rows, chunk(seq, n)) for n in range(KT)])
    out["ada"] = np.concatenate([np.stack([slab(ada_w_2[l], np.arange(n * 2 * P, n * 2 * P + P), np.arange(n * 2 * P + P, (n + 1) * 2 * P))
                                           for n in range(36)]) for l in range(DEPTH)])
    e, w = spans(EVEN_SPLITS), even_w_in_2[0]
    pair = lambda n, a=0: slab(w, chunk(e[n], a), chunk(e[n], a + 1))
    gap = -np.ones(16, int)
    lr = np.concatenate([e["lf"], gap, e["lb"], gap, np.tile(gap, 4)])
    tok = lambda w_, c: rows_by_partition(w_, c).reshape(P, -1)
    out["even"] = np.stack([pair("q"), pair("k"), slab(w, lr, np.tile(e["kr"], 2)), tok(w, e["v"][0:256]), tok(w, e["v"][256:512]),
                            pair("cq"), slab(w, chunk(e["cq"], 2), e["ckv"]), pair("r"), pair("r", 2)])
    uq = np.arange(768).reshape(4, 192)
    nope, rope_ = uq[:, 0:P], uq[:, P:192].reshape(2, P)
    out["uq"] = np.stack([slab(mla_w_uq_2[0], a_, b_) for a_, b_ in ((nope[0], nope[1]), (nope[2], nope[3]), (rope_[0], rope_[1]))])
    kv = np.arange(1024).reshape(4, 256)
    out["ukv"] = np.stack([slab(mla_w_ukv_2[0], kv[0, 0:P], kv[1, 0:P]), slab(mla_w_ukv_2[0], kv[2, 0:P], kv[3, 0:P]),
                           tok(mla_w_ukv_2[0], kv[0:2, P:].reshape(-1)), tok(mla_w_ukv_2[0], kv[2:4, P:].reshape(-1))])
    out["eout"], out["oout"] = whole(even_w_out_2[0]), whole(na_w_out_2[0])
    w = na_w_in_2[0]
    out["odd"] = np.stack([slab(w, seq[2 * n * P:(2 * n + 1) * P] + o, seq[(2 * n + 1) * P:(2 * n + 2) * P] + o)
                           for o in (0, D) for n in range(4)] + [tok(w, seq[256 * n:256 * n + 256] + 2 * D) for n in range(4)])
    shift = np.arange(64)[None, :] - (np.arange(P) % 64)[:, None] + 15
    rp = np.concatenate([na_rpb_2[0], np.zeros((16, 15, 1), na_rpb_2.dtype)], 2)[:, 4:11]
    out["rpb"] = rp[:, :, np.where((shift >= 0) & (shift <= 30), shift, 31)].transpose(2, 0, 1, 3)
    cols_of = [by_feature(norm_w), by_feature(final_norm_w), by_feature(conv_w), by_feature(pool_scale),
               np.concatenate([np.concatenate([pe_cmp[l].T, pe_cmp[l].T], 0) for l in range(DEPTH)], 1),
               by_feature(ada_b_2), np.stack([by_feature(c_2[0]), by_feature(c_ctx_2)], 2).reshape(P, -1),
               by_feature(gla_bg_f_2), by_feature(gla_bg_b_2), by_feature(gla_norm_g_2), by_feature(mla_q_norm_g_2),
               by_feature(mla_kv_norm_g_2)]
    out["vec"] = np.concatenate(cols_of, 1)
    pw = np.zeros((P, DEPTH, 2, P), pool_w.dtype)
    for l in range(DEPTH):
        for g in range(4):
            r = slice((g % 2) * HD, (g % 2) * HD + HD)
            pw[r, l, g // 2, r] = pool_w[l, g]
    wg = np.zeros((P, 2 * P), pool_w.dtype)
    wg[0:16], wg[32:48] = gla_wg2_f_2[0], gla_wg2_b_2[0]
    out["sml"] = np.concatenate([pw.reshape(P, -1), wg], 1)
    out.update(constants())
    return {n: np.ascontiguousarray(v) for n, v in out.items()}


def kernel(**inputs):
    import concourse.bacc as bacc
    from concourse.bass_utils import run_bass_kernel_spmd

    arrays = pack(**{n: np.asarray(v) for n, v in inputs.items()})
    nc = bacc.Bacc("TRN2", target_bir_lowering=False, num_devices=1)
    a = {n: nc.dram_tensor(n + "_dram", v.shape, mybir.dt.from_np(v.dtype), kind="ExternalInput").ap() for n, v in arrays.items()}
    a["out"] = nc.dram_tensor("out_dram", (P, KT, T), F32, kind="ExternalOutput").ap()
    build(nc, a)
    r = run_bass_kernel_spmd(nc, [{n + "_dram": v for n, v in arrays.items()}], core_ids=[0])
    y = r.results[0]["out_dram"]
    return np.ascontiguousarray(y.transpose(1, 0, 2).reshape(D, T).T[None])
```

```python
from contextlib import ExitStack

import numpy as np
import concourse.bass as bass
from concourse import mybir

F32 = mybir.dt.float32
F32R = mybir.dt.float32r
ALU = mybir.AluOpType
ACT = mybir.ActivationFunctionType
AX = mybir.AxisListType.X

P = 128
D = 1024
KT = D // P
T = 256
DEPTH = 2
EPS = 1e-6
HD = 64
DFF = 2816
FH = DFF // P // 2
ALPHA = (2 * DEPTH) ** 0.25
TOPK = T // 4
NCMP = (T - 32) // 16 + 1
GC = 64
MLA_SCALE = 192.0 ** -0.5
NEG = -1e30
FLOOR = 1e29
TAKEN = -3e38

SLAB = 2 * KT * P
RING = 4
IN_N = 16
IDX_AT = [9, 11]
ADA_N = 36

def layer_plan():
    plan, a = [], 0
    for k in range(IN_N):
        plan.append(("in", k))
        if k == 12:
            plan += [("cmp", 0), ("cmp", 1)]
        if k:
            plan.append(("ada", a))
            a += 1
    after = {}
    for u in range(-1, 8):
        n = 3 if u < 2 else 2
        after[u] = [(len(plan) + j, a + j) for j in range(n)]
        plan += [("ada", a + j) for j in range(n)]
        a += n
    assert a == ADA_N
    return plan + [("out", k) for k in range(4)], after


PLAN, UNIT_ADA = layer_plan()


def stage_table():
    runs = []
    for l in range(DEPTH):
        runs.append((f"layer{l}", len(PLAN), SLAB))
    for l in range(DEPTH):
        for f in (1, 2):
            if f == 2 and l == 0:
                runs += [("even", 9, 2 * KT * P), ("uq", 3, 6 * P), ("ukv", 4, 2 * P), ("eout", 4, 2 * KT * P)]
            if f == 2 and l == 1:
                runs += [("odd", 12, 2 * KT * P), ("oout", 4, 2 * KT * P)]
            for half in range(2):
                runs += [(f"ffi{f}{l}{half}", FH, 2 * KT * P), (f"ffo{f}{l}{half}", KT, FH * P)]
    return runs


RUNS = stage_table()
START, SIZE, KIND = {}, [], []
for _name, _n, _f in RUNS:
    START[_name] = len(SIZE)
    SIZE += [{"vb": KT * 148}.get(_name, _f)] * _n
    KIND += [kind for kind, _ in PLAN] if _name.startswith("layer") else ["dense"] * _n
for _l in range(DEPTH):
    SIZE[START[f"layer{_l}"] + PLAN.index(("in", 6))] = KT * 148
    SIZE[START[f"layer{_l}"] + PLAN.index(("in", 7))] = KT * P
NSLABS = len(SIZE)


def splitter(b):
    if KIND[b] == "cmp":
        return None
    layer_pos = [b - START[f"layer{l}"] for l in range(DEPTH)]
    if KIND[b] == "ada":
        a = PLAN[layer_pos[1] if layer_pos[1] >= 0 else layer_pos[0]][1]
        return "dve" if a % 3 == 2 else "pool"
    return "dve"


def before(test):
    return np.concatenate([[0], np.cumsum([test(b) for b in range(NSLABS)])]).tolist()


FIRST_LEN = START["ffi100"]
BANKED = before(lambda b: KIND[b] not in ("ada", "cmp"))
HI = before(lambda b: KIND[b] != "cmp")
LO = {e: before(lambda b: splitter(b) == e) for e in ("dve", "pool")}

def columns(parts):
    at, o = {}, 0
    for name, n in parts:
        at[name] = (o, n)
        o += n
    return at, o


CONST, CONST_N = columns([("ident", P), ("ones", P), ("permA", P), ("permI", P), ("permM", P), ("pairsum", 4)])
C1, C1_N = columns([("ropeA", 2 * T), ("ropeI", 2 * T), ("ropeC", 32), ("tri", T), ("cmpm", 32), ("invc", 2 * T)])
C2, C2_N = columns([("ropeM", 2 * T), ("gmask", 2 * GC), ("reset", 2 * T)])
VEC, VEC_N = columns([("norm", DEPTH * KT), ("fnorm", KT), ("conv", DEPTH * 6), ("pscale", DEPTH * 2), ("pe", DEPTH * 32),
                      ("adab", DEPTH * 72), ("c", 2 * KT), ("bg", 4), ("gnorm", 1), ("qnorm", 3), ("kvnorm", 1)])
SML, SML_N = columns([("poolw", DEPTH * 2 * P), ("wg2", 2 * P)])

ARENA = 0


class Idx:

    def __init__(self, base, reg=None):
        self.base, self.reg = base, reg

    def __add__(self, n):
        return Idx(self.base + n, self.reg)

    @property
    def slot(self):
        return self.base % RING

    @property
    def d(self):
        return BANKED[self.base]

    @property
    def par(self):
        return self.d % 2

    def count(self, per_group, at_zero):
        return at_zero if self.reg is None else self.reg * per_group + at_zero


UPTO = 9
LAST_X = 9


def build(nc, a):
    UPTO_SLAB = {1: START["layer1"], 2: START["ffi100"], 3: START["ffi100"], 4: START["even"], 5: START["ffi200"], 6: START["ffi110"],
                 7: START["odd"], 8: START["ffi210"], 9: NSLABS}[UPTO]
    ctx = ExitStack()
    sems = {}

    def sig(name):
        if name not in sems:
            sems[name] = ctx.enter_context(nc.semaphore(name))
        return sems[name]

    with ctx:
        base = [(nc.sbuf_base + 63) // 64 * 64]
        limit = nc.sbuf_usable_end

        def fixed(name, shape, dt=F32):
            n = int(np.prod(shape[1:])) * 4
            t = nc.alloc_sbuf_tensor_at(name, shape, dt, offset=base[0])
            base[0] += (n + 31) // 32 * 32
            return t

        raw_at = base[0]
        raw = fixed("raw", [P, RING, SLAB])
        rest = nc.alloc_sbuf_tensor_at("rest", [P, RING, SLAB], F32R, offset=raw_at)
        wh = fixed("wh", [P, RING, SLAB], F32R)
        X = fixed("X", [P, KT, 2 * T])
        xh = fixed("xh", [P, KT, 2 * T], F32R)
        xl = fixed("xl", [P, KT, 2 * T], F32R)
        const = fixed("const", [P, CONST_N])
        vec = fixed("vec", [P, VEC_N])
        sml = fixed("sml", [P, SML_N])
        mod = fixed("mod", [P, DEPTH, 9, KT, 2])
        sc = fixed("sc", [P, KT, 2])
        tiny = fixed("tiny", [P, 144])
        tiny2 = fixed("tiny2", [P, T])
        tiny3 = fixed("tiny3", [P, T])
        arena0 = base[0]

        def phase(spec):
            out, o = {}, arena0
            for name, shape, *dt in spec:
                n = (int(np.prod(shape[1:])) * 4 + 31) // 32 * 32
                out[name] = nc.alloc_sbuf_tensor_at(name, shape, dt[0] if dt else F32, offset=o)
                o += n
            assert o <= limit, (spec[0][0], o - limit)
            return out

        def cst(name, tab=None, at=None):
            at, tab = at or CONST, tab or const
            o, n = at[name]
            return tab[:, o:o + n]

        def vcol(name, i, n=1):
            o, _ = VEC[name]
            return vec[:, o + i:o + i + n]

        ident, ones = cst("ident"), cst("ones")
        PS = ctx.enter_context(nc.psum_tensor("PS", [P, 8, 512], F32))

        slab_full = [sig(f"slab_full{s}") for s in range(RING)]
        hi_done, slab_used = sig("hi_done"), sig("slab_used")
        lo_done = {"dve": sig("lo_done_dve"), "pool": sig("lo_done_pool")}
        drained = [sig("drained_even"), sig("drained_odd")]
        consts_in, acts_in = sig("consts_in"), sig("acts_in")
        out_stored = sig("out_stored")
        dve_step, act_step = sig("dve_step"), sig("act_step")
        b1 = phase([("CR", [P, 2, KT, P], F32R), ("TR", [P, 512]), ("c1", [P, C1_N]), ("MIX", [P, 8, T]), ("SM", [P, 2, 4, T]),
                    ("QK", [P, 7, T]), ("QI", [P, 3, T]), ("PT", [P, 2, 2, 512]), ("AB", [P, P + T]), ("CC", [P, 2, T]), ("CX", [P, 2, T]), ("CB", [P, 2, T]),
                    ("DU", [P, 2, 16 + T]), ("SG", [P, 8, T]), ("VT", [P, 2, T]), ("VW", [P, 2, 148]),
                    ("KC", [P, 2, 16]), ("VC", [16, P]), ("UP", [P, 2, 2 + T]), ("W2", [P, 2, 16 + T])])
        ff = phase([("HH", [P, FH, 2 * T], F32R), ("HL", [P, FH, 2 * T], F32R), ("SQ", [P, KT, 2 * T]),
                    ("HF", [P, 2, 2 * T]), ("SI", [P, 2, 2 * T]), ("NRM", [P, 4, 2 * T])])
        ev = phase([("c2", [P, C2_N]), ("Q", [P, 2, 2 * T]), ("K", [P, 2, 2 * T]), ("LK", [P, 2, 2 * T]),
                    ("V", [P, 4, 512]), ("CQ", [P, 4, 2 * T]), ("RS", [P, 4, 2 * T]),
                    ("W", [P, 12, 2 * T]), ("KDT", [P, 2, 4, P]), ("S", [P, 8, 2, P]),
                    ("OA", [P, 4, 2 * T])])
        ml = phase([("c2_", [P, C2_N]), ("PR", [P, 2, 512]), ("K_", [P, 2, 2 * T]), ("LK_", [P, 2, 2 * T]),
                    ("PTM", [P, 2, 512]), ("V_", [P, 2, 512]), ("CQ_", [P, 4, 2 * T]),
                    ("RS_", [P, 4, 2 * T]), ("SQ_", [P, 4, 2 * T]), ("QN", [P, 4, 2 * T]),
                    ("QR", [P, 2, 2 * T]), ("KN", [P, 4, 2 * T]), ("VM", [P, 4, 512])])
        od = phase([("nmask", [P, 64]), ("RPB", [P, 16, 7, 64]), ("NQ", [P, 8, T]), ("NK", [P, 8, 2 * T]),
                    ("NV", [P, 4, 1024]), ("NP", [P, 2, 512]), ("NPT", [P, 2, 512])])

        def turns_of(name):
            n = next(r[1] for r in RUNS if r[0] == name)
            turns = (n - (START[name] + n == NSLABS)) // 4
            return turns if turns >= 2 else 0

        def runs_of(eng, name, step, nxt=None):
            s0, n = START[name], dict((r[0], r[1]) for r in RUNS)[name]
            turns = turns_of(name)
            if turns:
                with eng.Fori(0, turns) as it:
                    for u in range(4):
                        step(Idx(s0 + u, it), it * 4 + u)
            for k in range(4 * turns, n):
                step(Idx(s0 + k), k)

        def width(i, after):
            turns = 1
            if i.reg is not None:
                turns = next(turns_of(name) for name, n, _ in RUNS if START[name] <= i.base < START[name] + n)
            return max([SIZE[n] for n in range(i.base + after, i.base + after + 4 * turns, 4) if n < NSLABS], default=0)

        def high(i):
            return wh[:, i.slot if i.base < FIRST_LEN else i.base % 2, :]

        def low(i):
            return rest[:, i.slot, :] if i.base < FIRST_LEN else wh[:, 2 + i.base % 2, :]

        def split_hi(act, i, n):
            act.wait_ge(slab_full[i.slot], i.count(16, 16 * (i.base // RING + 1)))
            if i.base >= FIRST_LEN:
                act.wait_ge(slab_used, i.count(4, i.base - 1))
            act.activation(high(i)[:, 0:n], raw[:, i.slot, 0:n], ACT.Copy).then_inc(hi_done, 1)

        def split_lo(eng, i, n, who="dve"):
            eng.wait_ge(hi_done, i.count(4, HI[i.base] + 1))
            eng.tensor_tensor(low(i)[:, 0:n], raw[:, i.slot, 0:n], high(i)[:, 0:n].bitcast(F32),
                              ALU.subtract).then_inc(lo_done[who], 1)

        def next_split(i):
            if i.base + 2 < FIRST_LEN:
                return 2 if KIND[i.base + 2] != "cmp" else 0
            return 1 if i.base + 1 >= FIRST_LEN and width(i, 1) else 0

        def act_ahead(act, i):
            n = next_split(i)
            if n:
                split_hi(act, i + n, width(i, n))

        def dve_ahead(dve, i):
            n = next_split(i)
            if n and splitter(i.base + n) == "dve":
                split_lo(dve, i + n, width(i, n))

        def wait_split(pe, i):
            who = splitter(i.base)
            pe.wait_ge(lo_done[who], i.count(4, LO[who][i.base] + 1))

        def slab_begin(pe, i):
            wait_split(pe, i)
            if i.d >= 2:
                pe.wait_ge(drained[i.par], i.count(2, i.d // 2))

        def product(pe, out, i, tiles, rows=slice(0, P), stage=None):
            hi, rest_ = high(i), low(i)
            for n, (o, h, lo) in enumerate(tiles):
                if stage is not None:
                    pe.wait_ge(ev_["xm_lo"], KT * stage + n + 1)
                for j, (w, x) in enumerate(((hi, h), (hi, lo), (rest_, h))):
                    m = pe.matmul(out, w[rows, o:o + P], x, start=n == 0 and j == 0,
                                  stop=n == len(tiles) - 1 and j == 2)
            return m

        def dense(pe, i, chunks, kts, xhi, xlo, c0, c1_, stage=None):
            slab_begin(pe, i)
            for c in range(chunks):
                m = product(pe, PS[:, 2 * i.par + c, 0:c1_ - c0], i,
                            [((c * kts + k) * P, xhi[:, k, c0:c1_], xlo[:, k, c0:c1_]) for k in range(kts)],
                            stage=None if c else stage)
            m.then_inc(slab_used, 1)

        def token_major(pe, i, ntok, n, xhi, xlo, kts, krow=0):
            slab_begin(pe, i)
            for tt in range(ntok):
                out = PS[:, 2 * i.par + tt // 2, (tt % 2) * 256:(tt % 2) * 256 + n]
                for k in range(kts):
                    for j, (x, w) in enumerate(((xhi, high(i)), (xhi, low(i)), (xlo, high(i)))):
                        m = pe.matmul(out, x[:, krow + k, tt * P:(tt + 1) * P], w[:, k * n:(k + 1) * n],
                                      start=k == 0 and j == 0, stop=k == kts - 1 and j == 2)
            m.then_inc(slab_used, 1)

        def dense_one(pe, i, chunks=2):
            slab_begin(pe, i)
            for c in range(chunks):
                m = product(pe, PS[:, i.par, c * T:(c + 1) * T], i,
                            [((c * KT + k) * P, xh[:, k, 0:T], xl[:, k, 0:T]) for k in range(KT)])
            m.then_inc(slab_used, 1)

        def bank(i):
            return PS[:, i.par, :].rearrange("p (c t) -> p c t", c=2)

        def banks(i, n):
            return PS[:, 2 * i.par:2 * i.par + 2, 0:n]

        class Chain:

            def __init__(self, eng, sem):
                self.eng, self.sem, self.n = eng, sem, 0

            def after(self, ins):
                self.n += 1
                ins.then_inc(self.sem, 1)
                self.eng.wait_ge(self.sem, self.n)

        def rstd(ch, dve, out, total, n):
            inverse_root(ch, dve, out, dve.tensor_scalar(out, total, 1.0 / n, EPS, ALU.mult, ALU.add))

        roots = {"dve": 0, "act": 0}

        def inverse_root(ch, dve, out, ins):
            roots["dve"] += 1
            ins.then_inc(ev_["var_ready"], 1)
            dve.wait_ge(ev_["root_done"], roots["dve"])
            ch.after(dve.reciprocal(out, out))

        def act_root(act, out):
            roots["act"] += 1
            act.wait_ge(ev_["var_ready"], roots["act"])
            act.activation(out, out, ACT.Sqrt).then_inc(ev_["root_done"], 1)

        def bc(ap, n):
            return ap.unsqueeze(1).broadcast_to([ap.shape[0], n, ap.shape[1]])

        def bl(ap, n):
            return ap.unsqueeze(len(ap.shape)).broadcast_to(list(ap.shape) + [n])

        IN = ["qi", "kika", "qa", "qb", "kskw", "va"]
        UNITS = [("S", 0), ("W", 0), ("C", 0), ("A", 0), ("S", 1), ("W", 1), ("C", 1), ("A", 1)]
        UN = len(UNITS)
        TR, c1 = b1["TR"], b1["c1"]
        CR = b1["CR"]
        SMF = b1["SM"][:, :, :, :].rearrange("p a b c -> p (a b c)")
        CXF = b1["CX"][:, :, :].rearrange("p c t -> p (c t)")
        BLK = b1["PT"][:, 0, 0, :].rearrange("p (n j) -> p n j", n=16)
        KCV = b1["PT"][:, 1, 0, 0:T]
        ccol = lambda name: cst(name, c1, C1)

        def keys_of(u):
            kind, blk = UNITS[u]
            return NCMP if kind == "C" else P * (blk + 1)

        names1 = """x_chunk v_done sc_lo cr_zero tr_ready mod_cols mod_read late_in ctx_in kc_raw conv_done conv_in perm_read sq_ready rms_in rms_out xm_written qi_raw perms_done roped blk_ready cmp_raw cmp_done idx_scores_out
                    idx_relu idx_used scores_out soft_max exp_done p_ready pt_ready pt_copied pv_done o_taken pool_in pool_out
                    var_ready root_done mixh_done mixl_done gates_e kc_ready rms_sum sc_ready x_ready
                    md_tmp xm_hi xm_lo x_scaled gate_act h_hi h_lo ln_sq ln_in ln_sum
                    z_out z_in z_ln ge_in ge_done kq_ready kd_t kdt_done att_out att_masked u_out s_ready og_out oa_done
                    gq_sum gq_sq mg_hi mg_ready cq_sq cq_sum cq_ready cq_hi cq_lo qk2_ready rm_out c2_in c3_in
                    fmax fsoft fexp fnorm ftr fcopy fpv fhi flo qkv_ready""".split()
        ev_ = {n: sig(n) for n in names1}

        block = ctx.enter_context(nc.Block())

        @block.sync
        def _(sp):
            for name, n, f in RUNS:
                if START[name] > UPTO_SLAB:
                    break

                def load(i, k, name=name):
                    if i.base >= RING + FIRST_LEN:
                        sp.wait_ge(lo_done["dve"], i.count(4, LO["dve"][i.base - RING] + 1))
                    elif i.base >= RING:
                        sp.wait_ge(slab_used, i.count(4, i.base - RING + 1))
                    src = a[name][bass.ds(k, 1)].rearrange("a p n -> p (a n)") if i.reg is not None else a[name][k]
                    f = SIZE[i.base]
                    sp.dma_start(raw[:, i.slot, 0:f], src[:, 0:f]).then_inc(slab_full[i.slot], 16)
                if START[name] == UPTO_SLAB:
                    load(Idx(UPTO_SLAB), 0)
                    load(Idx(UPTO_SLAB + 1), 1)
                    break
                if name.startswith("layer"):
                    for k in range(n):
                        load(Idx(START[name] + k), k)
                else:
                    runs_of(sp, name, load)
            if UPTO < 9:
                sp.wait_ge(ev_["x_ready"], UPTO)
            else:
                sp.wait_ge(ev_["x_chunk"], KT * 7)
            sp.dma_start(a["out"], X[:, :, 0:T]).then_inc(out_stored, 16)
            sp.wait_ge(out_stored, 16)

        FFN_STAGES = {0: (0, 1, 0, 2 * T), 2: (0, 2, 6, 2 * T), 3: (1, 1, 0, 2 * T), 5: (1, 2, 6, T)}
        WIDTH = [2 * T, 2 * T, 2 * T, 2 * T, T, T]
        SQ, HF, SI, NRM, HH, HL = (ff[n] for n in ("SQ", "HF", "SI", "NRM", "HH", "HL"))
        c2 = ev["c2"]
        W = ev["W"]
        work = lambda n: W[:, 2 * n:2 * n + 2, :]
        G_, B_, T1, QE, KE, QB = range(6)
        GATE_BUFFERS = ((T1, QB), (KE, B_))
        CH, CL = xh[:, 4:8, :], xl[:, 4:8, :]
        AM = W[:, 2 * T1:2 * T1 + 2, :].rearrange("p a (b t) -> p a b t", t=GC)
        ORDER = ([4, 5, 6, 7, 0, 1, 2, 3], [7, 6, 5, 4, 3, 2, 1, 0])
        MLA_UNITS = [(h, blk, 0) for h in range(4) for blk in range(2)] + [(h, blk, 1) for h in range(4) for blk in range(2)]
        NA_UNITS = [(h, blk, 0) for h in range(16) for blk in range(2)]

        def last_slabs(m):
            if m in (1, 4):
                s0 = START["eout" if m == 1 else "oout"]
                return [(Idx(s0 + n), slice(2 * n, 2 * n + 2)) for n in range(4)]
            s0 = START["ffo{1}{0}1".format(*FFN_STAGES[m])]
            return [(Idx(s0 + k), slice(k, k + 1)) for k in range(KT)]

        SQUARES = np.cumsum([0] + [len(last_slabs(m)) for m in range(6)]).tolist()

        def hidden_before(m, half):
            return ([0, 2, 3, 5].index(m) * 2 + half) * FH

        STAGES = [(0, 0), (0, 3), (0, 6), (1, 0), (1, 3), (1, 6)]

        def modulations(m):
            l, j = STAGES[m]
            for br in range(WIDTH[m - 1] // T if m else 2):
                cols = slice(br * T, (br + 1) * T)
                yield cols, (lambda k: mod[:, l, j + 1, k, br:br + 1]), (lambda k: mod[:, l, j, k, br:br + 1])

        def act_modulate(act, m):
            if m == 0:
                act.wait_ge(ev_["ctx_in"], 16)
            for k in range(KT):
                act.wait_ge(ev_["x_chunk"], KT * m + k + 1)
                for cols, scale, shift in modulations(m):
                    mm = act.activation(xh[:, k, cols], X[:, k, cols], ACT.Identity, bias=shift(k), scale=scale(k))
                mm.then_inc(ev_["xm_hi"], 1)
            act.wait_ge(ev_["xm_hi"], KT * (m + 1))
            act.wait_ge(ev_["v_done"], KT * (m + 1))
            act.activation(X[:, :, 0:WIDTH[m]], X[:, :, 0:WIDTH[m]], ACT.Copy, scale=ALPHA).then_inc(ev_["x_scaled"], 1)

        def pool_modulate(pool, m):
            if m == 0:
                pool.wait_ge(ev_["ctx_in"], 16)
            for k in range(KT):
                pool.wait_ge(ev_["x_chunk"], KT * m + k + 1)
                for cols, scale, shift in modulations(m):
                    mm = pool.tensor_scalar(SQ[:, k, cols], X[:, k, cols], scale(k), shift(k), ALU.mult, ALU.add)
                mm.then_inc(ev_["v_done"], 1)

        def dve_modulate(dve, m, norm):
            n = WIDTH[m - 1] if m else 2 * T

            def take_rest(k):
                dve.wait_ge(ev_["v_done"], KT * m + k + 1)
                dve.wait_ge(ev_["xm_hi"], KT * m + k + 1)
                dve.tensor_tensor(xl[:, k, 0:n], SQ[:, k, 0:n], xh[:, k, 0:n].bitcast(F32), ALU.subtract)\
                    .then_inc(ev_["xm_lo"], 1)
            for k in range(KT):
                norm(k).then_inc(ev_["x_chunk"], 1)
                if m < 6 and k:
                    take_rest(k - 1)
            if m < 6:
                take_rest(KT - 1)

        def last_pair(eng, i):
            for par in range(2):
                last = i.d - (i.d - par) % 2
                eng.wait_ge(drained[par], last // 2 + 1)

        def add_residual(dve, m, l, j, i, k, bank, inc):
            for br in range(WIDTH[m] // T):
                if i.reg is None:
                    xk, g = X[:, k, br * T:(br + 1) * T], mod[:, l, j, k, br:br + 1]
                else:
                    xk = X[:, bass.ds(k, 1), br * T:(br + 1) * T].rearrange("p a t -> p (a t)")
                    g = mod[:, l, j, bass.ds(k, 1), br]
                mm = dve.scalar_tensor_tensor(out=xk, in0=PS[:, bank, br * T:(br + 1) * T], scalar=g, in1=xk,
                                              op0=ALU.mult, op1=ALU.add)
            if inc:
                mm.then_inc(drained[i.par], 1)

        def act_squares(act, m, i, chunks):
            n = WIDTH[m]
            act.wait_ge(drained[i.par], i.d // 2 + 1)
            act.activation(SQ[:, chunks, 0:n], X[:, chunks, 0:n], ACT.Square).then_inc(ev_["ln_sq"], 1)

        def pool_stats(pool, ch, m, slabs):
            n = WIDTH[m]
            for s, (i, chunks) in enumerate(slabs):
                for j, (src, sem, count) in enumerate(((X, drained[i.par], i.d // 2 + 1), (SQ, ev_["ln_sq"], SQUARES[m] + s + 1))):
                    pool.wait_ge(sem, count)
                    for k in range(chunks.start, chunks.stop):
                        if k == 0:
                            continue
                        ins = pool.tensor_tensor(NRM[:, j, 0:n], src[:, 0, 0:n] if k == 1 else NRM[:, j, 0:n], src[:, k, 0:n], ALU.add)
                        if k < KT - 1:
                            ch.after(ins)
                        else:
                            ins.then_inc(ev_["ln_in"], 1)

        def pe_sums(pe, m):
            n = WIDTH[m]
            for j in range(2):
                pe.wait_ge(ev_["ln_in"], 2 * m + j + 1)
                pe.matmul(PS[:, 4 + j, 0:n], ones, NRM[:, j, 0:n], start=True, stop=True).then_inc(ev_["ln_sum"], 1)

        def post_norm(dve, ch, m):
            n = WIDTH[m]
            mean, var = NRM[:, 2, 0:n], NRM[:, 3, 0:n]
            dve.wait_ge(ev_["ln_sum"], 2 * m + 1)
            ch.after(dve.tensor_scalar(mean, PS[:, 4, 0:n], 1.0 / D, None, ALU.mult))
            ch.after(dve.tensor_tensor(var, mean, mean, ALU.mult))
            dve.wait_ge(ev_["ln_sum"], 2 * m + 2)
            ch.after(dve.scalar_tensor_tensor(out=var, in0=PS[:, 5, 0:n], scalar=1.0 / D, in1=var,
                                              op0=ALU.mult, op1=ALU.subtract))
            inverse_root(ch, dve, var, dve.tensor_scalar(var, var, 0.0, EPS, ALU.max, ALU.add))

            def norm(k):
                ch.after(dve.tensor_tensor(X[:, k, 0:n], X[:, k, 0:n], mean, ALU.subtract))
                return dve.tensor_tensor(X[:, k, 0:n], X[:, k, 0:n], var, ALU.mult)
            dve_modulate(dve, m + 1, norm)

        def act_ffn(act, m):
            l, f, j, n = FFN_STAGES[m]
            act_modulate(act, m)
            for half in range(2):
                def gate(i, k):
                    act_ahead(act, i)
                    act.wait_ge(slab_used, i.count(4, i.base + 1))
                    act.activation(SI[:, i.par, 0:n], PS[:, 2 * i.par, 0:n], ACT.Silu).then_inc(ev_["gate_act"], 1)
                runs_of(act, f"ffi{f}{l}{half}", gate)
                if half == 0:
                    runs_of(act, f"ffo{f}{l}0", lambda i, k: act_ahead(act, i))
            for i, chunks in last_slabs(m):
                act_ahead(act, i)
                act_squares(act, m, i, chunks)
            act_root(act, NRM[:, 3, 0:n])

        def pe_ffn(pe, m):
            l, f, j, n = FFN_STAGES[m]
            for half in range(2):
                first = START[f"ffi{f}{l}0"]
                runs_of(pe, f"ffi{f}{l}{half}", lambda i, k: dense(pe, i, 2, KT, xh, xl, 0, n, m if i.base == first else None))
                pe.wait_ge(ev_["h_lo"], hidden_before(m, half) + FH)
                runs_of(pe, f"ffo{f}{l}{half}", lambda i, k: dense(pe, i, 1, FH, HH, HL, 0, n))
            pe_sums(pe, m)

        def dve_ffn(dve, ch, m):
            l, f, j, n = FFN_STAGES[m]
            dve.wait_ge(ev_["x_scaled"], m + 1)
            for half in range(2):
                h0 = hidden_before(m, half)

                def hidden(i, k):
                    dve_ahead(dve, i)
                    dve.wait_ge(ev_["gate_act"], k + (h0 + 1))
                    hf = HF[:, i.par, 0:n]
                    dve.tensor_tensor(hf, SI[:, i.par, 0:n], PS[:, 2 * i.par + 1, 0:n], ALU.mult)\
                        .then_inc(drained[i.par], 1)
                    dve.wait_ge(drained[i.par], i.count(2, i.d // 2 + 1))
                    if i.reg is None:
                        hh, hl = HH[:, k, 0:n], HL[:, k, 0:n]
                    else:
                        hh = HH[:, bass.ds(k, 1), 0:n].rearrange("p a t -> p (a t)")
                        hl = HL[:, bass.ds(k, 1), 0:n].rearrange("p a t -> p (a t)")
                    dve.tensor_copy(hh, hf).then_inc(ev_["h_hi"], 1)
                    dve.wait_ge(ev_["h_hi"], k + (h0 + 1))
                    dve.tensor_tensor(hl, hf, hh.bitcast(F32), ALU.subtract).then_inc(ev_["h_lo"], 1)
                runs_of(dve, f"ffi{f}{l}{half}", hidden)

                def down(i, k):
                    dve_ahead(dve, i)
                    dve.wait_ge(slab_used, i.count(4, i.base + 1))
                    add_residual(dve, m, l, j + 2, i, k, 2 * i.par, True)
                runs_of(dve, f"ffo{f}{l}{half}", down)
            post_norm(dve, ch, m)

        def unit_keys(units, u):
            return (0, 2 * T) if units[u][2] == 0 else (T, 2 * T)

        def groups(units, na):
            step = 4 if na else 2
            return {g * step + step - 1: g for g in range(len(units) // step)}

        def pe_attend(pe, units, na, f0, g0, q_ap, k_ap, v_ap, pr, ptm):
            ends = groups(units, na)

            def score(u):
                h, blk, ctx_ = units[u]
                k0, k1 = unit_keys(units, u)
                if f0 + u >= 2 and u >= 2:
                    pe.wait_ge(ev_["fexp"], f0 + u - 1)
                pairs = q_ap(h, ctx_ * T + blk * P, k0, k1)
                for n, (q, k) in enumerate(pairs):
                    mm = pe.matmul(PS[:, u % 2, 0:k1 - k0], q, k, start=n == 0, stop=n == len(pairs) - 1)
                mm.then_inc(ev_["fmax"], 1)
            score(0)
            score(1)
            for u in range(len(units)):
                h, blk, ctx_ = units[u]
                k0, k1 = unit_keys(units, u)
                pe.wait_ge(ev_["fnorm"], f0 + u + 1)
                if u >= 2:
                    pe.wait_ge(ev_["fcopy"], f0 + u - 1)
                for kt in range((k1 - k0) // P):
                    mm = pe.transpose(PS[:, 2 + u % 2, kt * P:(kt + 1) * P], pr[:, u % 2, kt * P:(kt + 1) * P], ident)
                mm.then_inc(ev_["ftr"], 1)
                if u + 2 < len(units):
                    score(u + 2)
                pe.wait_ge(ev_["fcopy"], f0 + u + 1)
                g = u // (4 if na else 2)
                if g >= 2 and u % (4 if na else 2) == 0:
                    pe.wait_ge(ev_["flo"], g0 + g - 1)
                rows = slice((h % 2) * HD, (h % 2) * HD + HD) if na else slice(0, P)
                nk = (k1 - k0) // P
                for kt in range(nk):
                    mm = pe.matmul(PS[rows, 4 + g % 2, blk * P:(blk + 1) * P], v_ap(h, k0 // P + kt),
                                   ptm[:, u % 2, kt * P:(kt + 1) * P], start=kt == 0, stop=kt == nk - 1)
                mm.then_inc(ev_["fpv"], 1)

        def act_attend(act, units, na, f0, g0, scale, pr, ptm, chunk0):
            ends = groups(units, na)

            def exp(u):
                k0, k1 = unit_keys(units, u)
                act.wait_ge(ev_["fsoft"], f0 + u + 1)
                if u >= 2:
                    act.wait_ge(ev_["ftr"], f0 + u - 1)
                act.activation(pr[:, u % 2, 0:k1 - k0], PS[:, u % 2, 0:k1 - k0], ACT.Exp, scale=scale,
                               bias=tiny[:, u % 2:u % 2 + 1], accum_out=tiny[:, 2 + u % 2:3 + u % 2]).then_inc(ev_["fexp"], 1)

            def hi(g):
                size = 4 if na else 2
                act.wait_ge(ev_["fpv"], f0 + (g + 1) * size)
                ctx_ = units[g * size][2]
                act.activation(xh[:, chunk0 + g % (8 if na else 4), ctx_ * T:ctx_ * T + T], PS[:, 4 + g % 2, 0:T], ACT.Copy)\
                    .then_inc(ev_["fhi"], 1)
            exp(0)
            for u in range(len(units)):
                if u + 1 < len(units):
                    exp(u + 1)
                k0, k1 = unit_keys(units, u)
                act.wait_ge(ev_["ftr"], f0 + u + 1)
                if u >= 2:
                    act.wait_ge(ev_["fpv"], f0 + u - 1)
                act.activation(ptm[:, u % 2, 0:k1 - k0], PS[:, 2 + u % 2, 0:k1 - k0], ACT.Copy).then_inc(ev_["fcopy"], 1)
                if u - 1 in ends:
                    hi(ends[u - 1])
            hi(ends[len(units) - 1])

        def dve_attend(dve, ch, units, na, f0, g0, scale, pr, chunk0):
            ends = groups(units, na)

            def maxima(u):
                h, blk, ctx_ = units[u]
                k0, k1 = unit_keys(units, u)
                dve.wait_ge(ev_["fmax"], f0 + u + 1)
                s = PS[:, u % 2, 0:k1 - k0]
                if na:
                    for half in range(2):
                        r, rows = 2 * blk + half, slice(half * HD, half * HD + HD)
                        o = PS[rows, u % 2, 0:T].rearrange("p (r c) -> p r c", c=64)
                        mm = dve.tensor_tensor(o, o, od["RPB"][rows, h, 3 - r:7 - r, :], ALU.add)
                    ch.after(mm)
                nm = tiny[:, u % 2:u % 2 + 1]
                mm = dve.tensor_reduce(nm, s, AX, ALU.max, negate=True)
                if scale != 1.0:
                    ch.after(mm)
                    mm = dve.tensor_scalar(nm, nm, scale, None, ALU.mult)
                mm.then_inc(ev_["fsoft"], 1)

            def lo(g):
                size = 4 if na else 2
                dve.wait_ge(ev_["fhi"], g0 + g + 1)
                ctx_ = units[g * size][2]
                c = chunk0 + g % (8 if na else 4)
                dve.tensor_tensor(xl[:, c, ctx_ * T:ctx_ * T + T], PS[:, 4 + g % 2, 0:T],
                                  xh[:, c, ctx_ * T:ctx_ * T + T].bitcast(F32), ALU.subtract).then_inc(ev_["flo"], 1)
            maxima(0)
            for u in range(len(units)):
                if u + 1 < len(units):
                    maxima(u + 1)
                k0, k1 = unit_keys(units, u)
                dve.wait_ge(ev_["fexp"], f0 + u + 1)
                r = tiny[:, 4 + u % 2:5 + u % 2]
                mm = dve.reciprocal(r, tiny[:, 2 + u % 2:3 + u % 2])
                ch.after(mm)
                p = pr[:, u % 2, 0:k1 - k0]
                dve.tensor_scalar(p, p, r, None, ALU.mult).then_inc(ev_["fnorm"], 1)
                if u - 2 in ends:
                    lo(ends[u - 2])
            lo(ends[len(units) - 1])

        def act_even(act, ch):
            act.wait_ge(ev_["x_chunk"], KT + 1)
            act.dma_start(c2[:, :], a["c2"]).then_inc(ev_["c2_in"], 16)
            act_modulate(act, 1)
            s0 = START["even"]

            def act_gate_logs(d):
                t1, qb = GATE_BUFFERS[d]
                act.wait_ge(ev_["z_in"], d + 1)
                ch.after(act.activation(work(t1), work(t1), ACT.Exp))
                act.activation(work(t1), work(t1), ACT.Ln, bias=1.0).then_inc(ev_["z_ln"], 1)

            def act_gate_exps(d):
                t1, qb = GATE_BUFFERS[d]
                act.wait_ge(ev_["ge_in"], 2 * d + 1)
                ch.after(act.activation(work(QE), work(t1), ACT.Exp))
                act.activation(work(KE), work(t1), ACT.Exp, scale=-1.0)
                act.wait_ge(ev_["ge_in"], 2 * d + 2)
                act.activation(work(qb), work(B_), ACT.Exp).then_inc(ev_["ge_done"], 1)
                act.activation(work(G_), work(G_), ACT.Exp)
                act.activation(tiny[:, 32:48], tiny[:, 0:16], ACT.Exp).then_inc(ev_["ge_done"], 1)

            def turned_keys(d):
                act.wait_ge(ev_["kd_t"], d + 1)
                act.activation(ev["KDT"][:, :, :, :], PS[:, 4:6, :].rearrange("p a (t c) -> p a t c", c=P), ACT.Copy)\
                    .then_inc(ev_["kdt_done"], 1)

            for k in range(9):
                i = Idx(s0 + k)
                act_ahead(act, i)
                if k == 4:
                    act_gate_logs(0)
                if k == 5:
                    act_gate_exps(0)
                if k == 7:
                    turned_keys(0)
                    act.wait_ge(drained[1 - i.par], (i.d - 1) // 2 + 1)
                    act.activation(ml["VM"][:, :, :], ev["CQ"][:, :, :], ACT.Square).then_inc(ev_["cq_sq"], 1)
                if k >= 7:
                    act.wait_ge(slab_used, i.base + 1)
                    act.activation(ev["RS"][:, 2 * (k - 7):2 * (k - 7) + 2, :], banks(i, 2 * T), ACT.Silu)\
                        .then_inc(drained[i.par], 1)
            for j in range(2):
                act_root(act, ev["OA"][:, j, :])
            act.wait_ge(ev_["cq_ready"], 1)
            act.activation(CH, ev["CQ"][:, :, :], ACT.Copy).then_inc(ev_["cq_hi"], 1)
            act_gate_logs(1)
            act_gate_exps(1)
            turned_keys(1)
            act.wait_ge(ev_["oa_done"], 2)
            act.activation(W[:, 0:4, :], ev["OA"][:, :, :], ACT.Square).then_inc(ev_["gq_sq"], 1)
            act_ahead(act, Idx(START["uq"]))
            act_root(act, W[:, 0:4, :])
            act.wait_ge(ev_["mg_ready"], 1)
            act.activation(xh[:, 0:4, :], ev["OA"][:, :, :], ACT.Copy).then_inc(ev_["mg_hi"], 1)
            for k in range(1, 7):
                act_ahead(act, Idx(START["uq"] + k))
            act_attend(act, MLA_UNITS, False, 0, 0, MLA_SCALE, ml["PR"], ml["PTM"], 4)
            act_out(act, 1)

        def pe_even(pe):
            s0 = START["even"]

            def gate_inputs(d):
                o, _ = SML["wg2"]
                for ft in range(2):
                    r = slice(32 * d, 32 * d + 16)
                    mm = pe.matmul(PS[:, 4 + ft, :], sml[r, o + ft * P:o + (ft + 1) * P], ev["LK"][r, 0, :], start=True, stop=True)
                mm.then_inc(ev_["z_out"], 1)

            def turn_keys(d):
                pe.wait_ge(ev_["kq_ready"], d + 1)
                for ft in range(2):
                    for tt in range(4):
                        mm = pe.transpose(PS[:, 4 + ft, tt * P:(tt + 1) * P], W[:, 2 * G_ + ft, tt * P:(tt + 1) * P], ident)
                mm.then_inc(ev_["kd_t"], 1)

            for k in range(9):
                i = Idx(s0 + k)
                if k in (3, 4):
                    token_major(pe, i, 4, 256, xh, xl, KT)
                else:
                    dense(pe, i, 2, KT, xh, xl, 0, 2 * T, None if k else 1)
                if k == 3:
                    pe.wait_ge(drained[1 - i.par], (i.d - 1) // 2 + 1)
                    gate_inputs(0)
                if k == 6:
                    turn_keys(0)
                if k == 7:
                    pe.wait_ge(ev_["cq_sq"], 1)
                    for c in range(3):
                        pe.matmul(PS[:, 6, :], ones, ml["VM"][:, c, :], start=c == 0, stop=c == 2)
                    pe.matmul(PS[:, 7, :], ones, ml["VM"][:, 3, :], start=True, stop=True).then_inc(ev_["cq_sum"], 1)
            last_pair(pe, Idx(s0 + 8))
            for d in range(2):
                if d:
                    pe.wait_ge(ev_["oa_done"], d)
                    turn_keys(d)
                for c in range(8):
                    for h in range(4):
                        r, ft, tt = slice((h % 2) * HD, (h % 2) * HD + HD), h // 2, c // 2
                        mm = pe.matmul(PS[(c % 2) * HD:(c % 2) * HD + HD, h % 2, (tt * 2 + ft) * GC:(tt * 2 + ft + 1) * GC],
                                       W[r, 2 * KE + ft, c * GC:(c + 1) * GC], W[r, 2 * QE + ft, c * GC:(c + 1) * GC],
                                       start=True, stop=True)
                mm.then_inc(ev_["att_out"], 1)
                pe.wait_ge(ev_["kdt_done"], d + 1)
                if d == 0:
                    gate_inputs(1)
                    pe.wait_ge(ev_["cq_ready"], 1)
                for c in ORDER[d][:7]:
                    cp, tt = c % 2, c // 2
                    rows = slice(cp * HD, cp * HD + HD)
                    for h in range(4):
                        o = (tt % 2) * 256 + (h // 2) * P
                        mm = pe.matmul(PS[(h % 2) * HD:(h % 2) * HD + HD, 2 + 4 * cp + tt // 2, o:o + P],
                                       ev["KDT"][rows, h // 2, tt, (h % 2) * HD:(h % 2) * HD + HD],
                                       ev["V"][rows, tt, h * P:(h + 1) * P], start=True, stop=True)
                mm.then_inc(ev_["u_out"], 1)
                pe.wait_ge(ev_["att_masked"], d + 1)
                pe.wait_ge(ev_["z_in"], 2)
                pe.wait_ge(ev_["s_ready"], d + 1)
                for c in range(8):
                    cp, tt, n = c % 2, c // 2, ORDER[d].index(c)
                    tp = tt // 2
                    for h in range(4):
                        rows = slice(cp * HD, cp * HD + HD)
                        o = ((tt % 2) * 4 + h) * GC
                        pe.matmul(PS[:, 2 * tp + cp, o:o + GC], ev["V"][rows, tt, h * P:(h + 1) * P],
                                  AM[rows, h % 2, tt * 2 + h // 2, :], start=True, stop=True)
                        r = slice((h % 2) * HD, (h % 2) * HD + HD)
                        o = (h // 2) * T + (c % 4) * GC
                        mm = pe.matmul(PS[:, 4 + 2 * tp + h % 2, o:o + GC], ev["S"][r, n, h // 2, :],
                                       W[r, 2 * GATE_BUFFERS[d][1] + h // 2, c * GC:(c + 1) * GC], start=True, stop=True)
                mm.then_inc(ev_["og_out"], 1)
            pe.wait_ge(ev_["oa_done"], 2)
            pe.wait_ge(ev_["cq_lo"], 1)
            for k in range(3):
                dense(pe, Idx(START["uq"] + k), 2, 3, CH, CL, 0, 2 * T)
                if k == 0:
                    pe.wait_ge(ev_["gq_sq"], 1)
                    for h in range(4):
                        mm = pe.matmul(PS[:, 4 + h, :], ones, W[:, h, :], start=True, stop=True)
                    mm.then_inc(ev_["gq_sum"], 1)
            for k in range(4):
                i = Idx(START["ukv"] + k)
                if k < 2:
                    slab_begin(pe, i)
                    for c in range(2):
                        mm = product(pe, PS[:, 2 * i.par + c, :], i, [(c * P, CH[:, 3, :], CL[:, 3, :])])
                    mm.then_inc(slab_used, 1)
                else:
                    token_major(pe, i, 4, 256, CH, CL, 1, krow=3)
            last_pair(pe, Idx(START["ukv"] + 3))
            pe.wait_ge(ev_["mg_ready"], 1)
            pe.matmul(PS[:, 4, :], cst("permM"), ml["QR"][:, :, 0:T], start=True, stop=True)
            pe.matmul(PS[:, 5, 0:T], cst("permM"), ev["LK"][:, 1, 0:T], start=True, stop=True).then_inc(ev_["rm_out"], 1)
            pe.wait_ge(ev_["qk2_ready"], 1)

            def qk(h, q0, k0, k1):
                r = slice((h % 2) * HD, (h % 2) * HD + HD)
                return [(ml["QN"][:, h, q0:q0 + P], ml["KN"][:, h, k0:k1]), (ml["QR"][r, h // 2, q0:q0 + P], ev["LK"][r, 1, k0:k1])]
            pe_attend(pe, MLA_UNITS, False, 0, 0, qk, None, lambda h, tt: ml["VM"][:, tt, h * P:(h + 1) * P], ml["PR"], ml["PTM"])
            pe.wait_ge(ev_["flo"], 8)
            for k in range(4):
                dense(pe, Idx(START["eout"] + k), 2, KT, xh, xl, 0, 2 * T)
            pe_sums(pe, 1)

        def dve_even(dve, ch):
            s0 = START["even"]
            S, OA, CQ = ev["S"], ev["OA"], ev["CQ"]
            chunks = lambda t: t.rearrange("p f (c t) -> p (f c) t", t=GC)

            def gate_input(d):
                t1 = GATE_BUFFERS[d][0]
                dve.wait_ge(ev_["z_out"], d + 1)
                for ft in range(2):
                    mm = dve.tensor_scalar(W[:, 2 * G_ + ft, :], PS[:, 4 + ft, :], vcol("bg", 2 * d + ft), None, ALU.add)
                ch.after(mm)
                dve.scalar_tensor_tensor(out=work(t1), in0=work(G_), scalar=-1.0, in1=work(G_), op0=ALU.mult, op1=ALU.min)\
                    .then_inc(ev_["z_in"], 1)
                dve.wait_ge(ev_["z_in"], d + 1)

            def gate_sums(d):
                T1_ = GATE_BUFFERS[d][0]
                ch.after(dve.tensor_scalar(work(G_), work(G_), 0.0, 1.0 / 16, ALU.min, ALU.mult))
                dve.wait_ge(ev_["z_ln"], d + 1)
                ch.after(dve.scalar_tensor_tensor(out=work(G_), in0=work(T1_), scalar=-1.0 / 16, in1=work(G_),
                                                  op0=ALU.mult, op1=ALU.add))
                for ft in range(2):
                    mm = dve.tensor_tensor_scan(W[:, 2 * B_ + ft, :], cst("reset", c2, C2), W[:, 2 * G_ + ft, :], 0.0,
                                                ALU.mult, ALU.add)
                ch.after(mm)
                g, b, t1 = chunks(work(G_)), chunks(work(B_)), chunks(work(T1_))
                tot, ref = tiny[:, 0:16], tiny[:, 16:32]
                ch.after(dve.tensor_copy(tot, b[:, :, GC - 1]))
                if d:
                    ch.after(dve.tensor_tensor(b, bl(tot, GC), b, ALU.subtract))
                    ch.after(dve.tensor_tensor(b, b, g, ALU.add))
                ch.after(dve.tensor_copy(ref, b[:, :, GC // 2 - 1 + d]))
                ch.after(dve.tensor_tensor(t1, b, bl(ref, GC), ALU.subtract))
                dve.tensor_scalar(work(T1_), work(T1_), 80.0, -80.0, ALU.min, ALU.max).then_inc(ev_["ge_in"], 1)
                dve.tensor_tensor(g, bl(tot, GC), b, ALU.subtract).then_inc(ev_["ge_in"], 1)
                dve.wait_ge(ev_["ge_in"], 2 * d + 2)

            def gate_products(d):
                qb = GATE_BUFFERS[d][1]
                dve.wait_ge(ev_["ge_done"], 2 * d + 1)
                dve.tensor_tensor(work(QE), work(QE), ev["Q"][:, :, :], ALU.mult)
                dve.tensor_tensor(work(KE), work(KE), ev["K"][:, :, :], ALU.mult)
                dve.tensor_tensor(work(qb), work(qb), ev["Q"][:, :, :], ALU.mult)
                dve.wait_ge(ev_["ge_done"], 2 * d + 2)
                dve.tensor_tensor(work(G_), work(G_), ev["K"][:, :, :], ALU.mult).then_inc(ev_["kq_ready"], 1)

            for k in range(9):
                i = Idx(s0 + k)
                dve_ahead(dve, i)
                if k == 8:
                    dve.wait_ge(ev_["cq_sum"], 1)
                    for j, n in ((0, 384), (1, P)):
                        rstd(ch, dve, OA[:, j, :], PS[:, 6 + j, :], n)
                    dve.memset(S[:, 0, :, :], 0.0)
                    for c in range(4):
                        g = vcol("qnorm", c) if c < 3 else vcol("kvnorm", 0)
                        mm = dve.scalar_tensor_tensor(out=CQ[:, c, :], in0=CQ[:, c, :], scalar=g, in1=OA[:, c // 3, :],
                                                      op0=ALU.mult, op1=ALU.mult)
                    mm.then_inc(ev_["cq_ready"], 1)
                if k >= 7:
                    continue
                dve.wait_ge(slab_used, i.base + 1)
                if k == 0:
                    mm = dve.tensor_scalar(ev["Q"][:, :, :], banks(i, 2 * T), HD ** -0.5, None, ALU.mult)
                elif k in (1, 2):
                    mm = dve.tensor_copy(ev["K" if k == 1 else "LK"][:, :, :], banks(i, 2 * T))
                elif k in (3, 4):
                    mm = dve.tensor_copy(ev["V"][:, :, 256 * (k - 3):256 * (k - 2)],
                                         banks(i, 512).rearrange("p a (b n) -> p (a b) n", b=2))
                else:
                    mm = dve.tensor_copy(ev["CQ"][:, 2 * (k - 5):2 * (k - 5) + 2, :], banks(i, 2 * T))
                mm.then_inc(drained[i.par], 1)
                if k == 3:
                    gate_input(0)
                if k == 4:
                    dve.wait_ge(ev_["c2_in"], 16)
                    gate_sums(0)
                if k == 5:
                    gate_products(0)
            dve.wait_ge(ev_["cq_hi"], 1)
            dve.tensor_tensor(CL, CQ[:, :, :], CH.bitcast(F32), ALU.subtract).then_inc(ev_["cq_lo"], 1)
            dve.wait_ge(ev_["cq_lo"], 1)
            for d in range(2):
                dve.wait_ge(ev_["att_out"], d + 1)
                mk = cst("gmask", c2, C2)[:, d * GC:(d + 1) * GC]
                dve.tensor_tensor(AM[:, :, :, :].rearrange("p a b t -> p (a b) t"),
                                  PS[:, 0:2, :].rearrange("p a (b t) -> p (a b) t", t=GC), bc(mk, 16), ALU.mult)\
                    .then_inc(ev_["att_masked"], 1)
                if d == 0:
                    gate_input(1)
                dve.wait_ge(ev_["u_out"], d + 1)
                for n, c in enumerate(ORDER[d][:7]):
                    cp, tt = c % 2, c // 2
                    u = PS[:, 2 + 4 * cp + tt // 2, (tt % 2) * 256:(tt % 2) * 256 + 256].rearrange("p (f t) -> p f t", f=2)
                    if n == 0:
                        mm = dve.tensor_copy(S[:, 1, :, :], u)
                    else:
                        for ft in range(2):
                            mm = dve.scalar_tensor_tensor(out=S[:, n + 1, ft, :], in0=S[:, n, ft, :],
                                                          scalar=tiny[:, 32 + 8 * ft + c:33 + 8 * ft + c], in1=u[:, ft, :],
                                                          op0=ALU.mult, op1=ALU.add)
                    if n < 6:
                        ch.after(mm)
                mm.then_inc(ev_["s_ready"], 1)
                dve.wait_ge(ev_["s_ready"], d + 1)
                if d == 0:
                    gate_sums(1)
                    gate_products(1)
                dve.wait_ge(ev_["og_out"], d + 1)
                for tp in range(2):
                    for cp in range(2):
                        o = OA[:, :, tp * T:(tp + 1) * T].rearrange("p h (t c i) -> p t h c i", t=2, c=2)[:, :, :, cp, :]
                        src = PS[:, 2 * tp + cp, :].rearrange("p (t h i) -> p t h i", t=2, h=4)
                        if d == 0:
                            mm = dve.tensor_copy(o, src)
                        else:
                            mm = dve.tensor_tensor(o, o, src, ALU.add)
                    ch.after(mm)
                    for hp in range(2):
                        o = OA[:, :, tp * T:(tp + 1) * T].rearrange("p (f q) t -> p f q t", q=2)[:, :, hp, :]
                        src = PS[:, 4 + 2 * tp + hp, :].rearrange("p (f t) -> p f t", f=2)
                        mm = dve.tensor_tensor(o, o, src, ALU.add)
                    if tp == 0:
                        ch.after(mm)
                mm.then_inc(ev_["oa_done"], 1)
                dve.wait_ge(ev_["oa_done"], d + 1)
            QN, VM = ml["QN"], ml["VM"]
            for k in range(7):
                if k == 1:
                    dve.wait_ge(ev_["gq_sum"], 1)
                    rs = W[:, 0:4, :]
                    rstd(ch, dve, rs, PS[:, 4:8, :], P)
                    ch.after(dve.tensor_tensor(OA[:, :, :], OA[:, :, :], rs, ALU.mult))
                    dve.scalar_tensor_tensor(out=OA[:, :, :], in0=OA[:, :, :], scalar=vcol("gnorm", 0), in1=ev["RS"][:, :, :],
                                             op0=ALU.mult, op1=ALU.mult).then_inc(ev_["mg_ready"], 1)
                i = Idx(START["uq"] + k)
                dve_ahead(dve, i)
                dve.wait_ge(slab_used, i.base + 1)
                if k < 2:
                    mm = dve.tensor_copy(QN[:, 2 * k:2 * k + 2, :], banks(i, 2 * T))
                elif k == 2:
                    mm = dve.tensor_copy(ml["QR"][:, :, :], banks(i, 2 * T))
                elif k < 5:
                    mm = dve.tensor_copy(ml["KN"][:, 2 * (k - 3):2 * (k - 3) + 2, :], banks(i, 2 * T))
                else:
                    mm = dve.tensor_copy(VM[:, :, 256 * (k - 5):256 * (k - 4)],
                                         banks(i, 512).rearrange("p a (b n) -> p (a b) n", b=2))
                mm.then_inc(drained[i.par], 1)
            dve.wait_ge(ev_["mg_hi"], 1)
            ch.after(dve.tensor_tensor(xl[:, 0:4, :], OA[:, :, :], xh[:, 0:4, :].bitcast(F32), ALU.subtract))
            dve.wait_ge(ev_["rm_out"], 1)
            cs = cst("ropeM", c2, C2)
            CT, ST = cs[:, 0:T], cs[:, T:2 * T]
            LK, PR, QR = ev["LK"], ml["PR"], ml["QR"]
            rq, rk = PR[:, 0, :].rearrange("p (c t) -> p c t", c=2), PR[:, 1, 0:T]
            dve.tensor_tensor(rq, PS[:, 4, :].rearrange("p (c t) -> p c t", c=2), bc(ST, 2), ALU.mult)
            dve.tensor_tensor(rk, PS[:, 5, 0:T], ST, ALU.mult)
            dve.tensor_tensor(QR[:, :, 0:T], QR[:, :, 0:T], bc(CT, 2), ALU.mult)
            ch.after(dve.tensor_tensor(LK[:, 1, 0:T], LK[:, 1, 0:T], CT, ALU.mult))
            dve.tensor_tensor(QR[:, :, 0:T], QR[:, :, 0:T], rq, ALU.add)
            dve.tensor_tensor(LK[:, 1, 0:T], LK[:, 1, 0:T], rk, ALU.add).then_inc(ev_["qk2_ready"], 1)
            dve_attend(dve, ch, MLA_UNITS, False, 0, 0, MLA_SCALE, ml["PR"], 4)
            dve_out(dve, ch, 1, 0, "eout")

        def act_out(act, m):
            for i, chunks in last_slabs(m):
                act_ahead(act, i)
                act_squares(act, m, i, chunks)
            act_root(act, NRM[:, 3, 0:WIDTH[m]])

        def dve_out(dve, ch, m, l, name):
            dve.wait_ge(ev_["x_scaled"], m + 1)
            for k in range(4):
                i = Idx(START[name] + k)
                dve_ahead(dve, i)
                dve.wait_ge(slab_used, i.base + 1)
                for c in range(2):
                    add_residual(dve, m, l, 5, i, 2 * k + c, 2 * i.par + c, c == 1)
            post_norm(dve, ch, m)

        def act_odd(act, ch):
            act.wait_ge(ev_["x_chunk"], 4 * KT + 1)
            act.dma_start(od["nmask"][:, :], a["nmask"]).then_inc(ev_["c3_in"], 16)
            act.dma_start(od["RPB"][:, :, :, :], a["rpb"]).then_inc(ev_["c3_in"], 16)
            act_modulate(act, 4)
            for k in range(12):
                act_ahead(act, Idx(START["odd"] + k))
            act_attend(act, NA_UNITS, True, 16, 8, 1.0, od["NP"], od["NPT"], 0)
            act_out(act, 4)

        def pe_odd(pe):
            for k in range(12):
                i = Idx(START["odd"] + k)
                if k < 8:
                    dense(pe, i, 2, KT, xh, xl, 0, T if k < 4 else 2 * T, None if k else 4)
                else:
                    token_major(pe, i, 4, 256, xh, xl, KT)
            last_pair(pe, Idx(START["odd"] + 11))
            pe.wait_ge(ev_["qkv_ready"], 1)

            def qk(h, q0, k0, k1):
                r = slice((h % 2) * HD, (h % 2) * HD + HD)
                return [(od["NQ"][r, h // 2, q0:q0 + P], od["NK"][r, h // 2, k0:k1])]
            pe_attend(pe, NA_UNITS, True, 16, 8, qk, None, lambda h, tt: od["NV"][:, tt, h * HD:(h + 1) * HD], od["NP"], od["NPT"])
            pe.wait_ge(ev_["flo"], 16)
            for k in range(4):
                dense(pe, Idx(START["oout"] + k), 2, KT, xh, xl, 0, T)
            pe_sums(pe, 4)

        def dve_odd(dve, ch):
            for k in range(12):
                i = Idx(START["odd"] + k)
                dve_ahead(dve, i)
                dve.wait_ge(slab_used, i.base + 1)
                if k < 4:
                    mm = dve.tensor_scalar(od["NQ"][:, 2 * k:2 * k + 2, :], banks(i, T), HD ** -0.5, None, ALU.mult)
                elif k < 8:
                    mm = dve.tensor_copy(od["NK"][:, 2 * (k - 4):2 * (k - 4) + 2, :], banks(i, 2 * T))
                else:
                    mm = dve.tensor_copy(od["NV"][:, :, 256 * (k - 8):256 * (k - 7)],
                                         banks(i, 512).rearrange("p a (b n) -> p (a b) n", b=2))
                mm.then_inc(drained[i.par], 1)
            dve.wait_ge(ev_["c3_in"], 32)
            rp = od["RPB"][:, :, :, :].rearrange("p h d c -> p (h d) c")
            dve.tensor_tensor(rp, rp, bc(od["nmask"][:, :], 112), ALU.add).then_inc(ev_["qkv_ready"], 1)
            dve.wait_ge(ev_["qkv_ready"], 1)
            dve_attend(dve, ch, NA_UNITS, True, 16, 8, 1.0, od["NP"], 0)
            dve_out(dve, ch, 4, 1, "oout")

        def scalar_block2(act, ch):
            for m in range(6):
                if UPTO > 3:
                    act_ffn(act, m) if m in FFN_STAGES else (act_even if m == 1 else act_odd)(act, ch)

        def tensor_block2(pe):
            for m in range(6):
                if UPTO > 3:
                    pe_ffn(pe, m) if m in FFN_STAGES else (pe_even if m == 1 else pe_odd)(pe)

        def vector_block2(dve, ch):
            for m in range(6):
                if UPTO > 3:
                    dve_ffn(dve, ch, m) if m in FFN_STAGES else (dve_even if m == 1 else dve_odd)(dve, ch)

        @block.gpsimd
        def _(pool):
            ch = Chain(pool, sig("pool_step"))
            M, W2, DU, UP = b1["MIX"], b1["W2"], b1["DU"], b1["UP"]
            pool.memset(TR[:, :], 0.0).then_inc(ev_["cr_zero"], 1)
            pool.memset(DU[:, :, 0:16], 0.0)
            ch.after(pool.memset(UP[:, :, 0:2], 0.0))
            for l in range(DEPTH if UPTO > 1 else 1):
                s0 = START[f"layer{l}"]

                def copied(k):
                    d = BANKED[s0 + PLAN.index(("in", k))]
                    pool.wait_ge(drained[d % 2], d // 2 + 1)

                for pos, (kind, n) in enumerate(PLAN):
                    if splitter(s0 + pos) == "pool":
                        split_lo(pool, Idx(s0 + pos), SLAB, "pool")
                    if l == 0 and (kind, n) == ("ada", 7):
                        pool.wait_ge(consts_in, 2 * 16)
                        pool.wait_ge(ev_["late_in"], 2 * 16)
                    if (kind, n) == ("ada", 9):
                        copied(8)
                        copied(9)
                        ch.after(pool.tensor_tensor(UP[:, :, 2:], b1["CC"][:, :, :], b1["CX"][:, :, :], ALU.mult))
                        tap = b1["CX"]
                        for c in range(2):
                            y = M[:, 4 + c, :]
                            ch.after(pool.tensor_scalar(y, UP[:, c, 0:T], vcol("conv", l * 6 + c), None, ALU.mult))
                            for j in (1, 2):
                                ch.after(pool.tensor_scalar(tap[:, c, :], UP[:, c, j:j + T], vcol("conv", l * 6 + 2 * j + c), None, ALU.mult))
                                ch.after(pool.tensor_tensor(y, y, tap[:, c, :], ALU.add))
                    if (kind, n) == ("ada", 10):
                        copied(10)
                        ch.after(pool.tensor_tensor(W2[:, :, 1:], DU[:, :, 1:], DU[:, :, 0:15 + T], ALU.add))
                        pm, inv = b1["CC"], ccol("invc").rearrange("p (c t) -> p c t", c=2)
                        lo, hi = slice(0, HD), slice(HD, P)
                        a4 = M[:, 0:3, :].rearrange("p c t -> p (c t)")[:, 0:2 * (T + 16)].rearrange("p (c t) -> p c t", c=2)
                        a8 = CXF[:, 0:T + 16]
                        ch.after(pool.tensor_tensor(pm[lo, 0, :], W2[lo, 0, 16:], inv[lo, 0, :], ALU.mult))
                        ch.after(pool.tensor_tensor(a4[:, :, 3:], W2[:, :, 3:], W2[:, :, 1:14 + T], ALU.add))
                        ch.after(pool.tensor_tensor(pm[hi, 0, :], a4[hi, 0, 16:], inv[hi, 0, :], ALU.mult))
                        ch.after(pool.tensor_tensor(a8[:, 7:], a4[:, 1, 7:], a4[:, 1, 3:12 + T], ALU.add))
                        ch.after(pool.tensor_tensor(pm[lo, 1, :], a8[lo, 16:], inv[lo, 1, :], ALU.mult))
                        ch.after(pool.tensor_tensor(W2[:, 1, 16:], a8[:, 16:], a8[:, 8:8 + T], ALU.add))
                        ch.after(pool.tensor_tensor(pm[hi, 1, :], W2[hi, 1, 16:], inv[hi, 1, :], ALU.mult))
                        pool.tensor_tensor(W2[:, :, 16:], pm[:, :, :], DU[:, :, 16:], ALU.subtract).then_inc(ev_["pool_in"], 1)
                    if (kind, n) == ("ada", 13):
                        copied(11)
                        pool.tensor_tensor(M[:, 4:6, :], M[:, 4:6, :], b1["CB"][:, :, :], ALU.mult).then_inc(ev_["conv_done"], 1)
            if UPTO > 3:
                for m in range(6):
                    pool_modulate(pool, m)
                    pool_stats(pool, ch, m, last_slabs(m))

        @block.scalar
        def _(act):
            ch = Chain(act, act_step)
            act.dma_start(X[:, :, 0:T], a["x"]).then_inc(acts_in, 16)
            for dst, src in ((const, "const"), (vec, "vec")):
                act.dma_start(dst[:, :], a[src]).then_inc(consts_in, 16)

            def softmax_exp(l, u):
                n = keys_of(u)
                act.wait_ge(ev_["soft_max"], l * UN + u + 1)
                for g in range(4):
                    m = act.activation(b1["SM"][:, u % 2, g, 0:n], b1["SM"][:, u % 2, g, 0:n], ACT.Exp,
                                       bias=tiny[:, 8 * (u % 2) + g:8 * (u % 2) + g + 1],
                                       accum_out=tiny[:, 16 + 8 * (u % 2) + g:17 + 8 * (u % 2) + g])
                m.then_inc(ev_["exp_done"], 1)

            def block1(l):
                if l:
                    act.wait_ge(ev_["x_ready"], l)
                else:
                    act.wait_ge(acts_in, 16)
                act.activation(b1["MIX"][:, :, :], X[:, :, 0:T], ACT.Square).then_inc(ev_["sq_ready"], 1)
                if l == 0:
                    act.wait_ge(consts_in, 2 * 16)
                    o = VEC["c"][0]
                    act.activation(sc[:, :, :], vec[:, o:o + 2 * KT].rearrange("p (k b) -> p k b", b=2), ACT.Silu)\
                        .then_inc(ev_["sc_ready"], 1)
                    act.wait_ge(ev_["sc_ready"], 1)
                    act.wait_ge(ev_["cr_zero"], 1)
                    ch.after(act.activation(CR[:, :, :, :].rearrange("p a k n -> p (a k n)").rearrange("p (a n) -> p a n", a=4),
                                            bc(TR[:, :], 4), ACT.Copy))
                    act.activation(CR[:, 0, :, 0:2], sc[:, :, :], ACT.Copy)
                    act.activation(CR[:, 1, :, 64:66], sc[:, :, :], ACT.Copy).then_inc(ev_["sc_ready"], 1)
                    for b in range(2):
                        split_hi(act, Idx(b), SIZE[b])
                act_root(act, tiny3[:, :])
                act.wait_ge(ev_["rms_out"], 2 * l + 1)
                act.activation(xh[:, :, 0:T], b1["MIX"][:, :, :], ACT.Copy).then_inc(ev_["xm_written"], 1)
                s0 = START[f"layer{l}"]

                def ada_step(pos, a_):
                    act_ahead(act, Idx(s0 + pos))
                    if a_ % 4 == 3:
                        g = 9 * l + a_ // 4
                        act.wait_ge(slab_used, s0 + pos + 1)
                        if g:
                            act.wait_ge(ev_["mod_cols"], g)
                        act.activation(TR[:, :], PS[:, 7, :], ACT.Copy).then_inc(ev_["tr_ready"], 1)

                for pos, (kind, k) in enumerate(PLAN[:UNIT_ADA[-1][0][0]]):
                    i = Idx(s0 + pos)
                    if kind != "in":
                        ada_step(pos, k) if kind == "ada" else act_ahead(act, i)
                        continue
                    act_ahead(act, i)
                    if l == 0 and k == 1:
                        act.dma_start(c1[:, :], a["c1"]).then_inc(ev_["late_in"], 16)
                        act.dma_start(sml[:, :], a["sml"]).then_inc(ev_["late_in"], 16)
                    if l == 0 and k == 8:
                        act.dma_start(X[:, :, T:2 * T], a["ctx"]).then_inc(ev_["ctx_in"], 16)
                    if k == 7:
                        act.wait_ge(ev_["gates_e"], 2 * l + 1)
                        act.activation(tiny[:, 64:88], tiny[:, 64:88], ACT.Exp, scale=-1.0).then_inc(ev_["gates_e"], 1)
                    if k in IDX_AT:
                        blk = IDX_AT.index(k)
                        n = P * (blk + 1)
                        act.wait_ge(ev_["idx_scores_out"], 2 * l + blk + 1)
                        if blk:
                            act.wait_ge(ev_["idx_used"], 2 * l + 1)
                        for hg in range(2):
                            m = act.activation(SMF.rearrange("p (h b t) -> p b h t", h=2, b=4)[:, :, hg, 0:n],
                                               PS[:, 2:6, hg * T:hg * T + n], ACT.Relu)
                        m.then_inc(ev_["idx_relu"], 1)
                    if k >= 12:
                        act.wait_ge(slab_used, i.base + 1)
                        act.activation(b1["SG"][:, 2 * (k - 12):2 * (k - 12) + 2, :], bank(i), ACT.Silu)\
                            .then_inc(drained[i.par], 1)
                softmax_exp(l, 0)
                for step in UNIT_ADA[-1]:
                    ada_step(*step)
                for u in range(UN):
                    if u + 1 < UN:
                        softmax_exp(l, u + 1)
                    act.wait_ge(ev_["pt_ready"], l * UN + u + 1)
                    if u >= 2:
                        act.wait_ge(ev_["pv_done"], l * UN + u - 1)
                    kind, blk = UNITS[u]
                    if kind == "C":
                        m = act.activation(b1["PT"][0:NCMP, u % 2, 0, :], PS[0:NCMP, 0, :], ACT.Copy)
                    else:
                        m = act.activation(b1["PT"][:, u % 2, 0:blk + 1, :], PS[:, 0:1 + blk, :], ACT.Copy)
                    m.then_inc(ev_["pt_copied"], 1)
                    for step in UNIT_ADA[u]:
                        ada_step(*step)
                act.wait_ge(ev_["o_taken"], 4 * l + 4)
                act.activation(xh[:, :, 0:T], b1["MIX"][:, :, :], ACT.Copy).then_inc(ev_["mixh_done"], 1)
                for k in range(4):
                    act_ahead(act, Idx(s0 + PLAN.index(("out", k))))

            for l in range(DEPTH):
                if UPTO >= 1 + l:
                    block1(l)
            if UPTO >= 3:
                act.wait_ge(ev_["x_ready"], DEPTH)
                act.activation(b1["MIX"][:, :, :], X[:, :, 0:T], ACT.Square).then_inc(ev_["sq_ready"], 1)
                act_root(act, tiny3[:, :])
            scalar_block2(act, ch)

        def turn_group(pe, l, g):
            pe.wait_ge(ev_["tr_ready"], 9 * l + g + 1)
            o, _ = CONST["pairsum"]
            for c in range(4):
                out = PS[:, 6, 64 * g + 4 * c:64 * g + 4 * c + 4] if g < 3 else PS[:, 7, 4 * c:4 * c + 4]
                m = pe.matmul(out, TR[:, c * P:(c + 1) * P], const[:, o:o + 4], start=True, stop=True)
            m.then_inc(ev_["mod_cols"], 1)

        def ada_slab(pe, l, pos, n):
            i = Idx(START[f"layer{l}"] + pos)
            g, j = n // 4, n % 4
            if j == 0:
                if g:
                    turn_group(pe, l, g - 1)
                if 9 * l + g:
                    pe.wait_ge(ev_["mod_read"], 9 * l + g)
            wait_split(pe, i)
            for k in range(KT):
                for x, w in enumerate((high(i), low(i))):
                    m = pe.matmul(PS[:, 7, (j // 2) * 256:(j // 2) * 256 + 256], CR[:, j % 2, k, :], w[:, k * 256:(k + 1) * 256],
                                  start=j % 2 == 0 and k == 0 and x == 0, stop=j % 2 == 1 and k == KT - 1 and x == 1)
            m.then_inc(slab_used, 1)

        @block.tensor
        def _(pe):
            pe.wait_ge(consts_in, 2 * 16)
            pe.wait_ge(ev_["sc_ready"], 2)

            def scores(l, u):
                kind, blk = UNITS[u]
                if u >= 2:
                    pe.wait_ge(ev_["soft_max"], l * UN + u - 1)
                q = {"A": 0}.get(kind, 3)
                for g in range(4):
                    h = (g % 2) * 2 + g // 2
                    r = slice((h % 2) * HD, (h % 2) * HD + HD)
                    lhs = b1["QK"][r, q + h // 2, blk * P:(blk + 1) * P]
                    if kind == "C":
                        rhs = b1["KC"][r, 0, 0:NCMP]
                    else:
                        rhs = b1["QK"][r, {"A": 2, "S": 5, "W": 6}[kind], 0:keys_of(u)]
                    o = (h // 2) * T
                    m = pe.matmul(PS[:, 2 + (u % 2) * 2 + h % 2, o:o + keys_of(u)], lhs, rhs, start=True, stop=True)
                m.then_inc(ev_["scores_out"], 1)

            def compress(l, i, s):
                pe.wait_ge(ev_["idx_relu"], 2 * l + 2)
                pe.wait_ge(ev_["blk_ready"], l + 1)
                pe.wait_ge(slab_full[i.slot], 16 * (i.base // RING + 1))
                for half in range(2):
                    r = slice(half * HD, half * HD + HD)
                    for j in range(16):
                        m = pe.matmul(PS[:, 2 + half, 0:16], raw[r, i.slot, j * P:(j + 1) * P], BLK[r, :, s * 16 + j],
                                      start=s == 0 and j == 0, stop=s == 1 and j == 15)
                m.then_inc(slab_used, 1)

            def token_one(pe, i, n):
                slab_begin(pe, i)
                for tt in range(2):
                    for k in range(KT):
                        for j, (x, w) in enumerate(((xh, high(i)), (xh, low(i)), (xl, high(i)))):
                            m = pe.matmul(PS[:, i.par, tt * 256:tt * 256 + n], x[:, k, tt * P:(tt + 1) * P],
                                          w[:, k * n:(k + 1) * n], start=k == 0 and j == 0, stop=k == KT - 1 and j == 2)
                m.then_inc(slab_used, 1)

            def block1(l):
                pe.wait_ge(ev_["rms_in"], l + 1)
                pe.matmul(PS[:, 4, 0:T], ones, tiny2[:, :], start=True, stop=True).then_inc(ev_["rms_sum"], 1)
                s0 = START[f"layer{l}"]
                pe.wait_ge(ev_["rms_out"], 2 * l + 2)
                perm = (cst("permI"), cst("permA"))
                for pos, (kind, k) in enumerate(PLAN[:UNIT_ADA[-1][0][0]]):
                    i = Idx(s0 + pos)
                    if kind == "ada":
                        if (l, k) == (0, 0):
                            pe.wait_ge(ev_["sc_lo"], 1)
                        ada_slab(pe, l, pos, k)
                        continue
                    if kind == "cmp":
                        compress(l, i, k)
                        continue
                    if k == 5 or k == 6:
                        token_one(pe, i, 256 if k == 5 else 148)
                    else:
                        dense_one(pe, i, 1 if k == 7 else 2)
                    if k == 2:
                        for par in range(2):
                            pe.wait_ge(drained[par], (i.d - 2 + par) // 2 + 1)
                        pe.matmul(PS[:, 2, :], perm[0], b1["QI"][:, 0:2, :], start=True, stop=True)
                        pe.matmul(PS[:, 3, 0:T], perm[0], b1["QI"][:, 2, :], start=True, stop=True).then_inc(ev_["perms_done"], 1)
                    if k == 5:
                        pe.wait_ge(drained[1 - i.par], (i.d - 1) // 2 + 1)
                        pe.wait_ge(drained[i.par], (i.d - 2) // 2 + 1)
                        pe.wait_ge(ev_["roped"], 2 * l + 1)
                        for j in range(3):
                            pe.matmul(PS[:, 2 + j, :], perm[1], b1["QK"][:, 2 * j:2 * j + 2, :], start=True, stop=True)
                        pe.matmul(PS[:, 5, 0:T], perm[1], b1["QK"][:, 6, :], start=True, stop=True).then_inc(ev_["perms_done"], 1)
                    if k + 1 in IDX_AT:
                        blk = IDX_AT.index(k + 1)
                        pe.wait_ge(ev_["roped"], 2 * l + 2)
                        if blk:
                            pe.wait_ge(ev_["idx_relu"], 2 * l + 1)
                        for h in range(8):
                            r = slice((h % 4) * 32, (h % 4) * 32 + 32)
                            m = pe.matmul(PS[:, 2 + h % 4, (h // 4) * T:(h // 4) * T + P * (blk + 1)],
                                          b1["QI"][r, h // 4, blk * P:(blk + 1) * P], b1["QI"][r, 2, 0:P * (blk + 1)],
                                          start=True, stop=True)
                        m.then_inc(ev_["idx_scores_out"], 1)
                    if k == 14:
                        pe.wait_ge(ev_["kc_raw"], l + 1)
                        pe.matmul(PS[:, 4, 0:NCMP], perm[1], b1["KC"][:, 0, 0:NCMP], start=True, stop=True)
                        pe.transpose(PS[0:16, 4, P:2 * P], b1["KC"][:, 1, :], ident).then_inc(ev_["perms_done"], 1)
                last_pair(pe, Idx(s0 + PLAN.index(("in", IN_N - 1))))
                pe.wait_ge(ev_["mod_read"], 9 * l + 3)
                pe.wait_ge(ev_["late_in"], 2 * 16)
                pe.wait_ge(ev_["pool_in"], l + 1)
                for c in range(2):
                    o, _ = SML["poolw"]
                    m = pe.matmul(PS[:, 6, c * T:(c + 1) * T], sml[:, o + (2 * l + c) * P:o + (2 * l + c + 1) * P],
                                  b1["W2"][:, c, 16:16 + T], start=True, stop=True)
                m.then_inc(ev_["pool_out"], 1)
                pe.wait_ge(ev_["kc_ready"], l + 1)
                scores(l, 0)
                scores(l, 1)
                for step in UNIT_ADA[-1]:
                    ada_slab(pe, l, *step)
                for u in range(UN):
                    kind, blk = UNITS[u]
                    pe.wait_ge(ev_["p_ready"], l * UN + u + 1)
                    if u:
                        pe.wait_ge(ev_["pt_copied"], l * UN + u)
                    for kt in range(1 if kind == "C" else blk + 1):
                        n = NCMP if kind == "C" else P
                        for g in range(4):
                            h = (g % 2) * 2 + g // 2
                            m = pe.transpose(PS[0:n, kt, h * P:(h + 1) * P],
                                             b1["SM"][:, u % 2, (h % 2) * 2 + h // 2, kt * P:kt * P + n], ident)
                    m.then_inc(ev_["pt_ready"], 1)
                    if u + 2 < UN:
                        scores(l, u + 2)
                    for step in UNIT_ADA[u]:
                        ada_slab(pe, l, *step)
                    pe.wait_ge(ev_["pt_copied"], l * UN + u + 1)
                    if kind in "AS":
                        n_taken = {0: 0, 3: 1, 4: 2, 7: 3}[u]
                        pe.wait_ge(ev_["o_taken"], 4 * l + n_taken) if 4 * l + n_taken else None
                        if u == 0:
                            pe.wait_ge(ev_["pool_out"], 2 * l + 2)
                    if kind == "C":
                        m = pe.matmul(PS[:, 6, :], b1["VC"][0:NCMP, :], b1["PT"][0:NCMP, u % 2, 0, :], start=False, stop=True)
                    else:
                        for kt in range(blk + 1):
                            v = {"A": b1["VT"][:, kt, 0:P], "S": b1["VT"][:, kt, P:2 * P], "W": b1["VW"][:, kt, 0:P]}[kind]
                            m = pe.matmul(PS[:, 6, :], v, b1["PT"][:, u % 2, kt, :], start=kt == 0 and kind in "AS",
                                          stop=kt == blk and kind == "A")
                    m.then_inc(ev_["pv_done"], 1)
                turn_group(pe, l, 8)
                pe.wait_ge(ev_["mixl_done"], l + 1)
                for k in range(4):
                    dense_one(pe, Idx(s0 + PLAN.index(("out", k))))

            for l in range(DEPTH):
                if UPTO >= 1 + l:
                    block1(l)
            if UPTO >= 3:
                pe.wait_ge(ev_["rms_in"], 3)
                pe.matmul(PS[:, 4, 0:T], ones, tiny2[:, :], start=True, stop=True).then_inc(ev_["rms_sum"], 1)
            tensor_block2(pe)

        @block.vector
        def _(dve):
            ch = Chain(dve, dve_step)
            M, W2, DU = b1["MIX"], b1["W2"], b1["DU"]

            def rms(l):
                dve.wait_ge(ev_["sq_ready"], l + 1)
                dve.tensor_reduce(tiny2[:, :], M[:, :, :].rearrange("p k t -> p t k"), AX, ALU.add)\
                    .then_inc(ev_["rms_in"], 1)
                dve.wait_ge(ev_["rms_sum"], l + 1)
                rstd(ch, dve, tiny3[:, :], PS[:, 4, 0:T], D)

            def soft1(l, u):
                kind, blk = UNITS[u]
                n = keys_of(u)
                dve.wait_ge(ev_["scores_out"], l * UN + u + 1)
                if kind == "A":
                    bias = b1["AB"][:, 0:P] if blk == 0 else b1["AB"][:, P:]
                elif kind == "C":
                    bias = ccol("cmpm")[:, 16 * blk:16 * blk + NCMP]
                else:
                    bias = ccol("tri")[:, P:2 * P] if blk == 0 else ccol("tri")
                if u >= 2:
                    dve.wait_ge(ev_["pt_ready"], l * UN + u - 1)
                s = b1["SM"][:, u % 2, :, 0:n]
                src = PS[:, 2 + (u % 2) * 2:4 + (u % 2) * 2, :].rearrange("p a (b t) -> p (a b) t", b=2)[:, :, 0:n]
                ch.after(dve.scalar_tensor_tensor(out=s, in0=src, scalar=HD ** -0.5, in1=bc(bias, 4), op0=ALU.mult, op1=ALU.add))
                nm = tiny[:, 8 * (u % 2):8 * (u % 2) + 4]
                ch.after(dve.tensor_reduce(nm, s, AX, ALU.max, negate=True))
                dve.tensor_scalar(nm, nm, FLOOR, None, ALU.min).then_inc(ev_["soft_max"], 1)

            def soft2(l, u):
                kind, blk = UNITS[u]
                n = keys_of(u)
                dve.wait_ge(ev_["exp_done"], l * UN + u + 1)
                r = tiny[:, 32 + 8 * (u % 2):36 + 8 * (u % 2)]
                ch.after(dve.tensor_scalar(r, tiny[:, 16 + 8 * (u % 2):20 + 8 * (u % 2)], 1e-30, None, ALU.max))
                ch.after(dve.reciprocal(r, r))
                if kind != "A":
                    o = 96 + 12 * blk + 4 * "CSW".index(kind)
                    ch.after(dve.tensor_tensor(r, r, tiny[:, o:o + 4], ALU.mult))
                s = b1["SM"][:, u % 2, :, 0:n]
                dve.tensor_tensor(s, s, bl(r, n), ALU.mult).then_inc(ev_["p_ready"], 1)

            def take_o(l, u):
                kind, blk = UNITS[u]
                dve.wait_ge(ev_["pv_done"], l * UN + u + 1)
                c0 = 0 if kind == "A" else 2
                for par in range(2):
                    r = slice(par * HD, par * HD + HD)
                    o = PS[r, 6, :].rearrange("p (c h t) -> p c h t", c=2, h=2)[:, :, par, :]
                    m = dve.tensor_tensor(M[r, c0:c0 + 2, blk * P:(blk + 1) * P], o,
                                          b1["SG"][r, c0:c0 + 2, blk * P:(blk + 1) * P], ALU.mult)
                m.then_inc(ev_["o_taken"], 1)

            def top_sum(l, blk):
                n = P * (blk + 1)
                dve.wait_ge(ev_["idx_relu"], 2 * l + blk + 1)
                s = tiny2[:, 0:n]
                acc = ccol("tri")[:, P:2 * P] if blk == 0 else ccol("tri")
                for h in range(8):
                    ins = dve.scalar_tensor_tensor(out=s, in0=SMF[:, h * T:h * T + n],
                                                   scalar=b1["VW"][:, blk, P + h:P + h + 1], in1=acc, op0=ALU.mult, op1=ALU.add)
                    acc = s
                    if h == 7:
                        ins.then_inc(ev_["idx_used"], 1)
                        dve.wait_ge(ev_["idx_used"], 2 * l + blk + 1)
                    else:
                        ch.after(ins)

            def top_rounds(blk, rounds):
                s = tiny2[:, 0:P * (blk + 1)]
                for r in range(rounds):
                    ch.after(dve.max(tiny[:, 48:56], s))
                    ch.after(dve.match_replace(out=s, in_to_replace=tiny[:, 48:56], in_values=s, imm_value=TAKEN))

            def top_mask(blk):
                s = tiny2[:, 0:P * (blk + 1)]
                ab = b1["AB"][:, 0:P] if blk == 0 else b1["AB"][:, P:]
                tri = ccol("tri")[:, P:2 * P] if blk == 0 else ccol("tri")
                ch.after(dve.tensor_scalar(s, s, TAKEN / 2, -NEG, ALU.is_le, ALU.mult))
                ch.after(dve.scalar_tensor_tensor(out=ab, in0=s, scalar=NEG, in1=tri, op0=ALU.add, op1=ALU.add))

            def rope(l, j):
                t, nch, tab = ((b1["QI"], 3, "ropeI"), (b1["QK"], 7, "ropeA"))[j]
                dve.wait_ge(ev_["perms_done"], 3 * l + j + 1)
                cs = ccol(tab)
                src = PS[:, 2:4, :] if j == 0 else PS[:, 2:6, :]
                src = src.rearrange("p a b -> p (a b)")[:, 0:nch * T].rearrange("p (c t) -> p c t", t=T)
                rt = SMF[:, 0:nch * T].rearrange("p (c t) -> p c t", t=T)
                dve.tensor_tensor(rt, src, bc(cs[:, T:2 * T], nch), ALU.mult)
                ch.after(dve.tensor_tensor(t[:, :, :], t[:, :, :], bc(cs[:, 0:T], nch), ALU.mult))
                dve.tensor_tensor(t[:, :, :], t[:, :, :], rt, ALU.add).then_inc(ev_["roped"], 1)
                dve.wait_ge(ev_["roped"], 2 * l + j + 1)

            def rope_compressed(l):
                dve.wait_ge(ev_["perms_done"], 3 * l + 3)
                cs = ccol("ropeC")
                dve.tensor_copy(b1["VC"][:, :], PS[0:16, 4, P:2 * P])
                ch.after(dve.tensor_tensor(tiny[:, 128:128 + NCMP], PS[:, 4, 0:NCMP], cs[:, 16:16 + NCMP], ALU.mult))
                ch.after(dve.tensor_tensor(b1["KC"][:, 0, 0:NCMP], b1["KC"][:, 0, 0:NCMP], cs[:, 0:NCMP], ALU.mult))
                ch.after(dve.tensor_tensor(b1["KC"][:, 0, 0:NCMP], b1["KC"][:, 0, 0:NCMP], tiny[:, 128:128 + NCMP], ALU.add))
                dve.wait_ge(ev_["gates_e"], 2 * l + 2)
                ch.after(dve.tensor_scalar(tiny[:, 96:120], tiny[:, 64:88], 1.0, None, ALU.add))
                dve.reciprocal(tiny[:, 96:120], tiny[:, 96:120]).then_inc(ev_["kc_ready"], 1)

            def block1(l):
                if l:
                    dve.wait_ge(ev_["x_ready"], l)
                else:
                    dve.wait_ge(acts_in, 16)
                    dve.wait_ge(consts_in, 2 * 16)
                rms(l)
                for k in range(KT):
                    m = dve.scalar_tensor_tensor(out=M[:, k, :], in0=X[:, k, 0:T], scalar=vcol("norm", l * KT + k),
                                                 in1=tiny3[:, :], op0=ALU.mult, op1=ALU.mult)
                m.then_inc(ev_["rms_out"], 1)
                dve.wait_ge(ev_["xm_written"], l + 1)
                dve.tensor_tensor(xl[:, :, 0:T], M[:, :, :], xh[:, :, 0:T].bitcast(F32), ALU.subtract)\
                    .then_inc(ev_["rms_out"], 1)
                s0 = START[f"layer{l}"]
                if l == 0:
                    dve.wait_ge(ev_["sc_ready"], 2)
                    for j, o in enumerate((0, 64)):
                        m = dve.tensor_tensor(CR[:, j, :, o + 2:o + 4], sc[:, :, :], CR[:, j, :, o:o + 2].bitcast(F32), ALU.subtract)
                    m.then_inc(ev_["sc_lo"], 1)
                    for b in range(2):
                        split_lo(dve, Idx(b), SIZE[b])

                def mod_group(g):
                    dve.wait_ge(ev_["mod_cols"], 9 * l + g + 1)
                    o = VEC["adab"][0] + 72 * l + 8 * g
                    out = mod[:, l, :, :, :].rearrange("p j k b -> p (j k) b")[:, 8 * g:8 * g + 8, :]\
                        .rearrange("p (q h c) b -> p q h c b", q=2, h=2)
                    src = PS[:, 6, 64 * g:64 * g + 16] if g < 3 else PS[:, 7, 0:16]
                    for h in range(2):
                        m = dve.tensor_tensor(out[:, :, h, :, :], src.rearrange("p (q c h b) -> p q c h b", q=2, c=2, h=2)[:, :, :, h, :],
                                              bl(vec[:, o:o + 8].rearrange("p (q h c) -> p q h c", q=2, h=2)[:, :, h, :], 2), ALU.add)
                    m.then_inc(ev_["mod_read"], 1)

                def ada_step(pos, a_):
                    dve_ahead(dve, Idx(s0 + pos))
                    if a_ % 4 == 0 and a_:
                        mod_group(a_ // 4 - 1)

                QI, QK = b1["QI"], b1["QK"]
                for pos, (kind, k) in enumerate(PLAN[:UNIT_ADA[-1][0][0]]):
                    i = Idx(s0 + pos)
                    if kind != "in":
                        ada_step(pos, k) if kind == "ada" else dve_ahead(dve, i)
                        continue
                    dve_ahead(dve, i)
                    if k < 12:
                        dve.wait_ge(slab_used, i.base + 1)
                    if k == 0:
                        m = dve.tensor_copy(QI[:, 0:2, :], bank(i))
                    elif k == 1:
                        dve.tensor_copy(QI[:, 2, :], bank(i)[:, 0, :])
                        m = dve.tensor_copy(QK[:, 2, :], bank(i)[:, 1, :])
                    elif k in (2, 3, 4):
                        o = {2: 0, 3: 3, 4: 5}[k]
                        m = dve.tensor_copy(QK[:, o:o + 2, :], bank(i))
                    elif k == 5:
                        m = dve.tensor_copy(b1["VT"][:, :, :], bank(i))
                    elif k == 6:
                        m = dve.tensor_copy(b1["VW"][:, :, :], bank(i)[:, :, 0:148])
                    elif k == 7:
                        m = dve.tensor_copy(KCV, bank(i)[:, 0, :])
                    elif k in (8, 9, 11):
                        m = dve.tensor_copy(b1[{8: "CC", 9: "CX", 11: "CB"}[k]][:, :, :], bank(i))
                    elif k == 10:
                        m = dve.tensor_copy(DU[:, :, 16:16 + T], bank(i))
                    if k < 12:
                        m.then_inc(drained[i.par], 1)
                    if k == 3:
                        if l == 0:
                            dve.wait_ge(ev_["late_in"], 2 * 16)
                        rope(l, 0)
                    if k == 6:
                        dve.wait_ge(drained[i.par], i.d // 2 + 1)
                        dve.tensor_copy(tiny[:, 64:88].rearrange("p (b g) -> p b g", b=2), b1["VW"][:, :, P + 8:P + 20])\
                            .then_inc(ev_["gates_e"], 1)
                        rope(l, 1)
                    if k == 7:
                        dve.wait_ge(drained[i.par], i.d // 2 + 1)
                        o = VEC["pe"][0] + 32 * l
                        for half in range(2):
                            kv = KCV[:, 16 * half:16 * half + 240].rearrange("p (n j) -> p n j", j=16)
                            m = dve.tensor_tensor(BLK[:, 0:NCMP, 16 * half:16 * half + 16], kv,
                                                  bc(vec[:, o + 16 * half:o + 16 * half + 16], NCMP), ALU.add)
                        dve.memset(BLK[:, NCMP:16, :], 0.0).then_inc(ev_["blk_ready"], 1)
                    if k == 10:
                        top_sum(l, 0)
                        top_rounds(0, 4)
                    if k == 11:
                        top_rounds(0, 4)
                        top_mask(0)
                    if k == 12:
                        top_sum(l, 1)
                        top_rounds(1, 2)
                    if k == 13:
                        dve.wait_ge(slab_used, s0 + PLAN.index(("cmp", 1)) + 1)
                        dve.tensor_copy(b1["KC"][:, :, :], PS[:, 2:4, 0:16]).then_inc(ev_["kc_raw"], 1)
                        dve.wait_ge(ev_["kc_raw"], l + 1)
                        top_rounds(1, 3)
                    if k == 14:
                        top_rounds(1, 3)
                        top_mask(1)
                    if k == 15:
                        rope_compressed(l)
                dve.wait_ge(ev_["pool_out"], 2 * l + 1)
                for c in range(2):
                    m = dve.scalar_tensor_tensor(out=M[:, 6 + c, :], in0=PS[:, 6, c * T:(c + 1) * T],
                                                 scalar=vcol("pscale", 2 * l + c), in1=b1["SG"][:, 6 + c, :],
                                                 op0=ALU.mult, op1=ALU.mult)
                m.then_inc(ev_["pool_out"], 1)
                soft1(l, 0)
                soft1(l, 1)
                for step in UNIT_ADA[-1]:
                    ada_step(*step)
                dve.wait_ge(ev_["conv_done"], l + 1)
                ch.after(dve.tensor_tensor(M[:, 4:6, :], M[:, 4:6, :], b1["SG"][:, 4:6, :], ALU.mult))
                for u in range(UN):
                    soft2(l, u)
                    for step in UNIT_ADA[u]:
                        ada_step(*step)
                    if u + 2 < UN:
                        soft1(l, u + 2)
                    if u in (3, 4, 7):
                        take_o(l, u - 1)
                take_o(l, UN - 1)
                dve.wait_ge(ev_["mixh_done"], l + 1)
                dve.tensor_tensor(xl[:, :, 0:T], M[:, :, :], xh[:, :, 0:T].bitcast(F32), ALU.subtract)\
                    .then_inc(ev_["mixl_done"], 1)
                for k in range(4):
                    i = Idx(s0 + PLAN.index(("out", k)))
                    dve_ahead(dve, i)
                    dve.wait_ge(slab_used, i.base + 1)
                    m = dve.tensor_tensor(X[:, 2 * k:2 * k + 2, 0:T], X[:, 2 * k:2 * k + 2, 0:T], bank(i), ALU.add)
                    m.then_inc(drained[i.par], 1)
                for par in range(2):
                    last = i.d - (i.d - par) % 2
                    dve.wait_ge(drained[par], last // 2 + 1)
                mod_group(8)
                dve.wait_ge(ev_["mod_read"], 9 * (l + 1))
                for j in (1, 4, 7):
                    dve.tensor_scalar(mod[:, l, j, :, :], mod[:, l, j, :, :], 1.0, None, ALU.add)
                for j in (2, 8):
                    m = dve.tensor_scalar(mod[:, l, j, :, :], mod[:, l, j, :, :], 0.5, None, ALU.mult)
                m.then_inc(ev_["x_ready"], 1)

            for l in range(DEPTH):
                if UPTO >= 1 + l:
                    block1(l)
            if UPTO >= 3:
                dve.wait_ge(ev_["x_ready"], 2)
                rms(2)
                dve_modulate(dve, 0, lambda k: dve.scalar_tensor_tensor(out=X[:, k, 0:T], in0=X[:, k, 0:T], scalar=vcol("fnorm", k),
                                                                        in1=tiny3[:, :], op0=ALU.mult, op1=ALU.mult))
            vector_block2(dve, ch)


IN_SPLITS = (("a_q", 256), ("a_k", 64), ("a_v", 64), ("a_qi", 256), ("a_ki", 32), ("a_wi", 8), ("a_gate", 256),
             ("b_q", 256), ("b_kc", 64), ("b_vc", 64), ("b_ks", 64), ("b_vs", 64), ("b_kw", 64), ("b_vw", 64),
             ("b_g", 12), ("b_gate", 256), ("c_b", 256), ("c_c", 256), ("c_x", 256), ("c_gate", 256),
             ("d_u", 256), ("d_gate", 256))
EVEN_SPLITS = (("q", 256), ("k", 256), ("v", 512), ("r", 512), ("lf", 16), ("lb", 16), ("cq", 384), ("ckv", 128), ("kr", 64))


def spans(splits):
    at, o = {}, 0
    for name, n in splits:
        at[name] = np.arange(o, o + n)
        o += n
    return at


def rows_by_partition(w, cols):
    w = np.concatenate([w, np.zeros((w.shape[0], 1), w.dtype)], 1)
    return w[:, cols].reshape(-1, P, len(cols)).transpose(1, 0, 2)


def slab(w, *chunks):
    return np.concatenate([rows_by_partition(w, c).reshape(P, -1) for c in chunks], 1)


def by_feature(v):
    return v.reshape(-1, P).T


def rope_tables(pos_angles, head, rot, interleaved=False):
    n = pos_angles.shape[0]
    c, s, perm = np.ones((P, n), np.float32), np.zeros((P, n), np.float32), np.zeros((P, P), np.float32)
    cos, sin = np.cos(pos_angles).astype(np.float32), np.sin(pos_angles).astype(np.float32)
    for p in range(P):
        d = p % head
        if d >= rot:
            continue
        if interleaved:
            f, first, partner = d // 2, d % 2 == 0, p ^ 1
        else:
            half = rot // 2
            f, first, partner = d % half, d < half, p + half if d < half else p - half
        c[p], s[p], perm[partner, p] = cos[:, f], (-sin if first else sin)[:, f], 1.0
    return c, s, perm


def constants():
    t = np.arange(T)
    inv = lambda base, n: (np.float32(base) ** (-np.arange(n, dtype=np.float32) / n)).astype(np.float32)
    ang = lambda pos, f: (pos.astype(np.float32)[:, None] * f[None, :]).astype(np.float32)
    ca, sa, pa = rope_tables(ang(t, inv(500000.0, 8)), 64, 16)
    ci, si, pi = rope_tables(ang(t, inv(500000.0, 4)), 32, 8)
    cc, sc_, _ = rope_tables(ang(np.arange(16) * 16 + 31, inv(500000.0, 8)), 64, 16)
    f = inv(10000.0, 16)
    cm, sm, pm = rope_tables(np.concatenate([ang(t // 64, f), ang(t % 64, f)], 1), 64, 64, True)
    pairsum = np.zeros((P, 4))
    for h in range(2):
        for b in range(2):
            pairsum[[64 * h + b, 64 * h + 2 + b], 2 * h + b] = 1.0
    const = np.concatenate([np.eye(P), np.ones((P, P)), pa, pi, pm, pairsum], 1)
    q = np.arange(P)
    tri = np.concatenate([np.zeros((P, P)), np.where(q[None, :] > q[:, None], NEG, 0.0)], 1)
    cmpm = np.concatenate([np.where((np.arange(16) * 16 + 31)[None, :] <= (q + b * P)[:, None], 0.0, NEG) for b in range(2)], 1)
    win = np.array([[2, 8], [4, 16]])
    invc = np.stack([[1.0 / np.minimum(t + 1, win[p // HD][c]) for c in range(2)] for p in range(P)]).reshape(P, -1)
    c1 = np.concatenate([ca, sa, ci, si, cc, sc_, tri, cmpm, invc], 1)
    j, i = q[:, None] % GC, np.arange(GC)[None, :]
    reset = np.broadcast_to((np.arange(2 * T) % GC != 0), (P, 2 * T))
    c2 = np.concatenate([cm, sm, j <= i, j > i, reset], 1)
    col, key = q[:, None] % 64, np.arange(64)[None, :]
    start = np.clip(col - 8, 0, 48)
    nmask = np.where((key >= start) & (key < start + 16), 0.0, NEG)
    out = {"const": const, "c1": c1, "c2": c2, "nmask": nmask}
    assert const.shape[1] == CONST_N and c1.shape[1] == C1_N and c2.shape[1] == C2_N
    return {n: np.ascontiguousarray(v, dtype=np.float32) for n, v in out.items()}


def pack(x, norm_w, w_in, w_out, conv_w, pe_cmp, w_cmp_k, w_cmp_v, pool_w, pool_scale, final_norm_w,
         c_2, ctx_2, c_ctx_2, ada_w_2, ada_b_2, ffn1_w_in_2, ffn1_w_out_2, ffn2_w_in_2, ffn2_w_out_2,
         even_w_in_2, gla_wg2_f_2, gla_bg_f_2, gla_wg2_b_2, gla_bg_b_2, gla_norm_g_2, mla_q_norm_g_2,
         mla_kv_norm_g_2, mla_w_uq_2, mla_w_ukv_2, even_w_out_2, na_w_in_2, na_rpb_2, na_w_out_2):
    out = {}
    tokens = lambda v: np.ascontiguousarray(v[0].T.reshape(KT, P, T).transpose(1, 0, 2))
    out["x"], out["ctx"] = tokens(x), tokens(ctx_2)
    chunk = lambda idx, n=0: idx[n * P:(n + 1) * P]
    seq = np.arange(D)
    whole = lambda w: np.stack([slab(w, chunk(seq, 2 * n), chunk(seq, 2 * n + 1)) for n in range(4)])
    s = spans(IN_SPLITS)
    dup = lambda n: np.concatenate([s[n], s[n]])
    for l in range(DEPTH):
        w = w_in[l]
        pair = lambda n: slab(w, chunk(s[n]), chunk(s[n], 1))
        va = rows_by_partition(w, np.concatenate([dup("a_v"), dup("b_vs")])).reshape(P, -1)
        g = s["b_g"].reshape(2, 2, 3).transpose(2, 1, 0).reshape(-1)
        tok = lambda w_, c: rows_by_partition(w_, c).reshape(P, -1)
        dense = [pair("a_qi"), slab(w, np.tile(s["a_ki"], 4), dup("a_k")), pair("a_q"), pair("b_q"), slab(w, dup("b_ks"), dup("b_kw")),
                 va, tok(w, np.concatenate([dup("b_vw"), s["a_wi"], g])), slab(w, np.concatenate([s["b_kc"], s["b_vc"]]))]
        dense += [pair(n) for n in ("c_c", "c_x", "d_u", "c_b", "a_gate", "b_gate", "c_gate", "d_gate")]
        cw = np.concatenate([np.tile(v[l].reshape(32, HD, HD), (1, 1, 2)).transpose(1, 0, 2) for v in (w_cmp_k, w_cmp_v)], 0)
        slabs = {"in": dense, "cmp": cw.reshape(P, 2, -1).transpose(1, 0, 2), "out": whole(w_out[l]),
                 "ada": [tok(ada_w_2[l], np.arange(n * 256, n * 256 + 256)) for n in range(ADA_N)]}
        out[f"layer{l}"] = np.stack([np.pad(slabs[kind][n], ((0, 0), (0, SLAB - slabs[kind][n].shape[1]))) for kind, n in PLAN])
    cols = np.arange(DFF)
    for l in range(DEPTH):
        for f, wi, wo in ((1, ffn1_w_in_2[l], ffn1_w_out_2[l]), (2, ffn2_w_in_2[l], ffn2_w_out_2[l])):
            for half in range(2):
                ms = range(half * FH, half * FH + FH)
                out[f"ffi{f}{l}{half}"] = np.stack([slab(wi, chunk(cols, m), chunk(cols, m) + DFF) for m in ms])
                rows = wo[half * FH * P:(half + 1) * FH * P]
                out[f"ffo{f}{l}{half}"] = np.stack([slab(rows, chunk(seq, n)) for n in range(KT)])
    e, w = spans(EVEN_SPLITS), even_w_in_2[0]
    pair = lambda n, a=0: slab(w, chunk(e[n], a), chunk(e[n], a + 1))
    gap = -np.ones(16, int)
    lr = np.concatenate([e["lf"], gap, e["lb"], gap, np.tile(gap, 4)])
    tok = lambda w_, c: rows_by_partition(w_, c).reshape(P, -1)
    out["even"] = np.stack([pair("q"), pair("k"), slab(w, lr, np.tile(e["kr"], 2)), tok(w, e["v"][0:256]), tok(w, e["v"][256:512]),
                            pair("cq"), slab(w, chunk(e["cq"], 2), e["ckv"]), pair("r"), pair("r", 2)])
    uq = np.arange(768).reshape(4, 192)
    nope, rope_ = uq[:, 0:P], uq[:, P:192].reshape(2, P)
    out["uq"] = np.stack([slab(mla_w_uq_2[0], a_, b_) for a_, b_ in ((nope[0], nope[1]), (nope[2], nope[3]), (rope_[0], rope_[1]))])
    kv = np.arange(1024).reshape(4, 256)
    out["ukv"] = np.stack([slab(mla_w_ukv_2[0], kv[0, 0:P], kv[1, 0:P]), slab(mla_w_ukv_2[0], kv[2, 0:P], kv[3, 0:P]),
                           tok(mla_w_ukv_2[0], kv[0:2, P:].reshape(-1)), tok(mla_w_ukv_2[0], kv[2:4, P:].reshape(-1))])
    out["eout"], out["oout"] = whole(even_w_out_2[0]), whole(na_w_out_2[0])
    w = na_w_in_2[0]
    out["odd"] = np.stack([slab(w, seq[2 * n * P:(2 * n + 1) * P] + o, seq[(2 * n + 1) * P:(2 * n + 2) * P] + o)
                           for o in (0, D) for n in range(4)] + [tok(w, seq[256 * n:256 * n + 256] + 2 * D) for n in range(4)])
    shift = np.arange(64)[None, :] - (np.arange(P) % 64)[:, None] + 15
    rp = np.concatenate([na_rpb_2[0], np.zeros((16, 15, 1), na_rpb_2.dtype)], 2)[:, 4:11]
    out["rpb"] = rp[:, :, np.where((shift >= 0) & (shift <= 30), shift, 31)].transpose(2, 0, 1, 3)
    cols_of = [by_feature(norm_w), by_feature(final_norm_w), by_feature(conv_w), by_feature(pool_scale),
               np.concatenate([np.concatenate([pe_cmp[l].T, pe_cmp[l].T], 0) for l in range(DEPTH)], 1),
               by_feature(ada_b_2), np.stack([by_feature(c_2[0]), by_feature(c_ctx_2)], 2).reshape(P, -1),
               by_feature(gla_bg_f_2), by_feature(gla_bg_b_2), by_feature(gla_norm_g_2), by_feature(mla_q_norm_g_2),
               by_feature(mla_kv_norm_g_2)]
    out["vec"] = np.concatenate(cols_of, 1)
    pw = np.zeros((P, DEPTH, 2, P), pool_w.dtype)
    for l in range(DEPTH):
        for g in range(4):
            r = slice((g % 2) * HD, (g % 2) * HD + HD)
            pw[r, l, g // 2, r] = pool_w[l, g]
    wg = np.zeros((P, 2 * P), pool_w.dtype)
    wg[0:16], wg[32:48] = gla_wg2_f_2[0], gla_wg2_b_2[0]
    out["sml"] = np.concatenate([pw.reshape(P, -1), wg], 1)
    out.update(constants())
    return {n: np.ascontiguousarray(v) for n, v in out.items()}


def kernel(**inputs):
    import concourse.bacc as bacc
    from concourse.bass_utils import run_bass_kernel_spmd

    arrays = pack(**{n: np.asarray(v) for n, v in inputs.items()})
    nc = bacc.Bacc("TRN2", target_bir_lowering=False, num_devices=1)
    a = {n: nc.dram_tensor(n + "_dram", v.shape, mybir.dt.from_np(v.dtype), kind="ExternalInput").ap() for n, v in arrays.items()}
    a["out"] = nc.dram_tensor("out_dram", (P, KT, T), F32, kind="ExternalOutput").ap()
    build(nc, a)
    r = run_bass_kernel_spmd(nc, [{n + "_dram": v for n, v in arrays.items()}], core_ids=[0])
    y = r.results[0]["out_dram"]
    return np.ascontiguousarray(y.transpose(1, 0, 2).reshape(D, T).T[None])
```

```python
from contextlib import ExitStack

import numpy as np
import concourse.bass as bass
from concourse import mybir

F32 = mybir.dt.float32
F32R = mybir.dt.float32r
ALU = mybir.AluOpType
ACT = mybir.ActivationFunctionType
AX = mybir.AxisListType.X

P = 128
D = 1024
KT = D // P
T = 256
DEPTH = 2
EPS = 1e-6
HD = 64
DFF = 2816
FH = DFF // P // 2
ALPHA = (2 * DEPTH) ** 0.25
TOPK = T // 4
NCMP = (T - 32) // 16 + 1
GC = 64
MLA_SCALE = 192.0 ** -0.5
NEG = -1e30
FLOOR = 1e29
TAKEN = -3e38

SLAB = 2 * KT * P
RING = 4
IN_N = 16
IDX_AT = [9, 11]
GROUP, GROUPS = 12, 3
ADA_N = 36

def layer_plan():
    plan, a = [], 0
    for k in range(IN_N):
        plan.append(("in", k))
        if k == 12:
            plan += [("cmp", 0), ("cmp", 1)]
        if k:
            plan.append(("ada", a))
            a += 1
    after = {}
    for u in range(-1, 8):
        n = 3 if u < 2 else 2
        after[u] = [(len(plan) + j, a + j) for j in range(n)]
        plan += [("ada", a + j) for j in range(n)]
        a += n
    assert a == ADA_N
    return plan + [("out", k) for k in range(4)], after


PLAN, UNIT_ADA = layer_plan()


def stage_table():
    runs = []
    for l in range(DEPTH):
        runs.append((f"layer{l}", len(PLAN), SLAB))
    for l in range(DEPTH):
        for f in (1, 2):
            if f == 2 and l == 0:
                runs += [("even", 9, 2 * KT * P), ("uq", 3, 6 * P), ("ukv", 4, 2 * P), ("eout", 4, 2 * KT * P)]
            if f == 2 and l == 1:
                runs += [("odd", 12, 2 * KT * P), ("oout", 4, 2 * KT * P)]
            for half in range(2):
                runs += [(f"ffi{f}{l}{half}", FH, 2 * KT * P), (f"ffo{f}{l}{half}", KT, FH * P)]
    return runs


RUNS = stage_table()
START, SIZE, KIND = {}, [], []
for _name, _n, _f in RUNS:
    START[_name] = len(SIZE)
    SIZE += [{"vb": KT * 148}.get(_name, _f)] * _n
    KIND += [kind for kind, _ in PLAN] if _name.startswith("layer") else ["dense"] * _n
for _l in range(DEPTH):
    SIZE[START[f"layer{_l}"] + PLAN.index(("in", 6))] = KT * 148
    SIZE[START[f"layer{_l}"] + PLAN.index(("in", 7))] = KT * P
NSLABS = len(SIZE)


def splitter(b):
    if KIND[b] == "cmp":
        return None
    layer_pos = [b - START[f"layer{l}"] for l in range(DEPTH)]
    if KIND[b] == "ada":
        a = PLAN[layer_pos[1] if layer_pos[1] >= 0 else layer_pos[0]][1]
        return "dve" if a % 2 == 0 and a < IN_N - 1 else "pool"
    return "dve"


def before(test):
    return np.concatenate([[0], np.cumsum([test(b) for b in range(NSLABS)])]).tolist()


FIRST_LEN = START["ffi100"]
BANKED = before(lambda b: KIND[b] not in ("ada", "cmp"))
HI = before(lambda b: KIND[b] != "cmp")
LO = {e: before(lambda b: splitter(b) == e) for e in ("dve", "pool")}

def columns(parts):
    at, o = {}, 0
    for name, n in parts:
        at[name] = (o, n)
        o += n
    return at, o


CONST, CONST_N = columns([("ident", P), ("ones", P), ("permA", P), ("permI", P), ("permM", P), ("pairsum", GROUP)])
C1, C1_N = columns([("ropeA", 2 * T), ("ropeI", 2 * T), ("ropeC", 32), ("tri", T), ("cmpm", 32), ("invc", 2 * T)])
C2, C2_N = columns([("ropeM", 2 * T), ("gmask", 2 * GC), ("reset", 2 * T)])
VEC, VEC_N = columns([("norm", DEPTH * KT), ("fnorm", KT), ("conv", DEPTH * 6), ("pscale", DEPTH * 2), ("pe", DEPTH * 32),
                      ("adab", DEPTH * 72), ("c", 2 * KT), ("bg", 4), ("gnorm", 1), ("qnorm", 3), ("kvnorm", 1)])
SML, SML_N = columns([("poolw", DEPTH * 2 * P), ("wg2", 2 * P)])

class Idx:

    def __init__(self, base, reg=None):
        self.base, self.reg = base, reg

    def __add__(self, n):
        return Idx(self.base + n, self.reg)

    @property
    def slot(self):
        return self.base % RING

    @property
    def d(self):
        return BANKED[self.base]

    @property
    def par(self):
        return self.d % 2

    def count(self, per_group, at_zero):
        return at_zero if self.reg is None else self.reg * per_group + at_zero


def build(nc, a):
    ctx = ExitStack()
    sems = {}

    def sig(name):
        if name not in sems:
            sems[name] = ctx.enter_context(nc.semaphore(name))
        return sems[name]

    with ctx:
        base = [(nc.sbuf_base + 63) // 64 * 64]
        limit = nc.sbuf_usable_end

        def fixed(name, shape, dt=F32):
            n = int(np.prod(shape[1:])) * 4
            t = nc.alloc_sbuf_tensor_at(name, shape, dt, offset=base[0])
            base[0] += (n + 31) // 32 * 32
            return t

        raw_at = base[0]
        raw = fixed("raw", [P, RING, SLAB])
        rest = nc.alloc_sbuf_tensor_at("rest", [P, RING, SLAB], F32R, offset=raw_at)
        wh = fixed("wh", [P, RING, SLAB], F32R)
        X = fixed("X", [P, KT, 2 * T])
        xh = fixed("xh", [P, KT, 2 * T], F32R)
        xl = fixed("xl", [P, KT, 2 * T], F32R)
        const = fixed("const", [P, CONST_N])
        vec = fixed("vec", [P, VEC_N])
        sml = fixed("sml", [P, SML_N])
        mod = fixed("mod", [P, DEPTH, 9, KT, 2])
        sc = fixed("sc", [P, KT, 2])
        tiny = fixed("tiny", [P, 144])
        tiny2 = fixed("tiny2", [P, T])
        tiny3 = fixed("tiny3", [P, T])
        arena0 = base[0]

        def phase(spec):
            out, o = {}, arena0
            for name, shape, *dt in spec:
                n = (int(np.prod(shape[1:])) * 4 + 31) // 32 * 32
                out[name] = nc.alloc_sbuf_tensor_at(name, shape, dt[0] if dt else F32, offset=o)
                o += n
            assert o <= limit, (spec[0][0], o - limit)
            return out

        def cst(name, tab=None, at=None):
            at, tab = at or CONST, tab or const
            o, n = at[name]
            return tab[:, o:o + n]

        def vcol(name, i, n=1):
            o, _ = VEC[name]
            return vec[:, o + i:o + i + n]

        ident, ones = cst("ident"), cst("ones")
        PS = ctx.enter_context(nc.psum_tensor("PS", [P, 8, 512], F32))

        slab_full = [sig(f"slab_full{s}") for s in range(RING)]
        hi_done, slab_used = sig("hi_done"), sig("slab_used")
        lo_done = {"dve": sig("lo_done_dve"), "pool": sig("lo_done_pool")}
        drained = [sig("drained_even"), sig("drained_odd")]
        consts_in, acts_in = sig("consts_in"), sig("acts_in")
        out_stored = sig("out_stored")
        dve_step, act_step = sig("dve_step"), sig("act_step")
        b1 = phase([("CR", [P, KT, 2 * P], F32R), ("TR", [P, 512]), ("c1", [P, C1_N]), ("MIX", [P, 8, T]), ("SM", [P, 2, 4, T]),
                    ("QK", [P, 7, T]), ("QI", [P, 3, T]), ("PT", [P, 2, 2, 512]), ("AB", [P, P + T]), ("CC", [P, 2, T]), ("CX", [P, 2, T]), ("CB", [P, 2, T]),
                    ("DU", [P, 2, 16 + T]), ("SG", [P, 8, T]), ("VT", [P, 2, T]), ("VW", [P, 2, 148]),
                    ("KC", [P, 2, 16]), ("VC", [16, P]), ("UP", [P, 2, 2 + T]), ("W2", [P, 2, 16 + T])])
        ff = phase([("HH", [P, FH, 2 * T], F32R), ("HL", [P, FH, 2 * T], F32R), ("SQ", [P, KT, 2 * T]),
                    ("HF", [P, 2, 2 * T]), ("SI", [P, 2, 2 * T]), ("NRM", [P, 4, 2 * T])])
        ev = phase([("c2", [P, C2_N]), ("Q", [P, 2, 2 * T]), ("K", [P, 2, 2 * T]), ("LK", [P, 2, 2 * T]),
                    ("V", [P, 4, 512]), ("CQ", [P, 4, 2 * T]), ("RS", [P, 4, 2 * T]),
                    ("W", [P, 12, 2 * T]), ("KDT", [P, 2, 4, P]), ("S", [P, 8, 2, P]),
                    ("OA", [P, 4, 2 * T])])
        ml = phase([("c2_", [P, C2_N]), ("PR", [P, 2, 512]), ("K_", [P, 2, 2 * T]), ("LK_", [P, 2, 2 * T]),
                    ("PTM", [P, 2, 512]), ("V_", [P, 2, 512]), ("CQ_", [P, 4, 2 * T]),
                    ("RS_", [P, 4, 2 * T]), ("SQ_", [P, 4, 2 * T]), ("QN", [P, 4, 2 * T]),
                    ("QR", [P, 2, 2 * T]), ("KN", [P, 4, 2 * T]), ("VM", [P, 4, 512])])
        od = phase([("nmask", [P, 64]), ("RPB", [P, 16, 7, 64]), ("NQ", [P, 8, T]), ("NK", [P, 8, 2 * T]),
                    ("NV", [P, 4, 1024]), ("NP", [P, 2, 512]), ("NPT", [P, 2, 512])])

        def turns_of(name):
            n = next(r[1] for r in RUNS if r[0] == name)
            turns = (n - (START[name] + n == NSLABS)) // 4
            return turns if turns >= 2 else 0

        def runs_of(eng, name, step):
            s0, n = START[name], dict((r[0], r[1]) for r in RUNS)[name]
            turns = turns_of(name)
            if turns:
                with eng.Fori(0, turns) as it:
                    for u in range(4):
                        step(Idx(s0 + u, it), it * 4 + u)
            for k in range(4 * turns, n):
                step(Idx(s0 + k), k)

        def width(i, after):
            turns = 1
            if i.reg is not None:
                turns = next(turns_of(name) for name, n, _ in RUNS if START[name] <= i.base < START[name] + n)
            return max([SIZE[n] for n in range(i.base + after, i.base + after + 4 * turns, 4) if n < NSLABS], default=0)

        def high(i):
            return wh[:, i.slot if i.base < FIRST_LEN else i.base % 2, :]

        def low(i):
            return rest[:, i.slot, :] if i.base < FIRST_LEN else wh[:, 2 + i.base % 2, :]

        def split_hi(act, i, n):
            act.wait_ge(slab_full[i.slot], i.count(16, 16 * (i.base // RING + 1)))
            if i.base >= FIRST_LEN:
                act.wait_ge(slab_used, i.count(4, i.base - 1))
            act.activation(high(i)[:, 0:n], raw[:, i.slot, 0:n], ACT.Copy).then_inc(hi_done, 1)

        def split_lo(eng, i, n, who="dve"):
            eng.wait_ge(hi_done, i.count(4, HI[i.base] + 1))
            eng.tensor_tensor(low(i)[:, 0:n], raw[:, i.slot, 0:n], high(i)[:, 0:n].bitcast(F32),
                              ALU.subtract).then_inc(lo_done[who], 1)

        def next_split(i):
            if i.base + 2 < FIRST_LEN:
                return 2 if KIND[i.base + 2] != "cmp" else 0
            return 1 if i.base + 1 >= FIRST_LEN and width(i, 1) else 0

        def act_ahead(act, i):
            n = next_split(i)
            if n:
                split_hi(act, i + n, width(i, n))

        def dve_ahead(dve, i):
            n = next_split(i)
            if n and splitter(i.base + n) == "dve":
                split_lo(dve, i + n, width(i, n))

        def wait_split(pe, i):
            who = splitter(i.base)
            pe.wait_ge(lo_done[who], i.count(4, LO[who][i.base] + 1))

        def slab_begin(pe, i):
            wait_split(pe, i)
            if i.d >= 2:
                pe.wait_ge(drained[i.par], i.count(2, i.d // 2))

        def product(pe, out, i, tiles, rows=slice(0, P), ready=None):
            hi, rest_ = high(i), low(i)
            for n, (o, h, lo) in enumerate(tiles):
                if ready is not None:
                    pe.wait_ge(ready[0], ready[1] + n + 1)
                for j, (w, x) in enumerate(((hi, h), (hi, lo), (rest_, h))):
                    m = pe.matmul(out, w[rows, o:o + P], x, start=n == 0 and j == 0,
                                  stop=n == len(tiles) - 1 and j == 2)
            return m

        def dense(pe, i, chunks, kts, xhi, xlo, c0, c1_, ready=None):
            slab_begin(pe, i)
            for c in range(chunks):
                m = product(pe, PS[:, 2 * i.par + c, 0:c1_ - c0], i,
                            [((c * kts + k) * P, xhi[:, k, c0:c1_], xlo[:, k, c0:c1_]) for k in range(kts)],
                            ready=None if c else ready)
            m.then_inc(slab_used, 1)

        def token_major(pe, i, ntok, n, xhi, xlo, kts, krow=0):
            slab_begin(pe, i)
            for tt in range(ntok):
                out = PS[:, 2 * i.par + tt // 2, (tt % 2) * 256:(tt % 2) * 256 + n]
                for k in range(kts):
                    for j, (x, w) in enumerate(((xhi, high(i)), (xhi, low(i)), (xlo, high(i)))):
                        m = pe.matmul(out, x[:, krow + k, tt * P:(tt + 1) * P], w[:, k * n:(k + 1) * n],
                                      start=k == 0 and j == 0, stop=k == kts - 1 and j == 2)
            m.then_inc(slab_used, 1)

        def dense_one(pe, i, chunks=2, ready=None):
            slab_begin(pe, i)
            for c in range(chunks):
                m = product(pe, PS[:, i.par, c * T:(c + 1) * T], i,
                            [((c * KT + k) * P, xh[:, k, 0:T], xl[:, k, 0:T]) for k in range(KT)], ready=None if c else ready)
            m.then_inc(slab_used, 1)

        def bank(i):
            return PS[:, i.par, :].rearrange("p (c t) -> p c t", c=2)

        def banks(i, n):
            return PS[:, 2 * i.par:2 * i.par + 2, 0:n]

        class Chain:

            def __init__(self, eng, sem):
                self.eng, self.sem, self.n = eng, sem, 0

            def after(self, ins):
                self.n += 1
                ins.then_inc(self.sem, 1)
                self.eng.wait_ge(self.sem, self.n)

        def rstd(ch, dve, out, total, n):
            inverse_root(ch, dve, out, dve.tensor_scalar(out, total, 1.0 / n, EPS, ALU.mult, ALU.add))

        roots = {"dve": 0, "act": 0}

        def inverse_root(ch, dve, out, ins):
            roots["dve"] += 1
            ins.then_inc(on["var_ready"], 1)
            dve.wait_ge(on["root_done"], roots["dve"])
            ch.after(dve.reciprocal(out, out))

        def act_root(act, out):
            roots["act"] += 1
            act.wait_ge(on["var_ready"], roots["act"])
            act.activation(out, out, ACT.Sqrt).then_inc(on["root_done"], 1)

        def bc(ap, n):
            return ap.unsqueeze(1).broadcast_to([ap.shape[0], n, ap.shape[1]])

        def bl(ap, n):
            return ap.unsqueeze(len(ap.shape)).broadcast_to(list(ap.shape) + [n])

        UNITS = [("S", 0), ("W", 0), ("C", 0), ("A", 0), ("S", 1), ("W", 1), ("C", 1), ("A", 1)]
        UN = len(UNITS)
        TR, c1 = b1["TR"], b1["c1"]
        CR = b1["CR"]
        SMF = b1["SM"][:, :, :, :].rearrange("p a b c -> p (a b c)")
        CXF = b1["CX"][:, :, :].rearrange("p c t -> p (c t)")
        BLK = b1["PT"][:, 0, 0, :].rearrange("p (n j) -> p n j", n=16)
        KCV = b1["PT"][:, 1, 0, 0:T]
        ccol = lambda name: cst(name, c1, C1)

        def keys_of(u):
            kind, blk = UNITS[u]
            return NCMP if kind == "C" else P * (blk + 1)

        names = """xl_written mix_rest x_chunk v_done sc_lo cr_zero tr_ready mod_cols mod_read late_in ctx_in kc_raw conv_done
                    sq_ready rms_in rms_out xm_written perms_done roped blk_ready idx_scores_out idx_relu idx_used scores_out
                    soft_max exp_done p_ready pt_ready pt_copied pv_done o_taken pool_in pool_out var_ready root_done mixh_done
                    mixl_done gates_e kc_ready rms_sum sc_ready mod_final xm_hi xm_lo x_scaled gate_act h_hi h_lo ln_sq ln_in
                    ln_sum z_out z_in z_ln ge_in ge_done kq_ready kd_t kdt_done att_out att_masked u_out s_ready og_out oa_done
                    gq_sum gq_sq mg_hi mg_ready cq_sq cq_sum cq_ready cq_hi cq_lo qk2_ready rm_out c2_in c3_in fmax fsoft fexp
                    fnorm ftr fcopy fpv fhi flo qkv_ready""".split()
        on = {n: sig(n) for n in names}

        block = ctx.enter_context(nc.Block())

        @block.sync
        def _(sp):
            for name, n, f in RUNS:
                def load(i, k, name=name):
                    if i.base >= RING + FIRST_LEN:
                        sp.wait_ge(lo_done["dve"], i.count(4, LO["dve"][i.base - RING] + 1))
                    elif i.base >= RING:
                        sp.wait_ge(slab_used, i.count(4, i.base - RING + 1))
                    src = a[name][bass.ds(k, 1)].rearrange("a p n -> p (a n)") if i.reg is not None else a[name][k]
                    f = SIZE[i.base]
                    sp.dma_start(raw[:, i.slot, 0:f], src[:, 0:f]).then_inc(slab_full[i.slot], 16)
                if name.startswith("layer"):
                    for k in range(n):
                        load(Idx(START[name] + k), k)
                else:
                    runs_of(sp, name, load)
            sp.wait_ge(on["x_chunk"], KT * 7)
            sp.dma_start(a["out"], X[:, :, 0:T]).then_inc(out_stored, 16)
            sp.wait_ge(out_stored, 16)

        FFN_STAGES = {0: (0, 1, 0, 2 * T), 2: (0, 2, 6, 2 * T), 3: (1, 1, 0, 2 * T), 5: (1, 2, 6, T)}
        WIDTH = [2 * T, 2 * T, 2 * T, 2 * T, T, T]
        SQ, HF, SI, NRM, HH, HL = (ff[n] for n in ("SQ", "HF", "SI", "NRM", "HH", "HL"))
        c2 = ev["c2"]
        W = ev["W"]
        work = lambda n: W[:, 2 * n:2 * n + 2, :]
        G_, B_, T1, QE, KE, QB = range(6)
        GATE_BUFFERS = ((T1, QB), (KE, B_))
        CH, CL = xh[:, 4:8, :], xl[:, 4:8, :]
        AM = W[:, 2 * T1:2 * T1 + 2, :].rearrange("p a (b t) -> p a b t", t=GC)
        ORDER = ([4, 5, 6, 7, 0, 1, 2, 3], [7, 6, 5, 4, 3, 2, 1, 0])
        MLA_UNITS = [(h, blk, 0) for h in range(4) for blk in range(2)] + [(h, blk, 1) for h in range(4) for blk in range(2)]
        NA_UNITS = [(h, blk, 0) for h in range(16) for blk in range(2)]

        def last_slabs(m):
            if m in (1, 4):
                s0 = START["eout" if m == 1 else "oout"]
                return [(Idx(s0 + n), slice(2 * n, 2 * n + 2)) for n in range(4)]
            s0 = START["ffo{1}{0}1".format(*FFN_STAGES[m])]
            return [(Idx(s0 + k), slice(k, k + 1)) for k in range(KT)]

        SQUARES = np.cumsum([0] + [len(last_slabs(m)) for m in range(6)]).tolist()

        def hidden_before(m, half):
            return ([0, 2, 3, 5].index(m) * 2 + half) * FH

        STAGES = [(0, 0), (0, 3), (0, 6), (1, 0), (1, 3), (1, 6)]

        def modulations(m):
            l, j = STAGES[m]
            for br in range(WIDTH[m - 1] // T if m else 2):
                cols = slice(br * T, (br + 1) * T)
                yield cols, (lambda k: mod[:, l, j + 1, k, br:br + 1]), (lambda k: mod[:, l, j, k, br:br + 1])

        def act_modulate(act, m):
            if m == 0:
                act.wait_ge(on["ctx_in"], 16)
            for k in range(KT):
                act.wait_ge(on["x_chunk"], KT * m + k + 1)
                for cols, scale, shift in modulations(m):
                    mm = act.activation(xh[:, k, cols], X[:, k, cols], ACT.Identity, bias=shift(k), scale=scale(k))
                mm.then_inc(on["xm_hi"], 1)
            act.wait_ge(on["xm_hi"], KT * (m + 1))
            act.wait_ge(on["v_done"], KT * (m + 1))
            act.activation(X[:, :, 0:WIDTH[m]], X[:, :, 0:WIDTH[m]], ACT.Copy, scale=ALPHA).then_inc(on["x_scaled"], 1)

        def pool_modulate(pool, m):
            if m == 0:
                pool.wait_ge(on["ctx_in"], 16)
            for k in range(KT):
                pool.wait_ge(on["x_chunk"], KT * m + k + 1)
                for cols, scale, shift in modulations(m):
                    mm = pool.tensor_scalar(SQ[:, k, cols], X[:, k, cols], scale(k), shift(k), ALU.mult, ALU.add)
                mm.then_inc(on["v_done"], 1)

        def dve_modulate(dve, m, norm):
            n = WIDTH[m - 1] if m else 2 * T

            def take_rest(k):
                dve.wait_ge(on["v_done"], KT * m + k + 1)
                dve.wait_ge(on["xm_hi"], KT * m + k + 1)
                dve.tensor_tensor(xl[:, k, 0:n], SQ[:, k, 0:n], xh[:, k, 0:n].bitcast(F32), ALU.subtract)\
                    .then_inc(on["xm_lo"], 1)
            for k in range(KT):
                norm(k).then_inc(on["x_chunk"], 1)
                if m < 6 and k:
                    take_rest(k - 1)
            if m < 6:
                take_rest(KT - 1)

        def last_pair(eng, i):
            for par in range(2):
                last = i.d - (i.d - par) % 2
                eng.wait_ge(drained[par], last // 2 + 1)

        def add_residual(dve, m, l, j, i, k, bank, inc):
            for br in range(WIDTH[m] // T):
                if i.reg is None:
                    xk, g = X[:, k, br * T:(br + 1) * T], mod[:, l, j, k, br:br + 1]
                else:
                    xk = X[:, bass.ds(k, 1), br * T:(br + 1) * T].rearrange("p a t -> p (a t)")
                    g = mod[:, l, j, bass.ds(k, 1), br]
                mm = dve.scalar_tensor_tensor(out=xk, in0=PS[:, bank, br * T:(br + 1) * T], scalar=g, in1=xk,
                                              op0=ALU.mult, op1=ALU.add)
            if inc:
                mm.then_inc(drained[i.par], 1)

        def act_squares(act, m, i, chunks):
            n = WIDTH[m]
            act.wait_ge(drained[i.par], i.d // 2 + 1)
            act.activation(SQ[:, chunks, 0:n], X[:, chunks, 0:n], ACT.Square).then_inc(on["ln_sq"], 1)

        def pool_stats(pool, ch, m, slabs):
            n = WIDTH[m]
            for s, (i, chunks) in enumerate(slabs):
                for j, (src, sem, count) in enumerate(((X, drained[i.par], i.d // 2 + 1), (SQ, on["ln_sq"], SQUARES[m] + s + 1))):
                    pool.wait_ge(sem, count)
                    for k in range(chunks.start, chunks.stop):
                        if k == 0:
                            continue
                        ins = pool.tensor_tensor(NRM[:, j, 0:n], src[:, 0, 0:n] if k == 1 else NRM[:, j, 0:n], src[:, k, 0:n], ALU.add)
                        if k < KT - 1:
                            ch.after(ins)
                        else:
                            ins.then_inc(on["ln_in"], 1)

        def pe_sums(pe, m):
            n = WIDTH[m]
            for j in range(2):
                pe.wait_ge(on["ln_in"], 2 * m + j + 1)
                pe.matmul(PS[:, 4 + j, 0:n], ones, NRM[:, j, 0:n], start=True, stop=True).then_inc(on["ln_sum"], 1)

        def post_norm(dve, ch, m):
            n = WIDTH[m]
            mean, var = NRM[:, 2, 0:n], NRM[:, 3, 0:n]
            dve.wait_ge(on["ln_sum"], 2 * m + 1)
            ch.after(dve.tensor_scalar(mean, PS[:, 4, 0:n], 1.0 / D, None, ALU.mult))
            ch.after(dve.tensor_tensor(var, mean, mean, ALU.mult))
            dve.wait_ge(on["ln_sum"], 2 * m + 2)
            ch.after(dve.scalar_tensor_tensor(out=var, in0=PS[:, 5, 0:n], scalar=1.0 / D, in1=var,
                                              op0=ALU.mult, op1=ALU.subtract))
            dve.tensor_scalar(var, var, 0.0, EPS, ALU.max, ALU.add).then_inc(on["var_ready"], 1)
            roots["dve"] += 1
            for k in range(2):
                ch.after(dve.tensor_tensor(X[:, k, 0:n], X[:, k, 0:n], mean, ALU.subtract))
            dve.wait_ge(on["root_done"], roots["dve"])
            ch.after(dve.reciprocal(var, var))

            def norm(k):
                if k > 1:
                    ch.after(dve.tensor_tensor(X[:, k, 0:n], X[:, k, 0:n], mean, ALU.subtract))
                return dve.tensor_tensor(X[:, k, 0:n], X[:, k, 0:n], var, ALU.mult)
            dve_modulate(dve, m + 1, norm)

        def act_ffn(act, m):
            l, f, j, n = FFN_STAGES[m]
            act_modulate(act, m)
            for half in range(2):
                def gate(i, k):
                    act_ahead(act, i)
                    act.wait_ge(slab_used, i.count(4, i.base + 1))
                    act.activation(SI[:, i.par, 0:n], PS[:, 2 * i.par, 0:n], ACT.Silu).then_inc(on["gate_act"], 1)
                runs_of(act, f"ffi{f}{l}{half}", gate)
                if half == 0:
                    runs_of(act, f"ffo{f}{l}0", lambda i, k: act_ahead(act, i))
            for i, chunks in last_slabs(m):
                act_ahead(act, i)
                act_squares(act, m, i, chunks)
            act_root(act, NRM[:, 3, 0:n])

        def pe_ffn(pe, m):
            l, f, j, n = FFN_STAGES[m]
            for half in range(2):
                first = START[f"ffi{f}{l}0"]
                runs_of(pe, f"ffi{f}{l}{half}", lambda i, k: dense(pe, i, 2, KT, xh, xl, 0, n, (on["xm_lo"], KT * m) if i.base == first else None))
                down = START[f"ffo{f}{l}{half}"]
                runs_of(pe, f"ffo{f}{l}{half}", lambda i, k: dense(pe, i, 1, FH, HH, HL, 0, n,
                                                                   (on["h_lo"], hidden_before(m, half)) if i.base == down else None))
            pe_sums(pe, m)

        def dve_ffn(dve, ch, m):
            l, f, j, n = FFN_STAGES[m]
            dve.wait_ge(on["x_scaled"], m + 1)
            for half in range(2):
                h0 = hidden_before(m, half)

                def hidden(i, k):
                    dve_ahead(dve, i)
                    dve.wait_ge(on["gate_act"], k + (h0 + 1))
                    hf = HF[:, i.par, 0:n]
                    dve.tensor_tensor(hf, SI[:, i.par, 0:n], PS[:, 2 * i.par + 1, 0:n], ALU.mult)\
                        .then_inc(drained[i.par], 1)
                    dve.wait_ge(drained[i.par], i.count(2, i.d // 2 + 1))
                    if i.reg is None:
                        hh, hl = HH[:, k, 0:n], HL[:, k, 0:n]
                    else:
                        hh = HH[:, bass.ds(k, 1), 0:n].rearrange("p a t -> p (a t)")
                        hl = HL[:, bass.ds(k, 1), 0:n].rearrange("p a t -> p (a t)")
                    dve.tensor_copy(hh, hf).then_inc(on["h_hi"], 1)
                    dve.wait_ge(on["h_hi"], k + (h0 + 1))
                    dve.tensor_tensor(hl, hf, hh.bitcast(F32), ALU.subtract).then_inc(on["h_lo"], 1)
                runs_of(dve, f"ffi{f}{l}{half}", hidden)

                def down(i, k):
                    dve_ahead(dve, i)
                    dve.wait_ge(slab_used, i.count(4, i.base + 1))
                    add_residual(dve, m, l, j + 2, i, k, 2 * i.par, True)
                runs_of(dve, f"ffo{f}{l}{half}", down)
            post_norm(dve, ch, m)

        def unit_keys(units, u):
            return (0, 2 * T) if units[u][2] == 0 else (T, 2 * T)

        def groups(units, na):
            step = 4 if na else 2
            return {g * step + step - 1: g for g in range(len(units) // step)}

        def pe_attend(pe, units, na, f0, g0, q_ap, k_ap, v_ap, pr, ptm):

            def score(u):
                h, blk, ctx_ = units[u]
                k0, k1 = unit_keys(units, u)
                if f0 + u >= 2 and u >= 2:
                    pe.wait_ge(on["fexp"], f0 + u - 1)
                pairs = q_ap(h, ctx_ * T + blk * P, k0, k1)
                for n, (q, k) in enumerate(pairs):
                    mm = pe.matmul(PS[:, u % 2, 0:k1 - k0], q, k, start=n == 0, stop=n == len(pairs) - 1)
                mm.then_inc(on["fmax"], 1)
            score(0)
            score(1)

            def turn(u):
                k0, k1 = unit_keys(units, u)
                pe.wait_ge(on["fnorm"], f0 + u + 1)
                if u >= 2:
                    pe.wait_ge(on["fcopy"], f0 + u - 1)
                for kt in range((k1 - k0) // P):
                    mm = pe.transpose(PS[:, 2 + u % 2, kt * P:(kt + 1) * P], pr[:, u % 2, kt * P:(kt + 1) * P], ident)
                mm.then_inc(on["ftr"], 1)

            def output(u):
                h, blk, ctx_ = units[u]
                k0, k1 = unit_keys(units, u)
                pe.wait_ge(on["fcopy"], f0 + u + 1)
                g = u // (4 if na else 2)
                if g >= 2 and u % (4 if na else 2) == 0:
                    pe.wait_ge(on["flo"], g0 + g - 1)
                rows = slice((h % 2) * HD, (h % 2) * HD + HD) if na else slice(0, P)
                nk = (k1 - k0) // P
                for kt in range(nk):
                    mm = pe.matmul(PS[rows, 4 + g % 2, blk * P:(blk + 1) * P], v_ap(h, k0 // P + kt),
                                   ptm[:, u % 2, kt * P:(kt + 1) * P], start=kt == 0, stop=kt == nk - 1)
                mm.then_inc(on["fpv"], 1)

            for u in range(len(units)):
                turn(u)
                if u + 2 < len(units):
                    score(u + 2)
                if u:
                    output(u - 1)
            output(len(units) - 1)

        def act_attend(act, units, na, f0, g0, scale, pr, ptm, chunk0):
            ends = groups(units, na)

            def exp(u):
                k0, k1 = unit_keys(units, u)
                act.wait_ge(on["fsoft"], f0 + u + 1)
                if u >= 2:
                    act.wait_ge(on["ftr"], f0 + u - 1)
                act.activation(pr[:, u % 2, 0:k1 - k0], PS[:, u % 2, 0:k1 - k0], ACT.Exp, scale=scale,
                               bias=tiny[:, u % 2:u % 2 + 1], accum_out=tiny[:, 2 + u % 2:3 + u % 2]).then_inc(on["fexp"], 1)

            def hi(g):
                size = 4 if na else 2
                act.wait_ge(on["fpv"], f0 + (g + 1) * size)
                ctx_ = units[g * size][2]
                act.activation(xh[:, chunk0 + g % (8 if na else 4), ctx_ * T:ctx_ * T + T], PS[:, 4 + g % 2, 0:T], ACT.Copy)\
                    .then_inc(on["fhi"], 1)
            exp(0)
            for u in range(len(units)):
                if u + 1 < len(units):
                    exp(u + 1)
                k0, k1 = unit_keys(units, u)
                act.wait_ge(on["ftr"], f0 + u + 1)
                if u >= 2:
                    act.wait_ge(on["fpv"], f0 + u - 1)
                act.activation(ptm[:, u % 2, 0:k1 - k0], PS[:, 2 + u % 2, 0:k1 - k0], ACT.Copy).then_inc(on["fcopy"], 1)
                if u - 1 in ends:
                    hi(ends[u - 1])
            hi(ends[len(units) - 1])

        def dve_attend(dve, ch, units, na, f0, g0, scale, pr, chunk0):
            ends = groups(units, na)

            def maxima(u):
                h, blk, ctx_ = units[u]
                k0, k1 = unit_keys(units, u)
                dve.wait_ge(on["fmax"], f0 + u + 1)
                s = PS[:, u % 2, 0:k1 - k0]
                if na:
                    for half in range(2):
                        r, rows = 2 * blk + half, slice(half * HD, half * HD + HD)
                        o = PS[rows, u % 2, 0:T].rearrange("p (r c) -> p r c", c=64)
                        mm = dve.tensor_tensor(o, o, od["RPB"][rows, h, 3 - r:7 - r, :], ALU.add)
                    ch.after(mm)
                nm = tiny[:, u % 2:u % 2 + 1]
                mm = dve.tensor_reduce(nm, s, AX, ALU.max, negate=True)
                if scale != 1.0:
                    ch.after(mm)
                    mm = dve.tensor_scalar(nm, nm, scale, None, ALU.mult)
                mm.then_inc(on["fsoft"], 1)

            def lo(g):
                size = 4 if na else 2
                dve.wait_ge(on["fhi"], g0 + g + 1)
                ctx_ = units[g * size][2]
                c = chunk0 + g % (8 if na else 4)
                dve.tensor_tensor(xl[:, c, ctx_ * T:ctx_ * T + T], PS[:, 4 + g % 2, 0:T],
                                  xh[:, c, ctx_ * T:ctx_ * T + T].bitcast(F32), ALU.subtract).then_inc(on["flo"], 1)
            maxima(0)
            for u in range(len(units)):
                k0, k1 = unit_keys(units, u)
                dve.wait_ge(on["fexp"], f0 + u + 1)
                r = tiny[:, 4 + u % 2:5 + u % 2]
                mm = dve.reciprocal(r, tiny[:, 2 + u % 2:3 + u % 2])
                ch.after(mm)
                p = pr[:, u % 2, 0:k1 - k0]
                dve.tensor_scalar(p, p, r, None, ALU.mult).then_inc(on["fnorm"], 1)
                if u + 1 < len(units):
                    maxima(u + 1)
                if u - 2 in ends:
                    lo(ends[u - 2])
            lo(ends[len(units) - 1])

        def act_even(act, ch):
            act.wait_ge(on["x_chunk"], KT + 1)
            act.dma_start(c2[:, :], a["c2"]).then_inc(on["c2_in"], 16)
            act_modulate(act, 1)
            s0 = START["even"]

            def act_gate_logs(d):
                t1, qb = GATE_BUFFERS[d]
                act.wait_ge(on["z_in"], d + 1)
                ch.after(act.activation(work(t1), work(t1), ACT.Exp))
                act.activation(work(t1), work(t1), ACT.Ln, bias=1.0).then_inc(on["z_ln"], 1)

            def act_gate_exps(d):
                t1, qb = GATE_BUFFERS[d]
                act.wait_ge(on["ge_in"], 2 * d + 1)
                ch.after(act.activation(work(QE), work(t1), ACT.Exp))
                act.activation(work(KE), work(t1), ACT.Exp, scale=-1.0)
                act.wait_ge(on["ge_in"], 2 * d + 2)
                act.activation(work(qb), work(B_), ACT.Exp).then_inc(on["ge_done"], 1)
                act.activation(work(G_), work(G_), ACT.Exp)
                act.activation(tiny[:, 32:48], tiny[:, 0:16], ACT.Exp).then_inc(on["ge_done"], 1)

            def turned_keys(d):
                act.wait_ge(on["kd_t"], d + 1)
                act.activation(ev["KDT"][:, :, :, :], PS[:, 4:6, :].rearrange("p a (t c) -> p a t c", c=P), ACT.Copy)\
                    .then_inc(on["kdt_done"], 1)

            for k in range(9):
                i = Idx(s0 + k)
                act_ahead(act, i)
                if k == 4:
                    act_gate_logs(0)
                if k == 5:
                    act_gate_exps(0)
                if k == 7:
                    turned_keys(0)
                    act.wait_ge(drained[1 - i.par], (i.d - 1) // 2 + 1)
                    act.activation(ml["VM"][:, :, :], ev["CQ"][:, :, :], ACT.Square).then_inc(on["cq_sq"], 1)
                if k >= 7:
                    act.wait_ge(slab_used, i.base + 1)
                    act.activation(ev["RS"][:, 2 * (k - 7):2 * (k - 7) + 2, :], banks(i, 2 * T), ACT.Silu)\
                        .then_inc(drained[i.par], 1)
            for j in range(2):
                act_root(act, ev["OA"][:, j, :])
            act.wait_ge(on["cq_ready"], 1)
            act.activation(CH, ev["CQ"][:, :, :], ACT.Copy).then_inc(on["cq_hi"], 1)
            act_gate_logs(1)
            act_gate_exps(1)
            turned_keys(1)
            act.wait_ge(on["oa_done"], 2)
            act.activation(W[:, 0:4, :], ev["OA"][:, :, :], ACT.Square).then_inc(on["gq_sq"], 1)
            for k in range(7):
                act_ahead(act, Idx(START["uq"] + k))
                if k == 1:
                    act_root(act, W[:, 0:4, :])
                if k == 4:
                    act.wait_ge(on["mg_ready"], 1)
                    act.activation(xh[:, 0:4, :], ev["OA"][:, :, :], ACT.Copy).then_inc(on["mg_hi"], 1)
            act_attend(act, MLA_UNITS, False, 0, 0, MLA_SCALE, ml["PR"], ml["PTM"], 4)
            act_out(act, 1)

        def pe_even(pe):
            s0 = START["even"]

            def gate_inputs(d):
                o, _ = SML["wg2"]
                for ft in range(2):
                    r = slice(32 * d, 32 * d + 16)
                    mm = pe.matmul(PS[:, 4 + ft, :], sml[r, o + ft * P:o + (ft + 1) * P], ev["LK"][r, 0, :], start=True, stop=True)
                mm.then_inc(on["z_out"], 1)

            def turn_keys(d):
                pe.wait_ge(on["kq_ready"], d + 1)
                for ft in range(2):
                    for tt in range(4):
                        mm = pe.transpose(PS[:, 4 + ft, tt * P:(tt + 1) * P], W[:, 2 * G_ + ft, tt * P:(tt + 1) * P], ident)
                mm.then_inc(on["kd_t"], 1)

            for k in range(9):
                i = Idx(s0 + k)
                if k in (3, 4):
                    token_major(pe, i, 4, 256, xh, xl, KT)
                else:
                    dense(pe, i, 2, KT, xh, xl, 0, 2 * T, None if k else (on["xm_lo"], KT))
                if k == 3:
                    pe.wait_ge(drained[1 - i.par], (i.d - 1) // 2 + 1)
                    gate_inputs(0)
                if k == 6:
                    turn_keys(0)
                if k == 7:
                    pe.wait_ge(on["cq_sq"], 1)
                    for c in range(3):
                        pe.matmul(PS[:, 6, :], ones, ml["VM"][:, c, :], start=c == 0, stop=c == 2)
                    pe.matmul(PS[:, 7, :], ones, ml["VM"][:, 3, :], start=True, stop=True).then_inc(on["cq_sum"], 1)
            last_pair(pe, Idx(s0 + 8))
            for d in range(2):
                if d:
                    pe.wait_ge(on["oa_done"], d)
                    turn_keys(d)
                for c in range(8):
                    for h in range(4):
                        r, ft, tt = slice((h % 2) * HD, (h % 2) * HD + HD), h // 2, c // 2
                        mm = pe.matmul(PS[(c % 2) * HD:(c % 2) * HD + HD, h % 2, (tt * 2 + ft) * GC:(tt * 2 + ft + 1) * GC],
                                       W[r, 2 * KE + ft, c * GC:(c + 1) * GC], W[r, 2 * QE + ft, c * GC:(c + 1) * GC],
                                       start=True, stop=True)
                mm.then_inc(on["att_out"], 1)
                pe.wait_ge(on["kdt_done"], d + 1)
                if d == 0:
                    gate_inputs(1)
                    pe.wait_ge(on["cq_ready"], 1)
                for c in ORDER[d][:7]:
                    cp, tt = c % 2, c // 2
                    rows = slice(cp * HD, cp * HD + HD)
                    for h in range(4):
                        o = (tt % 2) * 256 + (h // 2) * P
                        mm = pe.matmul(PS[(h % 2) * HD:(h % 2) * HD + HD, 2 + 4 * cp + tt // 2, o:o + P],
                                       ev["KDT"][rows, h // 2, tt, (h % 2) * HD:(h % 2) * HD + HD],
                                       ev["V"][rows, tt, h * P:(h + 1) * P], start=True, stop=True)
                mm.then_inc(on["u_out"], 1)
                pe.wait_ge(on["att_masked"], d + 1)
                pe.wait_ge(on["z_in"], 2)
                pe.wait_ge(on["s_ready"], d + 1)
                for c in range(8):
                    cp, tt, n = c % 2, c // 2, ORDER[d].index(c)
                    tp = tt // 2
                    for h in range(4):
                        rows = slice(cp * HD, cp * HD + HD)
                        o = ((tt % 2) * 4 + h) * GC
                        pe.matmul(PS[:, 2 * tp + cp, o:o + GC], ev["V"][rows, tt, h * P:(h + 1) * P],
                                  AM[rows, h % 2, tt * 2 + h // 2, :], start=True, stop=True)
                        r = slice((h % 2) * HD, (h % 2) * HD + HD)
                        o = (h // 2) * T + (c % 4) * GC
                        mm = pe.matmul(PS[:, 4 + 2 * tp + h % 2, o:o + GC], ev["S"][r, n, h // 2, :],
                                       W[r, 2 * GATE_BUFFERS[d][1] + h // 2, c * GC:(c + 1) * GC], start=True, stop=True)
                mm.then_inc(on["og_out"], 1)
            pe.wait_ge(on["oa_done"], 2)
            pe.wait_ge(on["cq_lo"], 1)
            for k in range(3):
                dense(pe, Idx(START["uq"] + k), 2, 3, CH, CL, 0, 2 * T)
                if k == 0:
                    pe.wait_ge(on["gq_sq"], 1)
                    for h in range(4):
                        mm = pe.matmul(PS[:, 4 + h, :], ones, W[:, h, :], start=True, stop=True)
                    mm.then_inc(on["gq_sum"], 1)
            for k in range(4):
                i = Idx(START["ukv"] + k)
                if k < 2:
                    slab_begin(pe, i)
                    for c in range(2):
                        mm = product(pe, PS[:, 2 * i.par + c, :], i, [(c * P, CH[:, 3, :], CL[:, 3, :])])
                    mm.then_inc(slab_used, 1)
                else:
                    token_major(pe, i, 4, 256, CH, CL, 1, krow=3)
            last_pair(pe, Idx(START["ukv"] + 3))
            pe.wait_ge(on["mg_ready"], 1)
            pe.matmul(PS[:, 4, :], cst("permM"), ml["QR"][:, :, 0:T], start=True, stop=True)
            pe.matmul(PS[:, 5, 0:T], cst("permM"), ev["LK"][:, 1, 0:T], start=True, stop=True).then_inc(on["rm_out"], 1)
            pe.wait_ge(on["qk2_ready"], 1)

            def qk(h, q0, k0, k1):
                r = slice((h % 2) * HD, (h % 2) * HD + HD)
                return [(ml["QN"][:, h, q0:q0 + P], ml["KN"][:, h, k0:k1]), (ml["QR"][r, h // 2, q0:q0 + P], ev["LK"][r, 1, k0:k1])]
            pe_attend(pe, MLA_UNITS, False, 0, 0, qk, None, lambda h, tt: ml["VM"][:, tt, h * P:(h + 1) * P], ml["PR"], ml["PTM"])
            pe.wait_ge(on["flo"], 8)
            for k in range(4):
                dense(pe, Idx(START["eout"] + k), 2, KT, xh, xl, 0, 2 * T)
            pe_sums(pe, 1)

        def dve_even(dve, ch):
            s0 = START["even"]
            S, OA, CQ = ev["S"], ev["OA"], ev["CQ"]
            chunks = lambda t: t.rearrange("p f (c t) -> p (f c) t", t=GC)

            def gate_input(d):
                t1 = GATE_BUFFERS[d][0]
                dve.wait_ge(on["z_out"], d + 1)
                for ft in range(2):
                    mm = dve.tensor_scalar(W[:, 2 * G_ + ft, :], PS[:, 4 + ft, :], vcol("bg", 2 * d + ft), None, ALU.add)
                ch.after(mm)
                dve.scalar_tensor_tensor(out=work(t1), in0=work(G_), scalar=-1.0, in1=work(G_), op0=ALU.mult, op1=ALU.min)\
                    .then_inc(on["z_in"], 1)
                dve.wait_ge(on["z_in"], d + 1)

            def gate_sums(d):
                T1_ = GATE_BUFFERS[d][0]
                ch.after(dve.tensor_scalar(work(G_), work(G_), 0.0, 1.0 / 16, ALU.min, ALU.mult))
                dve.wait_ge(on["z_ln"], d + 1)
                ch.after(dve.scalar_tensor_tensor(out=work(G_), in0=work(T1_), scalar=-1.0 / 16, in1=work(G_),
                                                  op0=ALU.mult, op1=ALU.add))
                for ft in range(2):
                    mm = dve.tensor_tensor_scan(W[:, 2 * B_ + ft, :], cst("reset", c2, C2), W[:, 2 * G_ + ft, :], 0.0,
                                                ALU.mult, ALU.add)
                ch.after(mm)
                g, b, t1 = chunks(work(G_)), chunks(work(B_)), chunks(work(T1_))
                tot, ref = tiny[:, 0:16], tiny[:, 16:32]
                ch.after(dve.tensor_copy(tot, b[:, :, GC - 1]))
                if d:
                    ch.after(dve.tensor_tensor(b, bl(tot, GC), b, ALU.subtract))
                    ch.after(dve.tensor_tensor(b, b, g, ALU.add))
                ch.after(dve.tensor_copy(ref, b[:, :, GC // 2 - 1 + d]))
                ch.after(dve.tensor_tensor(t1, b, bl(ref, GC), ALU.subtract))
                dve.tensor_scalar(work(T1_), work(T1_), 80.0, -80.0, ALU.min, ALU.max).then_inc(on["ge_in"], 1)
                dve.tensor_tensor(g, bl(tot, GC), b, ALU.subtract).then_inc(on["ge_in"], 1)
                dve.wait_ge(on["ge_in"], 2 * d + 2)

            def gate_products(d):
                qb = GATE_BUFFERS[d][1]
                dve.wait_ge(on["ge_done"], 2 * d + 1)
                dve.tensor_tensor(work(QE), work(QE), ev["Q"][:, :, :], ALU.mult)
                dve.tensor_tensor(work(KE), work(KE), ev["K"][:, :, :], ALU.mult)
                dve.tensor_tensor(work(qb), work(qb), ev["Q"][:, :, :], ALU.mult)
                dve.wait_ge(on["ge_done"], 2 * d + 2)
                dve.tensor_tensor(work(G_), work(G_), ev["K"][:, :, :], ALU.mult).then_inc(on["kq_ready"], 1)

            for k in range(9):
                i = Idx(s0 + k)
                dve_ahead(dve, i)
                if k == 8:
                    dve.wait_ge(on["cq_sum"], 1)
                    for j, n in ((0, 384), (1, P)):
                        rstd(ch, dve, OA[:, j, :], PS[:, 6 + j, :], n)
                    dve.memset(S[:, 0, :, :], 0.0)
                    for c in range(4):
                        g = vcol("qnorm", c) if c < 3 else vcol("kvnorm", 0)
                        mm = dve.scalar_tensor_tensor(out=CQ[:, c, :], in0=CQ[:, c, :], scalar=g, in1=OA[:, c // 3, :],
                                                      op0=ALU.mult, op1=ALU.mult)
                    mm.then_inc(on["cq_ready"], 1)
                if k >= 7:
                    continue
                dve.wait_ge(slab_used, i.base + 1)
                if k == 0:
                    mm = dve.tensor_scalar(ev["Q"][:, :, :], banks(i, 2 * T), HD ** -0.5, None, ALU.mult)
                elif k in (1, 2):
                    mm = dve.tensor_copy(ev["K" if k == 1 else "LK"][:, :, :], banks(i, 2 * T))
                elif k in (3, 4):
                    mm = dve.tensor_copy(ev["V"][:, :, 256 * (k - 3):256 * (k - 2)],
                                         banks(i, 512).rearrange("p a (b n) -> p (a b) n", b=2))
                else:
                    mm = dve.tensor_copy(ev["CQ"][:, 2 * (k - 5):2 * (k - 5) + 2, :], banks(i, 2 * T))
                mm.then_inc(drained[i.par], 1)
                if k == 3:
                    gate_input(0)
                if k == 4:
                    dve.wait_ge(on["c2_in"], 16)
                    gate_sums(0)
                if k == 5:
                    gate_products(0)
            dve.wait_ge(on["cq_hi"], 1)
            dve.tensor_tensor(CL, CQ[:, :, :], CH.bitcast(F32), ALU.subtract).then_inc(on["cq_lo"], 1)
            dve.wait_ge(on["cq_lo"], 1)
            for d in range(2):
                dve.wait_ge(on["att_out"], d + 1)
                mk = cst("gmask", c2, C2)[:, d * GC:(d + 1) * GC]
                dve.tensor_tensor(AM[:, :, :, :].rearrange("p a b t -> p (a b) t"),
                                  PS[:, 0:2, :].rearrange("p a (b t) -> p (a b) t", t=GC), bc(mk, 16), ALU.mult)\
                    .then_inc(on["att_masked"], 1)
                if d == 0:
                    gate_input(1)
                dve.wait_ge(on["u_out"], d + 1)
                for n, c in enumerate(ORDER[d][:7]):
                    cp, tt = c % 2, c // 2
                    u = PS[:, 2 + 4 * cp + tt // 2, (tt % 2) * 256:(tt % 2) * 256 + 256].rearrange("p (f t) -> p f t", f=2)
                    if n == 0:
                        mm = dve.tensor_copy(S[:, 1, :, :], u)
                    else:
                        for ft in range(2):
                            mm = dve.scalar_tensor_tensor(out=S[:, n + 1, ft, :], in0=S[:, n, ft, :],
                                                          scalar=tiny[:, 32 + 8 * ft + c:33 + 8 * ft + c], in1=u[:, ft, :],
                                                          op0=ALU.mult, op1=ALU.add)
                    if n < 6:
                        ch.after(mm)
                mm.then_inc(on["s_ready"], 1)
                dve.wait_ge(on["s_ready"], d + 1)
                if d == 0:
                    gate_sums(1)
                    gate_products(1)
                dve.wait_ge(on["og_out"], d + 1)
                for tp in range(2):
                    for cp in range(2):
                        o = OA[:, :, tp * T:(tp + 1) * T].rearrange("p h (t c i) -> p t h c i", t=2, c=2)[:, :, :, cp, :]
                        src = PS[:, 2 * tp + cp, :].rearrange("p (t h i) -> p t h i", t=2, h=4)
                        if d == 0:
                            mm = dve.tensor_copy(o, src)
                        else:
                            mm = dve.tensor_tensor(o, o, src, ALU.add)
                    ch.after(mm)
                    for hp in range(2):
                        o = OA[:, :, tp * T:(tp + 1) * T].rearrange("p (f q) t -> p f q t", q=2)[:, :, hp, :]
                        src = PS[:, 4 + 2 * tp + hp, :].rearrange("p (f t) -> p f t", f=2)
                        mm = dve.tensor_tensor(o, o, src, ALU.add)
                    if tp == 0:
                        ch.after(mm)
                mm.then_inc(on["oa_done"], 1)
                dve.wait_ge(on["oa_done"], d + 1)
            QN, VM, rs = ml["QN"], ml["VM"], W[:, 0:4, :]
            for k in range(7):
                i = Idx(START["uq"] + k)
                dve_ahead(dve, i)
                dve.wait_ge(slab_used, i.base + 1)
                if k < 2:
                    mm = dve.tensor_copy(QN[:, 2 * k:2 * k + 2, :], banks(i, 2 * T))
                elif k == 2:
                    mm = dve.tensor_copy(ml["QR"][:, :, :], banks(i, 2 * T))
                elif k < 5:
                    mm = dve.tensor_copy(ml["KN"][:, 2 * (k - 3):2 * (k - 3) + 2, :], banks(i, 2 * T))
                else:
                    mm = dve.tensor_copy(VM[:, :, 256 * (k - 5):256 * (k - 4)],
                                         banks(i, 512).rearrange("p a (b n) -> p (a b) n", b=2))
                mm.then_inc(drained[i.par], 1)
                if k == 0:
                    dve.wait_ge(on["gq_sum"], 1)
                    dve.tensor_scalar(rs, PS[:, 4:8, :], 1.0 / P, EPS, ALU.mult, ALU.add).then_inc(on["var_ready"], 1)
                    roots["dve"] += 1
                if k == 1:
                    dve.wait_ge(on["root_done"], roots["dve"])
                    ch.after(dve.reciprocal(rs, rs))
                if k == 2:
                    ch.after(dve.tensor_tensor(OA[:, :, :], OA[:, :, :], rs, ALU.mult))
                if k == 3:
                    dve.scalar_tensor_tensor(out=OA[:, :, :], in0=OA[:, :, :], scalar=vcol("gnorm", 0), in1=ev["RS"][:, :, :],
                                             op0=ALU.mult, op1=ALU.mult).then_inc(on["mg_ready"], 1)
            dve.wait_ge(on["mg_hi"], 1)
            ch.after(dve.tensor_tensor(xl[:, 0:4, :], OA[:, :, :], xh[:, 0:4, :].bitcast(F32), ALU.subtract))
            dve.wait_ge(on["rm_out"], 1)
            cs = cst("ropeM", c2, C2)
            CT, ST = cs[:, 0:T], cs[:, T:2 * T]
            LK, PR, QR = ev["LK"], ml["PR"], ml["QR"]
            rq, rk = PR[:, 0, :].rearrange("p (c t) -> p c t", c=2), PR[:, 1, 0:T]
            dve.tensor_tensor(rq, PS[:, 4, :].rearrange("p (c t) -> p c t", c=2), bc(ST, 2), ALU.mult)
            dve.tensor_tensor(rk, PS[:, 5, 0:T], ST, ALU.mult)
            dve.tensor_tensor(QR[:, :, 0:T], QR[:, :, 0:T], bc(CT, 2), ALU.mult)
            ch.after(dve.tensor_tensor(LK[:, 1, 0:T], LK[:, 1, 0:T], CT, ALU.mult))
            dve.tensor_tensor(QR[:, :, 0:T], QR[:, :, 0:T], rq, ALU.add)
            dve.tensor_tensor(LK[:, 1, 0:T], LK[:, 1, 0:T], rk, ALU.add).then_inc(on["qk2_ready"], 1)
            dve_attend(dve, ch, MLA_UNITS, False, 0, 0, MLA_SCALE, ml["PR"], 4)
            dve_out(dve, ch, 1, 0, "eout")

        def act_out(act, m):
            for i, chunks in last_slabs(m):
                act_ahead(act, i)
                act_squares(act, m, i, chunks)
            act_root(act, NRM[:, 3, 0:WIDTH[m]])

        def dve_out(dve, ch, m, l, name):
            dve.wait_ge(on["x_scaled"], m + 1)
            for k in range(4):
                i = Idx(START[name] + k)
                dve_ahead(dve, i)
                dve.wait_ge(slab_used, i.base + 1)
                for c in range(2):
                    add_residual(dve, m, l, 5, i, 2 * k + c, 2 * i.par + c, c == 1)
            post_norm(dve, ch, m)

        def act_odd(act, ch):
            act.wait_ge(on["x_chunk"], 4 * KT + 1)
            act.dma_start(od["nmask"][:, :], a["nmask"]).then_inc(on["c3_in"], 16)
            act.dma_start(od["RPB"][:, :, :, :], a["rpb"]).then_inc(on["c3_in"], 16)
            act_modulate(act, 4)
            for k in range(12):
                act_ahead(act, Idx(START["odd"] + k))
            act_attend(act, NA_UNITS, True, 16, 8, 1.0, od["NP"], od["NPT"], 0)
            act_out(act, 4)

        def pe_odd(pe):
            for k in range(12):
                i = Idx(START["odd"] + k)
                if k < 8:
                    dense(pe, i, 2, KT, xh, xl, 0, T if k < 4 else 2 * T, None if k else (on["xm_lo"], 4 * KT))
                else:
                    token_major(pe, i, 4, 256, xh, xl, KT)
            last_pair(pe, Idx(START["odd"] + 11))
            pe.wait_ge(on["qkv_ready"], 1)

            def qk(h, q0, k0, k1):
                r = slice((h % 2) * HD, (h % 2) * HD + HD)
                return [(od["NQ"][r, h // 2, q0:q0 + P], od["NK"][r, h // 2, k0:k1])]
            pe_attend(pe, NA_UNITS, True, 16, 8, qk, None, lambda h, tt: od["NV"][:, tt, h * HD:(h + 1) * HD], od["NP"], od["NPT"])
            pe.wait_ge(on["flo"], 16)
            for k in range(4):
                dense(pe, Idx(START["oout"] + k), 2, KT, xh, xl, 0, T)
            pe_sums(pe, 4)

        def dve_odd(dve, ch):
            for k in range(12):
                i = Idx(START["odd"] + k)
                dve_ahead(dve, i)
                dve.wait_ge(slab_used, i.base + 1)
                if k < 4:
                    mm = dve.tensor_scalar(od["NQ"][:, 2 * k:2 * k + 2, :], banks(i, T), HD ** -0.5, None, ALU.mult)
                elif k < 8:
                    mm = dve.tensor_copy(od["NK"][:, 2 * (k - 4):2 * (k - 4) + 2, :], banks(i, 2 * T))
                else:
                    mm = dve.tensor_copy(od["NV"][:, :, 256 * (k - 8):256 * (k - 7)],
                                         banks(i, 512).rearrange("p a (b n) -> p (a b) n", b=2))
                mm.then_inc(drained[i.par], 1)
            dve.wait_ge(on["c3_in"], 32)
            rp = od["RPB"][:, :, :, :].rearrange("p h d c -> p (h d) c")
            dve.tensor_tensor(rp, rp, bc(od["nmask"][:, :], 112), ALU.add).then_inc(on["qkv_ready"], 1)
            dve.wait_ge(on["qkv_ready"], 1)
            dve_attend(dve, ch, NA_UNITS, True, 16, 8, 1.0, od["NP"], 0)
            dve_out(dve, ch, 4, 1, "oout")

        def scalar_block2(act, ch):
            for m in range(6):
                act_ffn(act, m) if m in FFN_STAGES else (act_even if m == 1 else act_odd)(act, ch)

        def tensor_block2(pe):
            for m in range(6):
                pe_ffn(pe, m) if m in FFN_STAGES else (pe_even if m == 1 else pe_odd)(pe)

        def vector_block2(dve, ch):
            for m in range(6):
                dve_ffn(dve, ch, m) if m in FFN_STAGES else (dve_even if m == 1 else dve_odd)(dve, ch)

        @block.gpsimd
        def _(pool):
            ch = Chain(pool, sig("pool_step"))
            M, W2, DU, UP = b1["MIX"], b1["W2"], b1["DU"], b1["UP"]
            pool.memset(TR[:, :], 0.0).then_inc(on["cr_zero"], 1)
            pool.memset(DU[:, :, 0:16], 0.0)
            ch.after(pool.memset(UP[:, :, 0:2], 0.0))

            def sum_squares(n):
                for k in range(1, KT):
                    pool.wait_ge(on["sq_ready"], 4 * n + k // 2 + 1)
                    ins = pool.tensor_tensor(tiny2[:, :], M[:, 0, :] if k == 1 else tiny2[:, :], M[:, k, :], ALU.add)
                    ch.after(ins) if k < KT - 1 else ins.then_inc(on["rms_in"], 1)

            for l in range(DEPTH):
                s0 = START[f"layer{l}"]

                sum_squares(l)

                def copied(k):
                    d = BANKED[s0 + PLAN.index(("in", k))]
                    pool.wait_ge(drained[d % 2], d // 2 + 1)

                for pos, (kind, n) in enumerate(PLAN):
                    if splitter(s0 + pos) == "pool":
                        split_lo(pool, Idx(s0 + pos), SLAB, "pool")
                    if l == 0 and (kind, n) == ("ada", 7):
                        pool.wait_ge(consts_in, 2 * 16)
                        pool.wait_ge(on["late_in"], 2 * 16)
                    if (kind, n) == ("ada", 9):
                        copied(8)
                        copied(9)
                        ch.after(pool.tensor_tensor(UP[:, :, 2:], b1["CC"][:, :, :], b1["CX"][:, :, :], ALU.mult))
                        tap = b1["CX"]
                        for c in range(2):
                            y = M[:, 4 + c, :]
                            ch.after(pool.tensor_scalar(y, UP[:, c, 0:T], vcol("conv", l * 6 + c), None, ALU.mult))
                            for j in (1, 2):
                                ch.after(pool.tensor_scalar(tap[:, c, :], UP[:, c, j:j + T], vcol("conv", l * 6 + 2 * j + c), None, ALU.mult))
                                ch.after(pool.tensor_tensor(y, y, tap[:, c, :], ALU.add))
                    if (kind, n) == ("ada", 10):
                        copied(10)
                        ch.after(pool.tensor_tensor(W2[:, :, 1:], DU[:, :, 1:], DU[:, :, 0:15 + T], ALU.add))
                        pm, inv = b1["CC"], ccol("invc").rearrange("p (c t) -> p c t", c=2)
                        lo, hi = slice(0, HD), slice(HD, P)
                        a4 = M[:, 0:3, :].rearrange("p c t -> p (c t)")[:, 0:2 * (T + 16)].rearrange("p (c t) -> p c t", c=2)
                        a8 = CXF[:, 0:T + 16]
                        ch.after(pool.tensor_tensor(pm[lo, 0, :], W2[lo, 0, 16:], inv[lo, 0, :], ALU.mult))
                        ch.after(pool.tensor_tensor(a4[:, :, 3:], W2[:, :, 3:], W2[:, :, 1:14 + T], ALU.add))
                        ch.after(pool.tensor_tensor(pm[hi, 0, :], a4[hi, 0, 16:], inv[hi, 0, :], ALU.mult))
                        ch.after(pool.tensor_tensor(a8[:, 7:], a4[:, 1, 7:], a4[:, 1, 3:12 + T], ALU.add))
                        ch.after(pool.tensor_tensor(pm[lo, 1, :], a8[lo, 16:], inv[lo, 1, :], ALU.mult))
                        ch.after(pool.tensor_tensor(W2[:, 1, 16:], a8[:, 16:], a8[:, 8:8 + T], ALU.add))
                        ch.after(pool.tensor_tensor(pm[hi, 1, :], W2[hi, 1, 16:], inv[hi, 1, :], ALU.mult))
                        pool.tensor_tensor(W2[:, :, 16:], pm[:, :, :], DU[:, :, 16:], ALU.subtract).then_inc(on["pool_in"], 1)
                    if (kind, n) == ("ada", 13):
                        copied(11)
                        pool.tensor_tensor(M[:, 4:6, :], M[:, 4:6, :], b1["CB"][:, :, :], ALU.mult).then_inc(on["conv_done"], 1)
            sum_squares(2)
            for m in range(6):
                pool_modulate(pool, m)
                pool_stats(pool, ch, m, last_slabs(m))

        @block.scalar
        def _(act):
            ch = Chain(act, act_step)
            act.dma_start(X[:, :, 0:T], a["x"]).then_inc(acts_in, 16)
            for dst, src in ((const, "const"), (vec, "vec")):
                act.dma_start(dst[:, :], a[src]).then_inc(consts_in, 16)

            def squares(n):
                act.activation(b1["MIX"][:, 2 * n:2 * n + 2, :], X[:, 2 * n:2 * n + 2, 0:T], ACT.Square).then_inc(on["sq_ready"], 1)

            def softmax_exp(l, u):
                n = keys_of(u)
                act.wait_ge(on["soft_max"], l * UN + u + 1)
                for g in range(4):
                    m = act.activation(b1["SM"][:, u % 2, g, 0:n], b1["SM"][:, u % 2, g, 0:n], ACT.Exp,
                                       bias=tiny[:, 8 * (u % 2) + g:8 * (u % 2) + g + 1],
                                       accum_out=tiny[:, 16 + 8 * (u % 2) + g:17 + 8 * (u % 2) + g])
                m.then_inc(on["exp_done"], 1)

            def block1(l):
                if l == 0:
                    act.wait_ge(acts_in, 16)
                    for n in range(4):
                        squares(n)
                if l == 0:
                    act.wait_ge(consts_in, 2 * 16)
                    o = VEC["c"][0]
                    act.activation(sc[:, :, :], vec[:, o:o + 2 * KT].rearrange("p (k b) -> p k b", b=2), ACT.Silu)\
                        .then_inc(on["sc_ready"], 1)
                    act.wait_ge(on["sc_ready"], 1)
                    act.wait_ge(on["cr_zero"], 1)
                    ch.after(act.activation(CR[:, :, :].rearrange("p k n -> p (k n)").rearrange("p (a n) -> p a n", a=4),
                                            bc(TR[:, :], 4), ACT.Copy))
                    act.activation(CR[:, :, P:P + 2], sc[:, :, :], ACT.Copy).then_inc(on["sc_ready"], 1)
                    for b in range(2):
                        split_hi(act, Idx(b), SIZE[b])
                act_root(act, tiny3[:, :])
                for k in range(KT):
                    act.wait_ge(on["rms_out"], KT * l + k + 1)
                    act.activation(xh[:, k, 0:T], b1["MIX"][:, k, :], ACT.Copy).then_inc(on["xm_written"], 1)
                s0 = START[f"layer{l}"]

                def ada_step(pos, a_):
                    act_ahead(act, Idx(s0 + pos))
                    if a_ % GROUP == GROUP - 1:
                        g = GROUPS * l + a_ // GROUP
                        act.wait_ge(slab_used, s0 + pos + 1)
                        if g:
                            act.wait_ge(on["mod_cols"], g)
                        act.activation(TR[:, :], PS[:, 7, :], ACT.Copy).then_inc(on["tr_ready"], 1)

                for pos, (kind, k) in enumerate(PLAN[:UNIT_ADA[-1][0][0]]):
                    i = Idx(s0 + pos)
                    if kind != "in":
                        ada_step(pos, k) if kind == "ada" else act_ahead(act, i)
                        continue
                    act_ahead(act, i)
                    if l == 0 and k == 1:
                        act.dma_start(c1[:, :], a["c1"]).then_inc(on["late_in"], 16)
                        act.dma_start(sml[:, :], a["sml"]).then_inc(on["late_in"], 16)
                    if l == 0 and k == 8:
                        act.dma_start(X[:, :, T:2 * T], a["ctx"]).then_inc(on["ctx_in"], 16)
                    if k == 7:
                        act.wait_ge(on["gates_e"], 2 * l + 1)
                        act.activation(tiny[:, 64:88], tiny[:, 64:88], ACT.Exp, scale=-1.0).then_inc(on["gates_e"], 1)
                    if k in IDX_AT:
                        blk = IDX_AT.index(k)
                        n = P * (blk + 1)
                        act.wait_ge(on["idx_scores_out"], 2 * l + blk + 1)
                        if blk:
                            act.wait_ge(on["idx_used"], 2 * l + 1)
                        for hg in range(2):
                            m = act.activation(SMF.rearrange("p (h b t) -> p b h t", h=2, b=4)[:, :, hg, 0:n],
                                               PS[:, 2:6, hg * T:hg * T + n], ACT.Relu)
                        m.then_inc(on["idx_relu"], 1)
                    if k >= 12:
                        act.wait_ge(slab_used, i.base + 1)
                        act.activation(b1["SG"][:, 2 * (k - 12):2 * (k - 12) + 2, :], bank(i), ACT.Silu)\
                            .then_inc(drained[i.par], 1)
                softmax_exp(l, 0)
                for step in UNIT_ADA[-1]:
                    ada_step(*step)
                for u in range(UN):
                    if u + 1 < UN:
                        softmax_exp(l, u + 1)
                    act.wait_ge(on["pt_ready"], l * UN + u + 1)
                    if u >= 2:
                        act.wait_ge(on["pv_done"], l * UN + u - 1)
                    kind, blk = UNITS[u]
                    if kind == "C":
                        m = act.activation(b1["PT"][0:NCMP, u % 2, 0, :], PS[0:NCMP, 0, :], ACT.Copy)
                    else:
                        m = act.activation(b1["PT"][:, u % 2, 0:blk + 1, :], PS[:, 0:1 + blk, :], ACT.Copy)
                    m.then_inc(on["pt_copied"], 1)
                    if u == 1:
                        act.wait_ge(on["mix_rest"], l + 1)
                        act.activation(xh[:, 4:8, 0:T], b1["MIX"][:, 4:8, :], ACT.Copy).then_inc(on["mixh_done"], 1)
                    for step in UNIT_ADA[u]:
                        ada_step(*step)
                act.wait_ge(on["o_taken"], 4 * l + 4)
                act.activation(xh[:, 0:4, 0:T], b1["MIX"][:, 0:4, :], ACT.Copy).then_inc(on["mixh_done"], 1)
                for k in range(4):
                    i = Idx(s0 + PLAN.index(("out", k)))
                    act_ahead(act, i)
                    act.wait_ge(drained[i.par], i.d // 2 + 1)
                    squares(k)

            for l in range(DEPTH):
                block1(l)
            act_root(act, tiny3[:, :])
            scalar_block2(act, ch)

        def turn_group(pe, l, g):
            pe.wait_ge(on["tr_ready"], GROUPS * l + g + 1)
            o, _ = CONST["pairsum"]
            for c in range(4):
                m = pe.matmul(PS[:, 6 if g == 0 else 7, GROUP * c:GROUP * (c + 1)], TR[:, c * P:(c + 1) * P], const[:, o:o + GROUP],
                              start=True, stop=True)
            m.then_inc(on["mod_cols"], 1)

        def ada_slab(pe, l, pos, n):
            i = Idx(START[f"layer{l}"] + pos)
            g, j = n // GROUP, n % GROUP
            if j == 0:
                if g:
                    turn_group(pe, l, g - 1)
                if GROUPS * l + g:
                    pe.wait_ge(on["mod_read"], GROUPS * l + g)
            half, row = j // (GROUP // 2), 4 * (j % (GROUP // 2))
            wait_split(pe, i)
            for k in range(KT):
                for x, w in enumerate((high(i), low(i))):
                    m = pe.matmul(PS[:, 7, half * 256:half * 256 + 256], CR[:, k, P - row:2 * P - row], w[:, k * 256:(k + 1) * 256],
                                  start=row == 0 and k == 0 and x == 0, stop=j % (GROUP // 2) == GROUP // 2 - 1 and k == KT - 1 and x == 1)
            m.then_inc(slab_used, 1)

        @block.tensor
        def _(pe):
            pe.wait_ge(consts_in, 2 * 16)
            pe.wait_ge(on["sc_ready"], 2)

            def scores(l, u):
                kind, blk = UNITS[u]
                if u >= 2:
                    pe.wait_ge(on["soft_max"], l * UN + u - 1)
                q = {"A": 0}.get(kind, 3)
                for g in range(4):
                    h = (g % 2) * 2 + g // 2
                    r = slice((h % 2) * HD, (h % 2) * HD + HD)
                    lhs = b1["QK"][r, q + h // 2, blk * P:(blk + 1) * P]
                    if kind == "C":
                        rhs = b1["KC"][r, 0, 0:NCMP]
                    else:
                        rhs = b1["QK"][r, {"A": 2, "S": 5, "W": 6}[kind], 0:keys_of(u)]
                    o = (h // 2) * T
                    m = pe.matmul(PS[:, 2 + (u % 2) * 2 + h % 2, o:o + keys_of(u)], lhs, rhs, start=True, stop=True)
                m.then_inc(on["scores_out"], 1)

            def compress(l, i, s):
                pe.wait_ge(on["idx_relu"], 2 * l + 2)
                pe.wait_ge(on["blk_ready"], l + 1)
                pe.wait_ge(slab_full[i.slot], 16 * (i.base // RING + 1))
                for half in range(2):
                    r = slice(half * HD, half * HD + HD)
                    for j in range(16):
                        m = pe.matmul(PS[:, 2 + half, 0:16], raw[r, i.slot, j * P:(j + 1) * P], BLK[r, :, s * 16 + j],
                                      start=s == 0 and j == 0, stop=s == 1 and j == 15)
                m.then_inc(slab_used, 1)

            def token_one(pe, i, n):
                slab_begin(pe, i)
                for tt in range(2):
                    for k in range(KT):
                        for j, (x, w) in enumerate(((xh, high(i)), (xh, low(i)), (xl, high(i)))):
                            m = pe.matmul(PS[:, i.par, tt * 256:tt * 256 + n], x[:, k, tt * P:(tt + 1) * P],
                                          w[:, k * n:(k + 1) * n], start=k == 0 and j == 0, stop=k == KT - 1 and j == 2)
                m.then_inc(slab_used, 1)

            def block1(l):
                pe.wait_ge(on["rms_in"], l + 1)
                pe.matmul(PS[:, 4, 0:T], ones, tiny2[:, :], start=True, stop=True).then_inc(on["rms_sum"], 1)
                s0 = START[f"layer{l}"]
                perm = (cst("permI"), cst("permA"))
                for pos, (kind, k) in enumerate(PLAN[:UNIT_ADA[-1][0][0]]):
                    i = Idx(s0 + pos)
                    if kind == "ada":
                        if (l, k) == (0, 0):
                            pe.wait_ge(on["sc_lo"], 1)
                        ada_slab(pe, l, pos, k)
                        continue
                    if kind == "cmp":
                        compress(l, i, k)
                        continue
                    if k == 5 or k == 6:
                        token_one(pe, i, 256 if k == 5 else 148)
                    else:
                        dense_one(pe, i, 1 if k == 7 else 2, None if k else (on["xl_written"], KT * l))
                    if k == 2:
                        for par in range(2):
                            pe.wait_ge(drained[par], (i.d - 2 + par) // 2 + 1)
                        pe.matmul(PS[:, 2, :], perm[0], b1["QI"][:, 0:2, :], start=True, stop=True)
                        pe.matmul(PS[:, 3, 0:T], perm[0], b1["QI"][:, 2, :], start=True, stop=True).then_inc(on["perms_done"], 1)
                    if k == 5:
                        pe.wait_ge(drained[1 - i.par], (i.d - 1) // 2 + 1)
                        pe.wait_ge(drained[i.par], (i.d - 2) // 2 + 1)
                        pe.wait_ge(on["roped"], 2 * l + 1)
                        for j in range(3):
                            pe.matmul(PS[:, 2 + j, :], perm[1], b1["QK"][:, 2 * j:2 * j + 2, :], start=True, stop=True)
                        pe.matmul(PS[:, 5, 0:T], perm[1], b1["QK"][:, 6, :], start=True, stop=True).then_inc(on["perms_done"], 1)
                    if k + 1 in IDX_AT:
                        blk = IDX_AT.index(k + 1)
                        pe.wait_ge(on["roped"], 2 * l + 2)
                        if blk:
                            pe.wait_ge(on["idx_relu"], 2 * l + 1)
                        for h in range(8):
                            r = slice((h % 4) * 32, (h % 4) * 32 + 32)
                            m = pe.matmul(PS[:, 2 + h % 4, (h // 4) * T:(h // 4) * T + P * (blk + 1)],
                                          b1["QI"][r, h // 4, blk * P:(blk + 1) * P], b1["QI"][r, 2, 0:P * (blk + 1)],
                                          start=True, stop=True)
                        m.then_inc(on["idx_scores_out"], 1)
                    if k == 14:
                        pe.wait_ge(on["kc_raw"], l + 1)
                        pe.matmul(PS[:, 4, 0:NCMP], perm[1], b1["KC"][:, 0, 0:NCMP], start=True, stop=True)
                        pe.transpose(PS[0:16, 4, P:2 * P], b1["KC"][:, 1, :], ident).then_inc(on["perms_done"], 1)
                last_pair(pe, Idx(s0 + PLAN.index(("in", IN_N - 1))))
                pe.wait_ge(on["mod_read"], GROUPS * l + 1)
                pe.wait_ge(on["late_in"], 2 * 16)
                pe.wait_ge(on["pool_in"], l + 1)
                for c in range(2):
                    o, _ = SML["poolw"]
                    m = pe.matmul(PS[:, 6, c * T:(c + 1) * T], sml[:, o + (2 * l + c) * P:o + (2 * l + c + 1) * P],
                                  b1["W2"][:, c, 16:16 + T], start=True, stop=True)
                m.then_inc(on["pool_out"], 1)
                pe.wait_ge(on["kc_ready"], l + 1)
                scores(l, 0)
                scores(l, 1)
                for step in UNIT_ADA[-1]:
                    ada_slab(pe, l, *step)
                for u in range(UN):
                    kind, blk = UNITS[u]
                    pe.wait_ge(on["p_ready"], l * UN + u + 1)
                    if u:
                        pe.wait_ge(on["pt_copied"], l * UN + u)
                    for kt in range(1 if kind == "C" else blk + 1):
                        n = NCMP if kind == "C" else P
                        for g in range(4):
                            h = (g % 2) * 2 + g // 2
                            m = pe.transpose(PS[0:n, kt, h * P:(h + 1) * P],
                                             b1["SM"][:, u % 2, (h % 2) * 2 + h // 2, kt * P:kt * P + n], ident)
                    m.then_inc(on["pt_ready"], 1)
                    if u + 2 < UN:
                        scores(l, u + 2)
                    for step in UNIT_ADA[u]:
                        ada_slab(pe, l, *step)
                    pe.wait_ge(on["pt_copied"], l * UN + u + 1)
                    if kind in "AS":
                        n_taken = {0: 0, 3: 1, 4: 2, 7: 3}[u]
                        if 4 * l + n_taken:
                            pe.wait_ge(on["o_taken"], 4 * l + n_taken)
                        if u == 0:
                            pe.wait_ge(on["pool_out"], 2 * l + 2)
                    if kind == "C":
                        m = pe.matmul(PS[:, 6, :], b1["VC"][0:NCMP, :], b1["PT"][0:NCMP, u % 2, 0, :], start=False, stop=True)
                    else:
                        for kt in range(blk + 1):
                            v = {"A": b1["VT"][:, kt, 0:P], "S": b1["VT"][:, kt, P:2 * P], "W": b1["VW"][:, kt, 0:P]}[kind]
                            m = pe.matmul(PS[:, 6, :], v, b1["PT"][:, u % 2, kt, :], start=kt == 0 and kind in "AS",
                                          stop=kt == blk and kind == "A")
                    m.then_inc(on["pv_done"], 1)
                turn_group(pe, l, GROUPS - 1)
                pe.wait_ge(on["mixl_done"], 2 * l + 2)
                for k in range(4):
                    dense_one(pe, Idx(s0 + PLAN.index(("out", k))))

            for l in range(DEPTH):
                block1(l)
            pe.wait_ge(on["rms_in"], 3)
            pe.matmul(PS[:, 4, 0:T], ones, tiny2[:, :], start=True, stop=True).then_inc(on["rms_sum"], 1)
            tensor_block2(pe)

        @block.vector
        def _(dve):
            ch = Chain(dve, dve_step)
            M, W2, DU = b1["MIX"], b1["W2"], b1["DU"]

            def rms(l):
                dve.wait_ge(on["rms_sum"], l + 1)
                rstd(ch, dve, tiny3[:, :], PS[:, 4, 0:T], D)

            def soft1(l, u):
                kind, blk = UNITS[u]
                n = keys_of(u)
                dve.wait_ge(on["scores_out"], l * UN + u + 1)
                if kind == "A":
                    bias = b1["AB"][:, 0:P] if blk == 0 else b1["AB"][:, P:]
                elif kind == "C":
                    bias = ccol("cmpm")[:, 16 * blk:16 * blk + NCMP]
                else:
                    bias = ccol("tri")[:, P:2 * P] if blk == 0 else ccol("tri")
                if u >= 2:
                    dve.wait_ge(on["pt_ready"], l * UN + u - 1)
                s = b1["SM"][:, u % 2, :, 0:n]
                src = PS[:, 2 + (u % 2) * 2:4 + (u % 2) * 2, :].rearrange("p a (b t) -> p (a b) t", b=2)[:, :, 0:n]
                ch.after(dve.scalar_tensor_tensor(out=s, in0=src, scalar=HD ** -0.5, in1=bc(bias, 4), op0=ALU.mult, op1=ALU.add))
                nm = tiny[:, 8 * (u % 2):8 * (u % 2) + 4]
                ch.after(dve.tensor_reduce(nm, s, AX, ALU.max, negate=True))
                dve.tensor_scalar(nm, nm, FLOOR, None, ALU.min).then_inc(on["soft_max"], 1)

            def soft2(l, u):
                kind, blk = UNITS[u]
                n = keys_of(u)
                dve.wait_ge(on["exp_done"], l * UN + u + 1)
                r = tiny[:, 32 + 8 * (u % 2):36 + 8 * (u % 2)]
                ch.after(dve.tensor_scalar(r, tiny[:, 16 + 8 * (u % 2):20 + 8 * (u % 2)], 1e-30, None, ALU.max))
                ch.after(dve.reciprocal(r, r))
                if kind != "A":
                    o = 96 + 12 * blk + 4 * "CSW".index(kind)
                    ch.after(dve.tensor_tensor(r, r, tiny[:, o:o + 4], ALU.mult))
                s = b1["SM"][:, u % 2, :, 0:n]
                dve.tensor_tensor(s, s, bl(r, n), ALU.mult).then_inc(on["p_ready"], 1)

            def take_o(l, u):
                kind, blk = UNITS[u]
                dve.wait_ge(on["pv_done"], l * UN + u + 1)
                c0 = 0 if kind == "A" else 2
                for par in range(2):
                    r = slice(par * HD, par * HD + HD)
                    o = PS[r, 6, :].rearrange("p (c h t) -> p c h t", c=2, h=2)[:, :, par, :]
                    m = dve.tensor_tensor(M[r, c0:c0 + 2, blk * P:(blk + 1) * P], o,
                                          b1["SG"][r, c0:c0 + 2, blk * P:(blk + 1) * P], ALU.mult)
                m.then_inc(on["o_taken"], 1)

            def top_sum(l, blk):
                n = P * (blk + 1)
                dve.wait_ge(on["idx_relu"], 2 * l + blk + 1)
                s = tiny2[:, 0:n]
                acc = ccol("tri")[:, P:2 * P] if blk == 0 else ccol("tri")
                for h in range(8):
                    ins = dve.scalar_tensor_tensor(out=s, in0=SMF[:, h * T:h * T + n],
                                                   scalar=b1["VW"][:, blk, P + h:P + h + 1], in1=acc, op0=ALU.mult, op1=ALU.add)
                    acc = s
                    if h == 7:
                        ins.then_inc(on["idx_used"], 1)
                        dve.wait_ge(on["idx_used"], 2 * l + blk + 1)
                    else:
                        ch.after(ins)

            def top_rounds(blk, rounds):
                s = tiny2[:, 0:P * (blk + 1)]
                for r in range(rounds):
                    ch.after(dve.max(tiny[:, 48:56], s))
                    ch.after(dve.match_replace(out=s, in_to_replace=tiny[:, 48:56], in_values=s, imm_value=TAKEN))

            def top_mask(blk):
                s = tiny2[:, 0:P * (blk + 1)]
                ab = b1["AB"][:, 0:P] if blk == 0 else b1["AB"][:, P:]
                tri = ccol("tri")[:, P:2 * P] if blk == 0 else ccol("tri")
                ch.after(dve.tensor_scalar(s, s, TAKEN / 2, -NEG, ALU.is_le, ALU.mult))
                ch.after(dve.scalar_tensor_tensor(out=ab, in0=s, scalar=NEG, in1=tri, op0=ALU.add, op1=ALU.add))

            def rope(l, j):
                t, nch, tab = ((b1["QI"], 3, "ropeI"), (b1["QK"], 7, "ropeA"))[j]
                dve.wait_ge(on["perms_done"], 3 * l + j + 1)
                cs = ccol(tab)
                src = PS[:, 2:4, :] if j == 0 else PS[:, 2:6, :]
                src = src.rearrange("p a b -> p (a b)")[:, 0:nch * T].rearrange("p (c t) -> p c t", t=T)
                rt = SMF[:, 0:nch * T].rearrange("p (c t) -> p c t", t=T)
                dve.tensor_tensor(rt, src, bc(cs[:, T:2 * T], nch), ALU.mult)
                ch.after(dve.tensor_tensor(t[:, :, :], t[:, :, :], bc(cs[:, 0:T], nch), ALU.mult))
                dve.tensor_tensor(t[:, :, :], t[:, :, :], rt, ALU.add).then_inc(on["roped"], 1)
                dve.wait_ge(on["roped"], 2 * l + j + 1)

            def rope_compressed(l):
                dve.wait_ge(on["perms_done"], 3 * l + 3)
                cs = ccol("ropeC")
                dve.tensor_copy(b1["VC"][:, :], PS[0:16, 4, P:2 * P])
                ch.after(dve.tensor_tensor(tiny[:, 128:128 + NCMP], PS[:, 4, 0:NCMP], cs[:, 16:16 + NCMP], ALU.mult))
                ch.after(dve.tensor_tensor(b1["KC"][:, 0, 0:NCMP], b1["KC"][:, 0, 0:NCMP], cs[:, 0:NCMP], ALU.mult))
                ch.after(dve.tensor_tensor(b1["KC"][:, 0, 0:NCMP], b1["KC"][:, 0, 0:NCMP], tiny[:, 128:128 + NCMP], ALU.add))
                dve.wait_ge(on["gates_e"], 2 * l + 2)
                ch.after(dve.tensor_scalar(tiny[:, 96:120], tiny[:, 64:88], 1.0, None, ALU.add))
                dve.reciprocal(tiny[:, 96:120], tiny[:, 96:120]).then_inc(on["kc_ready"], 1)

            def block1(l):
                if l:
                    dve.wait_ge(on["mod_final"], l)
                else:
                    dve.wait_ge(acts_in, 16)
                    dve.wait_ge(consts_in, 2 * 16)
                rms(l)
                for k in range(KT + 1):
                    if k < KT:
                        dve.scalar_tensor_tensor(out=M[:, k, :], in0=X[:, k, 0:T], scalar=vcol("norm", l * KT + k),
                                                 in1=tiny3[:, :], op0=ALU.mult, op1=ALU.mult).then_inc(on["rms_out"], 1)
                    if k:
                        dve.wait_ge(on["rms_out"], KT * l + k)
                        dve.wait_ge(on["xm_written"], KT * l + k)
                        dve.tensor_tensor(xl[:, k - 1, 0:T], M[:, k - 1, :], xh[:, k - 1, 0:T].bitcast(F32), ALU.subtract)\
                            .then_inc(on["xl_written"], 1)
                s0 = START[f"layer{l}"]
                if l == 0:
                    dve.wait_ge(on["sc_ready"], 2)
                    dve.tensor_tensor(CR[:, :, P + 2:P + 4], sc[:, :, :], CR[:, :, P:P + 2].bitcast(F32), ALU.subtract)\
                        .then_inc(on["sc_lo"], 1)
                    for b in range(2):
                        split_lo(dve, Idx(b), SIZE[b])

                def mod_group(g):
                    dve.wait_ge(on["mod_cols"], GROUPS * l + g + 1)
                    n = 2 * GROUP
                    o = VEC["adab"][0] + 72 * l + n * g
                    out = mod[:, l, :, :, :].rearrange("p j k b -> p (j k) b")[:, n * g:n * g + n, :]\
                        .rearrange("p (q s c) b -> p q s c b", q=2, c=2)
                    src = PS[:, 6 if g == 0 else 7, 0:4 * GROUP].rearrange("p (q c s b) -> p q s c b", q=2, c=2, b=2)
                    for half in range(2):
                        m = dve.tensor_tensor(out[:, half, :, :, :], src[:, half, :, :, :],
                                              bl(vec[:, o:o + n].rearrange("p (q s c) -> p q s c", q=2, c=2)[:, half, :, :], 2), ALU.add)
                    m.then_inc(on["mod_read"], 1)

                def ada_step(pos, a_):
                    dve_ahead(dve, Idx(s0 + pos))
                    if a_ % GROUP == 0 and a_:
                        mod_group(a_ // GROUP - 1)

                QI, QK = b1["QI"], b1["QK"]
                for pos, (kind, k) in enumerate(PLAN[:UNIT_ADA[-1][0][0]]):
                    i = Idx(s0 + pos)
                    if kind != "in":
                        ada_step(pos, k) if kind == "ada" else dve_ahead(dve, i)
                        continue
                    dve_ahead(dve, i)
                    if k < 12:
                        dve.wait_ge(slab_used, i.base + 1)
                    if k == 0:
                        m = dve.tensor_copy(QI[:, 0:2, :], bank(i))
                    elif k == 1:
                        dve.tensor_copy(QI[:, 2, :], bank(i)[:, 0, :])
                        m = dve.tensor_copy(QK[:, 2, :], bank(i)[:, 1, :])
                    elif k in (2, 3, 4):
                        o = {2: 0, 3: 3, 4: 5}[k]
                        m = dve.tensor_copy(QK[:, o:o + 2, :], bank(i))
                    elif k == 5:
                        m = dve.tensor_copy(b1["VT"][:, :, :], bank(i))
                    elif k == 6:
                        m = dve.tensor_copy(b1["VW"][:, :, :], bank(i)[:, :, 0:148])
                    elif k == 7:
                        m = dve.tensor_copy(KCV, bank(i)[:, 0, :])
                    elif k in (8, 9, 11):
                        m = dve.tensor_copy(b1[{8: "CC", 9: "CX", 11: "CB"}[k]][:, :, :], bank(i))
                    elif k == 10:
                        m = dve.tensor_copy(DU[:, :, 16:16 + T], bank(i))
                    if k < 12:
                        m.then_inc(drained[i.par], 1)
                    if k == 3:
                        if l == 0:
                            dve.wait_ge(on["late_in"], 2 * 16)
                        rope(l, 0)
                    if k == 6:
                        dve.wait_ge(drained[i.par], i.d // 2 + 1)
                        dve.tensor_copy(tiny[:, 64:88].rearrange("p (b g) -> p b g", b=2), b1["VW"][:, :, P + 8:P + 20])\
                            .then_inc(on["gates_e"], 1)
                        rope(l, 1)
                    if k == 7:
                        dve.wait_ge(drained[i.par], i.d // 2 + 1)
                        o = VEC["pe"][0] + 32 * l
                        for half in range(2):
                            kv = KCV[:, 16 * half:16 * half + 240].rearrange("p (n j) -> p n j", j=16)
                            m = dve.tensor_tensor(BLK[:, 0:NCMP, 16 * half:16 * half + 16], kv,
                                                  bc(vec[:, o + 16 * half:o + 16 * half + 16], NCMP), ALU.add)
                        dve.memset(BLK[:, NCMP:16, :], 0.0).then_inc(on["blk_ready"], 1)
                    if k == 10:
                        top_sum(l, 0)
                        top_rounds(0, 4)
                    if k == 11:
                        top_rounds(0, 4)
                        top_mask(0)
                    if k == 12:
                        top_sum(l, 1)
                        top_rounds(1, 2)
                    if k == 13:
                        dve.wait_ge(slab_used, s0 + PLAN.index(("cmp", 1)) + 1)
                        dve.tensor_copy(b1["KC"][:, :, :], PS[:, 2:4, 0:16]).then_inc(on["kc_raw"], 1)
                        dve.wait_ge(on["kc_raw"], l + 1)
                        top_rounds(1, 3)
                    if k == 14:
                        top_rounds(1, 3)
                        top_mask(1)
                    if k == 15:
                        rope_compressed(l)
                dve.wait_ge(on["pool_out"], 2 * l + 1)
                for c in range(2):
                    m = dve.scalar_tensor_tensor(out=M[:, 6 + c, :], in0=PS[:, 6, c * T:(c + 1) * T],
                                                 scalar=vcol("pscale", 2 * l + c), in1=b1["SG"][:, 6 + c, :],
                                                 op0=ALU.mult, op1=ALU.mult)
                m.then_inc(on["pool_out"], 1)
                soft1(l, 0)
                soft1(l, 1)
                for step in UNIT_ADA[-1]:
                    ada_step(*step)
                dve.wait_ge(on["conv_done"], l + 1)
                dve.tensor_tensor(M[:, 4:6, :], M[:, 4:6, :], b1["SG"][:, 4:6, :], ALU.mult).then_inc(on["mix_rest"], 1)
                for u in range(UN):
                    soft2(l, u)
                    for step in UNIT_ADA[u]:
                        ada_step(*step)
                    if u + 2 < UN:
                        soft1(l, u + 2)
                    if u in (3, 4, 7):
                        take_o(l, u - 1)
                    if u == 2:
                        dve.wait_ge(on["mix_rest"], l + 1)
                        dve.wait_ge(on["pool_out"], 2 * l + 2)
                        dve.wait_ge(on["mixh_done"], 2 * l + 1)
                        dve.tensor_tensor(xl[:, 4:8, 0:T], M[:, 4:8, :], xh[:, 4:8, 0:T].bitcast(F32), ALU.subtract)\
                            .then_inc(on["mixl_done"], 1)
                take_o(l, UN - 1)
                dve.wait_ge(on["mixh_done"], 2 * l + 2)
                dve.tensor_tensor(xl[:, 0:4, 0:T], M[:, 0:4, :], xh[:, 0:4, 0:T].bitcast(F32), ALU.subtract)\
                    .then_inc(on["mixl_done"], 1)
                for k in range(4):
                    i = Idx(s0 + PLAN.index(("out", k)))
                    dve_ahead(dve, i)
                    dve.wait_ge(slab_used, i.base + 1)
                    m = dve.tensor_tensor(X[:, 2 * k:2 * k + 2, 0:T], X[:, 2 * k:2 * k + 2, 0:T], bank(i), ALU.add)
                    m.then_inc(drained[i.par], 1)
                for par in range(2):
                    last = i.d - (i.d - par) % 2
                    dve.wait_ge(drained[par], last // 2 + 1)
                mod_group(GROUPS - 1)
                dve.wait_ge(on["mod_read"], GROUPS * (l + 1))
                for j in (1, 4, 7):
                    dve.tensor_scalar(mod[:, l, j, :, :], mod[:, l, j, :, :], 1.0, None, ALU.add)
                for j in (2, 8):
                    m = dve.tensor_scalar(mod[:, l, j, :, :], mod[:, l, j, :, :], 0.5, None, ALU.mult)
                m.then_inc(on["mod_final"], 1)

            for l in range(DEPTH):
                block1(l)
            dve.wait_ge(on["mod_final"], 2)
            rms(2)
            dve_modulate(dve, 0, lambda k: dve.scalar_tensor_tensor(out=X[:, k, 0:T], in0=X[:, k, 0:T], scalar=vcol("fnorm", k),
                                                                    in1=tiny3[:, :], op0=ALU.mult, op1=ALU.mult))
            vector_block2(dve, ch)


IN_SPLITS = (("a_q", 256), ("a_k", 64), ("a_v", 64), ("a_qi", 256), ("a_ki", 32), ("a_wi", 8), ("a_gate", 256),
             ("b_q", 256), ("b_kc", 64), ("b_vc", 64), ("b_ks", 64), ("b_vs", 64), ("b_kw", 64), ("b_vw", 64),
             ("b_g", 12), ("b_gate", 256), ("c_b", 256), ("c_c", 256), ("c_x", 256), ("c_gate", 256),
             ("d_u", 256), ("d_gate", 256))
EVEN_SPLITS = (("q", 256), ("k", 256), ("v", 512), ("r", 512), ("lf", 16), ("lb", 16), ("cq", 384), ("ckv", 128), ("kr", 64))


def spans(splits):
    at, o = {}, 0
    for name, n in splits:
        at[name] = np.arange(o, o + n)
        o += n
    return at


def rows_by_partition(w, cols):
    w = np.concatenate([w, np.zeros((w.shape[0], 1), w.dtype)], 1)
    return w[:, cols].reshape(-1, P, len(cols)).transpose(1, 0, 2)


def slab(w, *chunks):
    return np.concatenate([rows_by_partition(w, c).reshape(P, -1) for c in chunks], 1)


def by_feature(v):
    return v.reshape(-1, P).T


def rope_tables(pos_angles, head, rot, interleaved=False):
    n = pos_angles.shape[0]
    c, s, perm = np.ones((P, n), np.float32), np.zeros((P, n), np.float32), np.zeros((P, P), np.float32)
    cos, sin = np.cos(pos_angles).astype(np.float32), np.sin(pos_angles).astype(np.float32)
    for p in range(P):
        d = p % head
        if d >= rot:
            continue
        if interleaved:
            f, first, partner = d // 2, d % 2 == 0, p ^ 1
        else:
            half = rot // 2
            f, first, partner = d % half, d < half, p + half if d < half else p - half
        c[p], s[p], perm[partner, p] = cos[:, f], (-sin if first else sin)[:, f], 1.0
    return c, s, perm


def constants():
    t = np.arange(T)
    inv = lambda base, n: (np.float32(base) ** (-np.arange(n, dtype=np.float32) / n)).astype(np.float32)
    ang = lambda pos, f: (pos.astype(np.float32)[:, None] * f[None, :]).astype(np.float32)
    ca, sa, pa = rope_tables(ang(t, inv(500000.0, 8)), 64, 16)
    ci, si, pi = rope_tables(ang(t, inv(500000.0, 4)), 32, 8)
    cc, sc_, _ = rope_tables(ang(np.arange(16) * 16 + 31, inv(500000.0, 8)), 64, 16)
    f = inv(10000.0, 16)
    cm, sm, pm = rope_tables(np.concatenate([ang(t // 64, f), ang(t % 64, f)], 1), 64, 64, True)
    pairsum = np.zeros((P, GROUP))
    for j in range(GROUP // 2):
        for b in range(2):
            pairsum[[4 * j + b, 4 * j + 2 + b], 2 * j + b] = 1.0
    const = np.concatenate([np.eye(P), np.ones((P, P)), pa, pi, pm, pairsum], 1)
    q = np.arange(P)
    tri = np.concatenate([np.zeros((P, P)), np.where(q[None, :] > q[:, None], NEG, 0.0)], 1)
    cmpm = np.concatenate([np.where((np.arange(16) * 16 + 31)[None, :] <= (q + b * P)[:, None], 0.0, NEG) for b in range(2)], 1)
    win = np.array([[2, 8], [4, 16]])
    invc = np.stack([[1.0 / np.minimum(t + 1, win[p // HD][c]) for c in range(2)] for p in range(P)]).reshape(P, -1)
    c1 = np.concatenate([ca, sa, ci, si, cc, sc_, tri, cmpm, invc], 1)
    j, i = q[:, None] % GC, np.arange(GC)[None, :]
    reset = np.broadcast_to((np.arange(2 * T) % GC != 0), (P, 2 * T))
    c2 = np.concatenate([cm, sm, j <= i, j > i, reset], 1)
    col, key = q[:, None] % 64, np.arange(64)[None, :]
    start = np.clip(col - 8, 0, 48)
    nmask = np.where((key >= start) & (key < start + 16), 0.0, NEG)
    out = {"const": const, "c1": c1, "c2": c2, "nmask": nmask}
    assert const.shape[1] == CONST_N and c1.shape[1] == C1_N and c2.shape[1] == C2_N
    return {n: np.ascontiguousarray(v, dtype=np.float32) for n, v in out.items()}


def pack(x, norm_w, w_in, w_out, conv_w, pe_cmp, w_cmp_k, w_cmp_v, pool_w, pool_scale, final_norm_w,
         c_2, ctx_2, c_ctx_2, ada_w_2, ada_b_2, ffn1_w_in_2, ffn1_w_out_2, ffn2_w_in_2, ffn2_w_out_2,
         even_w_in_2, gla_wg2_f_2, gla_bg_f_2, gla_wg2_b_2, gla_bg_b_2, gla_norm_g_2, mla_q_norm_g_2,
         mla_kv_norm_g_2, mla_w_uq_2, mla_w_ukv_2, even_w_out_2, na_w_in_2, na_rpb_2, na_w_out_2):
    out = {}
    tokens = lambda v: np.ascontiguousarray(v[0].T.reshape(KT, P, T).transpose(1, 0, 2))
    out["x"], out["ctx"] = tokens(x), tokens(ctx_2)
    chunk = lambda idx, n=0: idx[n * P:(n + 1) * P]
    seq = np.arange(D)
    whole = lambda w: np.stack([slab(w, chunk(seq, 2 * n), chunk(seq, 2 * n + 1)) for n in range(4)])
    s = spans(IN_SPLITS)
    dup = lambda n: np.concatenate([s[n], s[n]])
    for l in range(DEPTH):
        w = w_in[l]
        pair = lambda n: slab(w, chunk(s[n]), chunk(s[n], 1))
        va = rows_by_partition(w, np.concatenate([dup("a_v"), dup("b_vs")])).reshape(P, -1)
        g = s["b_g"].reshape(2, 2, 3).transpose(2, 1, 0).reshape(-1)
        tok = lambda w_, c: rows_by_partition(w_, c).reshape(P, -1)
        dense = [pair("a_qi"), slab(w, np.tile(s["a_ki"], 4), dup("a_k")), pair("a_q"), pair("b_q"), slab(w, dup("b_ks"), dup("b_kw")),
                 va, tok(w, np.concatenate([dup("b_vw"), s["a_wi"], g])), slab(w, np.concatenate([s["b_kc"], s["b_vc"]]))]
        dense += [pair(n) for n in ("c_c", "c_x", "d_u", "c_b", "a_gate", "b_gate", "c_gate", "d_gate")]
        cw = np.concatenate([np.tile(v[l].reshape(32, HD, HD), (1, 1, 2)).transpose(1, 0, 2) for v in (w_cmp_k, w_cmp_v)], 0)
        slabs = {"in": dense, "cmp": cw.reshape(P, 2, -1).transpose(1, 0, 2), "out": whole(w_out[l]),
                 "ada": [tok(ada_w_2[l], np.arange(n * 256, n * 256 + 256)) for n in range(ADA_N)]}
        out[f"layer{l}"] = np.stack([np.pad(slabs[kind][n], ((0, 0), (0, SLAB - slabs[kind][n].shape[1]))) for kind, n in PLAN])
    cols = np.arange(DFF)
    for l in range(DEPTH):
        for f, wi, wo in ((1, ffn1_w_in_2[l], ffn1_w_out_2[l]), (2, ffn2_w_in_2[l], ffn2_w_out_2[l])):
            for half in range(2):
                ms = range(half * FH, half * FH + FH)
                out[f"ffi{f}{l}{half}"] = np.stack([slab(wi, chunk(cols, m), chunk(cols, m) + DFF) for m in ms])
                rows = wo[half * FH * P:(half + 1) * FH * P]
                out[f"ffo{f}{l}{half}"] = np.stack([slab(rows, chunk(seq, n)) for n in range(KT)])
    e, w = spans(EVEN_SPLITS), even_w_in_2[0]
    pair = lambda n, a=0: slab(w, chunk(e[n], a), chunk(e[n], a + 1))
    gap = -np.ones(16, int)
    lr = np.concatenate([e["lf"], gap, e["lb"], gap, np.tile(gap, 4)])
    tok = lambda w_, c: rows_by_partition(w_, c).reshape(P, -1)
    out["even"] = np.stack([pair("q"), pair("k"), slab(w, lr, np.tile(e["kr"], 2)), tok(w, e["v"][0:256]), tok(w, e["v"][256:512]),
                            pair("cq"), slab(w, chunk(e["cq"], 2), e["ckv"]), pair("r"), pair("r", 2)])
    uq = np.arange(768).reshape(4, 192)
    nope, rope_ = uq[:, 0:P], uq[:, P:192].reshape(2, P)
    out["uq"] = np.stack([slab(mla_w_uq_2[0], a_, b_) for a_, b_ in ((nope[0], nope[1]), (nope[2], nope[3]), (rope_[0], rope_[1]))])
    kv = np.arange(1024).reshape(4, 256)
    out["ukv"] = np.stack([slab(mla_w_ukv_2[0], kv[0, 0:P], kv[1, 0:P]), slab(mla_w_ukv_2[0], kv[2, 0:P], kv[3, 0:P]),
                           tok(mla_w_ukv_2[0], kv[0:2, P:].reshape(-1)), tok(mla_w_ukv_2[0], kv[2:4, P:].reshape(-1))])
    out["eout"], out["oout"] = whole(even_w_out_2[0]), whole(na_w_out_2[0])
    w = na_w_in_2[0]
    out["odd"] = np.stack([slab(w, seq[2 * n * P:(2 * n + 1) * P] + o, seq[(2 * n + 1) * P:(2 * n + 2) * P] + o)
                           for o in (0, D) for n in range(4)] + [tok(w, seq[256 * n:256 * n + 256] + 2 * D) for n in range(4)])
    shift = np.arange(64)[None, :] - (np.arange(P) % 64)[:, None] + 15
    rp = np.concatenate([na_rpb_2[0], np.zeros((16, 15, 1), na_rpb_2.dtype)], 2)[:, 4:11]
    out["rpb"] = rp[:, :, np.where((shift >= 0) & (shift <= 30), shift, 31)].transpose(2, 0, 1, 3)
    cols_of = [by_feature(norm_w), by_feature(final_norm_w), by_feature(conv_w), by_feature(pool_scale),
               np.concatenate([np.concatenate([pe_cmp[l].T, pe_cmp[l].T], 0) for l in range(DEPTH)], 1),
               by_feature(ada_b_2), np.stack([by_feature(c_2[0]), by_feature(c_ctx_2)], 2).reshape(P, -1),
               by_feature(gla_bg_f_2), by_feature(gla_bg_b_2), by_feature(gla_norm_g_2), by_feature(mla_q_norm_g_2),
               by_feature(mla_kv_norm_g_2)]
    out["vec"] = np.concatenate(cols_of, 1)
    pw = np.zeros((P, DEPTH, 2, P), pool_w.dtype)
    for l in range(DEPTH):
        for g in range(4):
            r = slice((g % 2) * HD, (g % 2) * HD + HD)
            pw[r, l, g // 2, r] = pool_w[l, g]
    wg = np.zeros((P, 2 * P), pool_w.dtype)
    wg[0:16], wg[32:48] = gla_wg2_f_2[0], gla_wg2_b_2[0]
    out["sml"] = np.concatenate([pw.reshape(P, -1), wg], 1)
    out.update(constants())
    return {n: np.ascontiguousarray(v) for n, v in out.items()}


def kernel(**inputs):
    import concourse.bacc as bacc
    from concourse.bass_utils import run_bass_kernel_spmd

    arrays = pack(**{n: np.asarray(v) for n, v in inputs.items()})
    nc = bacc.Bacc("TRN2", target_bir_lowering=False, num_devices=1)
    a = {n: nc.dram_tensor(n + "_dram", v.shape, mybir.dt.from_np(v.dtype), kind="ExternalInput").ap() for n, v in arrays.items()}
    a["out"] = nc.dram_tensor("out_dram", (P, KT, T), F32, kind="ExternalOutput").ap()
    build(nc, a)
    r = run_bass_kernel_spmd(nc, [{n + "_dram": v for n, v in arrays.items()}], core_ids=[0])
    y = r.results[0]["out_dram"]
    return np.ascontiguousarray(y.transpose(1, 0, 2).reshape(D, T).T[None])
```
